# Optimizing a Trainium2 kernel written in Bass

```python
import math
import jax, jax.numpy as jnp
from jax import lax
import numpy as np

D_MODEL = 1024
BATCH = 1
SEQ = 1024
DEPTH = 2
DEC_BATCH = 8
DEC_SEQ = 4
PAST_LEN = 512
PAGE_SIZE = 128

N_A = DEPTH // 2
N_B = DEPTH - N_A
H_A = 4
DK_A = D_MODEL // 2 // H_A
DV_A = D_MODEL // H_A
KA = H_A * DK_A
VA = H_A * DV_A
GATE_RANK = 16
GATE_NORMALIZER = 16.0
GLA_CHUNK = 64
IN_A = 2 * KA + 2 * VA + GATE_RANK
H_B = 8
DQK_B = D_MODEL // (2 * H_B)
DV_B = 2 * DQK_B
QB = H_B * 2 * DQK_B
ZB = H_B * DV_B
Q_BLOCK = 128
EPS = 1e-6

kernel_name = "yoco_gla_diffattn_step"

def rms_norm(x, g):
    x32 = x.astype(jnp.float32)
    y = x32 * lax.rsqrt(jnp.mean(x32 * x32, axis=-1, keepdims=True) + EPS)
    return (y * g.astype(jnp.float32)).astype(x.dtype)

def ada_mod(x, c, g, w_ada, b_ada, n):
    mod = jax.nn.silu(c) @ w_ada + b_ada
    parts = [p[:, None, :] for p in jnp.split(mod, n, axis=-1)]
    h = rms_norm(x, g) * (1.0 + parts[1]) + parts[0]
    return h, parts[2:]

def gla_recurrence(q, k, v, logg, s0):
    b_, t_ = q.shape[:2]
    c_ = math.gcd(t_, GLA_CHUNK)
    n_ = t_ // c_

    def to_chunks(a):
        return a.reshape(b_, n_, c_, *a.shape[2:]).swapaxes(0, 1)

    causal = jnp.tril(jnp.ones((c_, c_), bool))[None, :, :, None, None]

    def step(s, inp):
        qc, kc, vc, gc = inp
        cum = jnp.cumsum(gc, axis=1)
        o_inter = jnp.einsum('bthk,bhkv->bthv', qc * jnp.exp(cum), s)
        rel = jnp.where(causal, cum[:, :, None] - cum[:, None, :], -jnp.inf)
        attn = jnp.einsum('bthk,bshk,btshk->bhts', qc, kc, jnp.exp(rel))
        o_intra = jnp.einsum('bhts,bshv->bthv', attn, vc)
        last = cum[:, -1]
        s_new = jnp.exp(last)[..., None] * s + jnp.einsum(
            'bshk,bshv->bhkv', kc * jnp.exp(last[:, None] - cum), vc)
        return s_new, o_inter + o_intra

    s_fin, o = lax.scan(step, s0, (to_chunks(q), to_chunks(k), to_chunks(v), to_chunks(logg)))
    return o.swapaxes(0, 1).reshape(b_, t_, H_A, DV_A), s_fin

def gla_block(x, c, s0, norm_g, ada_w, ada_b, w_in, w_g2, b_g, onorm_g, w_out):
    f32 = jnp.float32
    h, (gate,) = ada_mod(x, c, norm_g, ada_w, ada_b, 3)
    b_, t_, _ = h.shape
    q, k, v, z, glow = jnp.split(h @ w_in, [KA, 2 * KA, 2 * KA + VA, 2 * KA + 2 * VA], axis=-1)
    q = q.reshape(b_, t_, H_A, DK_A).astype(f32) * (DK_A ** -0.5)
    k = k.reshape(b_, t_, H_A, DK_A).astype(f32)
    v = v.reshape(b_, t_, H_A, DV_A).astype(f32)
    logg = (jax.nn.log_sigmoid((glow @ w_g2 + b_g).astype(f32)) / GATE_NORMALIZER).reshape(b_, t_, H_A, DK_A)
    o, s_fin = gla_recurrence(q, k, v, logg, s0.astype(f32))
    o = rms_norm(o, onorm_g).reshape(b_, t_, VA).astype(x.dtype)
    out = (o * jax.nn.silu(z)) @ w_out
    return x + gate * out, s_fin.astype(s0.dtype)

def shared_kv(x, c, g_kv, ada_w_kv, ada_b_kv, w_k, w_v, g_k):
    h, _ = ada_mod(x, c, g_kv, ada_w_kv, ada_b_kv, 2)
    b_, t_, _ = h.shape
    k = rms_norm((h @ w_k).reshape(b_, t_, H_B, 2, DQK_B), g_k)
    v = (h @ w_v).reshape(b_, t_, H_B, DV_B)
    return k, v

def diff_scores(q, k, q_pos, k_pos):
    s = jnp.einsum('bqhcd,bkhcd->bhcqk', q, k, preferred_element_type=jnp.float32) * (DQK_B ** -0.5)
    slopes = 2.0 ** (-8.0 * jnp.arange(1, H_B + 1, dtype=jnp.float32) / H_B)
    dist = (q_pos[:, None] - k_pos[None, :]).astype(jnp.float32)
    s = s - (slopes[:, None, None] * dist)[None, :, None]
    return jnp.where(k_pos[None, :] <= q_pos[:, None], s, -jnp.inf)

def diff_weights(s, lam):
    p = jax.nn.softmax(s, axis=-1)
    return p[:, :, 0] - lam * p[:, :, 1]

def diff_attn_prompt(q, k, v, lam):
    b_, t_ = q.shape[:2]
    nb = t_ // Q_BLOCK
    k_pos = jnp.arange(t_)
    v32 = v.astype(jnp.float32)
    qb = q.reshape(b_, nb, Q_BLOCK, H_B, 2, DQK_B).swapaxes(0, 1)

    def block(args):
        qi, i = args
        q_pos = i * Q_BLOCK + jnp.arange(Q_BLOCK)
        w = diff_weights(diff_scores(qi, k, q_pos, k_pos), lam)
        return jnp.einsum('bhqk,bkhe->bqhe', w, v32)

    o = lax.map(block, (qb, jnp.arange(nb)))
    return o.swapaxes(0, 1).reshape(b_, t_, H_B, DV_B)

def diff_attn_sample(q, k_new, v_new, k_past, v_past, lam):
    t_ = q.shape[1]
    past = k_past.shape[1]
    q_pos = past + jnp.arange(t_)
    s = jnp.concatenate([diff_scores(q, k_past, q_pos, jnp.arange(past)),
                         diff_scores(q, k_new, q_pos, q_pos)], axis=-1)
    w = diff_weights(s, lam)
    return (jnp.einsum('bhqk,bkhe->bqhe', w[..., :past], v_past.astype(jnp.float32))
            + jnp.einsum('bhqk,bkhe->bqhe', w[..., past:], v_new.astype(jnp.float32)))

def diff_block(x, c, attend, lam, lam_init, norm_g, ada_w, ada_b, w_in, g_q, g_sub, w_out):
    h, (gate,) = ada_mod(x, c, norm_g, ada_w, ada_b, 3)
    b_, t_, _ = h.shape
    q, z = jnp.split(h @ w_in, [QB], axis=-1)
    q = rms_norm(q.reshape(b_, t_, H_B, 2, DQK_B), g_q)
    o = attend(q, lam)
    o = rms_norm(o, g_sub) * (1.0 - lam_init)
    out = (o.reshape(b_, t_, ZB).astype(x.dtype) * jax.nn.silu(z)) @ w_out
    return x + gate * out

def setup_inputs(seed: int = 0) -> dict:
    key = jax.random.key(seed)
    keys = iter(jax.random.split(key, 48))
    f32 = jnp.float32

    def nrm(shape, scale):
        return jax.random.normal(next(keys), shape, f32) * scale

    def gain(shape):
        return 1.0 + nrm(shape, 0.02)

    D = D_MODEL
    n_pages = PAST_LEN // PAGE_SIZE
    n_pool = (DEC_BATCH * n_pages * 5 + 3) // 4
    perm = jax.random.permutation(next(keys), n_pool)[: DEC_BATCH * n_pages]
    page_table = perm.reshape(DEC_BATCH, n_pages).astype(jnp.int32)
    return {
        "x_prompt": nrm((BATCH, SEQ, D), 1.0),
        "x_sample": nrm((DEC_BATCH, DEC_SEQ, D), 1.0),
        "c_prompt": nrm((BATCH, D), 1.0),
        "c_sample": nrm((DEC_BATCH, D), 1.0),
        "state_gla": nrm((N_A, DEC_BATCH, H_A, DK_A, DV_A), 1.0),
        "cache_k": nrm((n_pool, PAGE_SIZE, H_B, 2, DQK_B), 1.0),
        "cache_v": nrm((n_pool, PAGE_SIZE, H_B, DV_B), 1.0),
        "page_table": page_table,
        "norm_a": gain((N_A, D)),
        "ada_w_a": nrm((N_A, D, 3 * D), 0.5 * D ** -0.5),
        "ada_b_a": nrm((N_A, 3 * D), 0.01),
        "w_in_a": nrm((N_A, D, IN_A), D ** -0.5),
        "w_g2_a": nrm((N_A, GATE_RANK, KA), GATE_RANK ** -0.5),
        "b_g_a": nrm((N_A, KA), 0.1),
        "onorm_a": gain((N_A, DV_A)),
        "w_out_a": nrm((N_A, VA, D), VA ** -0.5),
        "norm_kv": gain((D,)),
        "ada_w_kv": nrm((D, 2 * D), 0.5 * D ** -0.5),
        "ada_b_kv": nrm((2 * D,), 0.01),
        "w_k": nrm((D, QB), D ** -0.5),
        "w_v": nrm((D, ZB), D ** -0.5),
        "g_k": gain((DQK_B,)),
        "norm_b": gain((N_B, D)),
        "ada_w_b": nrm((N_B, D, 3 * D), 0.5 * D ** -0.5),
        "ada_b_b": nrm((N_B, 3 * D), 0.01),
        "w_in_b": nrm((N_B, D, QB + ZB), D ** -0.5),
        "g_q": gain((N_B, DQK_B)),
        "lambda_q1": nrm((N_B, DQK_B), 0.1),
        "lambda_k1": nrm((N_B, DQK_B), 0.1),
        "lambda_q2": nrm((N_B, DQK_B), 0.1),
        "lambda_k2": nrm((N_B, DQK_B), 0.1),
        "subln_b": gain((N_B, DV_B)),
        "w_out_b": nrm((N_B, ZB, D), ZB ** -0.5),
    }

def reference(x_prompt, x_sample, c_prompt, c_sample, state_gla, cache_k, cache_v, page_table,
              norm_a, ada_w_a, ada_b_a, w_in_a, w_g2_a, b_g_a, onorm_a, w_out_a,
              norm_kv, ada_w_kv, ada_b_kv, w_k, w_v, g_k,
              norm_b, ada_w_b, ada_b_b, w_in_b, g_q, lambda_q1, lambda_k1, lambda_q2, lambda_k2,
              subln_b, w_out_b):
    f32 = jnp.float32
    yp, ys = x_prompt, x_sample
    s0_prompt = jnp.zeros((x_prompt.shape[0], H_A, DK_A, DV_A), state_gla.dtype)
    gla_p, gla_s = [], []
    for l in range(N_A):
        prm = (norm_a[l], ada_w_a[l], ada_b_a[l], w_in_a[l], w_g2_a[l], b_g_a[l], onorm_a[l], w_out_a[l])
        yp, sp = gla_block(yp, c_prompt, s0_prompt, *prm)
        ys, ss = gla_block(ys, c_sample, state_gla[l], *prm)
        gla_p.append(sp)
        gla_s.append(ss)
    kp, vp = shared_kv(yp, c_prompt, norm_kv, ada_w_kv, ada_b_kv, w_k, w_v, g_k)
    ks, vs = shared_kv(ys, c_sample, norm_kv, ada_w_kv, ada_b_kv, w_k, w_v, g_k)
    nb_, n_pages = page_table.shape
    past = n_pages * PAGE_SIZE
    k_past = cache_k[page_table].reshape(nb_, past, H_B, 2, DQK_B)
    v_past = cache_v[page_table].reshape(nb_, past, H_B, DV_B)
    for j in range(N_B):
        lam_init = 0.8 - 0.6 * math.exp(-0.3 * (N_A + j))
        lam = (jnp.exp(jnp.sum(lambda_q1[j].astype(f32) * lambda_k1[j].astype(f32)))
               - jnp.exp(jnp.sum(lambda_q2[j].astype(f32) * lambda_k2[j].astype(f32))) + lam_init)
        prm = (norm_b[j], ada_w_b[j], ada_b_b[j], w_in_b[j], g_q[j], subln_b[j], w_out_b[j])
        yp = diff_block(yp, c_prompt, lambda q, lm: diff_attn_prompt(q, kp, vp, lm), lam, lam_init, *prm)
        ys = diff_block(ys, c_sample, lambda q, lm: diff_attn_sample(q, ks, vs, k_past, v_past, lm),
                        lam, lam_init, *prm)
    return (yp, ys, jnp.stack(gla_p), jnp.stack(gla_s), kp, vp, ks, vs)


_drawn_inputs = setup_inputs


def setup_inputs(seed=0):
    import zlib

    import numpy as np

    out = dict(_drawn_inputs(seed))
    spreads = {}
    factors = {'onorm_a': 8.0,
     'norm_kv': 2.987,
     'ada_b_kv': 4.321,
     'g_k': 3.582,
     'norm_b': 8.0,
     'ada_b_b': 8.0,
     'g_q': 8.0,
     'lambda_q1': 2.689,
     'lambda_k1': 3.353,
     'lambda_q2': 3.958,
     'lambda_k2': 200.0,
     'subln_b': 63.335}
    for name, (base, spread) in spreads.items():
        noise = np.random.default_rng([zlib.crc32(name.encode()), seed]).standard_normal(out[name].shape)
        drawn = base * np.exp(spread * noise) if base else spread * noise
        out[name] = __import__('jax').numpy.asarray(drawn.astype(out[name].dtype))
    for name, factor in factors.items():
        out[name] = (out[name] * factor).astype(out[name].dtype)
    return out
```

```python
from contextlib import ExitStack

import numpy as np

import concourse.bass as bass
from concourse import mybir

F32 = mybir.dt.float32
I32 = mybir.dt.int32
ALU = mybir.AluOpType
ACT = mybir.ActivationFunctionType
AX = mybir.AxisListType

P = 128
D = 1024
KC = D // P
TP = 1024
NT = TP // P
SB, SL = 8, 4
TS = SB * SL
T = TP + TS
NC = SB + 1
THIRD = T // 3
HA, DK, DV = 4, 128, 256
RANK = 16
HB, DQ, DE = 8, 64, 128
PAST, PAGE = 512, 128
NPG = PAST // PAGE
EPS = 1e-6
LEVELS = [64, 32, 16, 8, 4, 2, 1]
NL = len(LEVELS)
SLEV = [5, 6]
SR = 2 * TS
NEG = -1.0e30

V_ADA, V_NORM_A, V_NORM_KV, V_NORM_B, V_BG, V_ONORM, V_SUBLN, V_GQ, V_GK, V_N = 0, 64, 72, 80, 88, 92, 94, 95, 96, 97
M_A, M_KV, M_B, M_N = 0, 24, 40, 64


class Chain:

    def __init__(self, eng, sem, base=0):
        self.eng, self.sem, self.base, self.n = eng, sem, base, 0

    def link(self, instruction):
        self.n += 1
        instruction.then_inc(self.sem, 1)
        self.eng.wait_ge(self.sem, self.base + self.n)


def apart(eng, passed):
    eng.sem_inc(passed, 1)


def thirds(ap):
    return [ap[:, THIRD * j:THIRD * (j + 1)] for j in range(3)]


def bcast(ap, *shape):
    return ap.broadcast_to(list(shape))


def build(nc, A, OUT, SCR):
    g = ExitStack()
    with g:
        def sb(name, shape, ctx=g, dt=F32):
            return ctx.enter_context(nc.sbuf_tensor(name, shape, dt))

        def sem(name, ctx=g):
            return ctx.enter_context(nc.semaphore(name))

        made = {}

        def shared(name):
            if name not in made:
                made[name] = sem(name)
            return made[name]

        K = {"sem": shared}
        K["ident"] = sb("ident", [P, P])
        K["ones"] = sb("ones", [P, P])
        K["vec"] = sb("vec", [P, V_N])
        K["mod"] = sb("mod", [P, M_N, NC])
        K["eps"] = sb("eps", [P, 1])
        K["nlam"] = sb("nlam", [P, 1])
        K["B1"] = sb("B1", [P, KC, T])
        K["B2"] = sb("B2", [P, KC, T])
        K["G"] = sb("G", [P, KC, T])
        setup(nc, A, SCR, K)
        gla(nc, A, OUT, K)
        out_proj(nc, A["w_out_a"], SCR["xT"], SCR["x1T"], K["B2"], M_A + 16, K, 0)
        normed(nc, K)
        attention(nc, A, OUT, K)
        out_proj(nc, A["w_out_b"], SCR["x1T"], None, K["B1"], M_B + 16, K, 1)
        store_y(nc, OUT, K)


def stats_and_affine(nc, K, src, rs, sq, ps, affine, use):
    S = {n: K["sem"]("n_" + n) for n in ("sq_used", "sq_ready", "ln_ready", "rs_ready", "xr_ready", "aff_ready", "s_mul")}
    U, M0 = use * KC, use * KC

    def act(eng, before_affine):
        for k in range(KC):
            if k >= 2:
                eng.wait_ge(S["sq_used"], U + k - 1)
            nc.scalar.activation(sq[:, k % 2, :], src[:, k, :], ACT.Square).then_inc(S["sq_ready"], 1)
        eng.wait_ge(S["sq_used"], U + KC)
        nc.scalar.activation(rs[:].rearrange("p (j t) -> p j t", j=3), ps[:, 0:3, 0:THIRD], ACT.Ln,
                             scale=1.0 / D, bias=K["eps"][:, 0:1]).then_inc(S["ln_ready"], 1)
        eng.wait_ge(S["ln_ready"], use + 1)
        nc.scalar.activation(rs[:], rs[:], ACT.Exp, scale=-0.5).then_inc(S["rs_ready"], 1)
        before_affine(eng)
        for k in range(KC):
            eng.wait_ge(S["xr_ready"], U + k + 1)
            for dst, a, b in affine:
                nc.scalar.activation(dst[:, k, 0:TP], src[:, k, 0:TP], ACT.Identity, scale=K["mod"][:, a + k, 0:1],
                                     bias=K["mod"][:, b + k, 0:1]).then_inc(S["aff_ready"], 1)

    def pe(eng):
        for k in range(KC):
            eng.wait_ge(S["sq_ready"], U + k + 1)
            for j, part in enumerate(thirds(sq[:, k % 2, :])):
                mm = nc.tensor.matmul(ps[:, j, 0:THIRD], K["ones"][:], part, start=(k == 0), stop=(k == KC - 1))
            mm.then_inc(S["sq_used"], 1)

    def dve(eng, tmp):
        eng.wait_ge(S["rs_ready"], use + 1)
        for k in range(KC):
            nc.vector.tensor_tensor(src[:, k, :], src[:, k, :], rs[:], ALU.mult).then_inc(S["xr_ready"], 1)
        for k in range(KC):
            eng.wait_ge(S["xr_ready"], U + k + 1)
            xs = src[:, k, TP:T].rearrange("p (b t) -> p b t", b=SB)
            for n, (dst, a, b) in enumerate(affine):
                av = bcast(K["mod"][:, a + k, 1:NC].unsqueeze(2), P, SB, SL)
                nc.vector.tensor_tensor(tmp[:, k, n], xs, av, ALU.mult).then_inc(S["s_mul"], 1)
        for k in range(KC):
            for n, (dst, a, b) in enumerate(affine):
                eng.wait_ge(S["s_mul"], M0 + (k + 1) * len(affine))
                bv = bcast(K["mod"][:, b + k, 1:NC].unsqueeze(2), P, SB, SL)
                nc.vector.tensor_tensor(dst[:, k, TP:T].rearrange("p (b t) -> p b t", b=SB), tmp[:, k, n], bv, ALU.add)

    return act, pe, dve


def setup(nc, A, SCR, K):
    with ExitStack() as c:
        sem = lambda n: K["sem"]("su_" + n)
        tile = lambda n, s: c.enter_context(nc.sbuf_tensor("su_" + n, s, F32))
        psT = c.enter_context(nc.psum_tensor("su_psT", [P, 2, 512], F32))
        psM = c.enter_context(nc.psum_tensor("su_psM", [P, 2, 512], F32))
        psS = c.enter_context(nc.psum_tensor("su_psS", [P, 4, 512], F32))
        rows = tile("rows", [V_N, P])
        crow = tile("crow", [NC, D])
        cth = tile("cth", [NC, D])
        cT = tile("cT", [P, KC, NC])
        lam = tile("lam", [1, 4, DQ])
        lamp = tile("lamp", [1, DQ])
        lams = tile("lams", [1, 2])
        lame = tile("lame", [P, 2])
        xt = tile("xt", [P, 2, D])
        w = tile("w", [P, 4, KC, 256])
        rs = tile("rs", [P, T])
        sq = tile("sq", [P, 2, T])
        tmp = tile("tmp", [P, KC, 1, SB, SL])
        B1, mod, vec, ident, ones = K["B1"], K["mod"], K["vec"], K["ident"], K["ones"]
        s_const, s_rows, s_c, s_lam = sem("const_in"), sem("rows_in"), sem("c_in"), sem("lam_in")
        s_x = [sem(f"x_in{j}") for j in range(2)]
        s_w = [sem(f"w_in{j}") for j in range(4)]
        s_wfree, s_set = sem("w_used"), sem("eps_set")
        s_vecT, s_vec = sem("vec_turned"), sem("vec_ready")
        s_cth, s_csil, s_cps, s_cT = sem("c_tanh"), sem("c_silu"), sem("c_turned"), sem("cT_ready")
        s_lsum, s_lps, s_lexp, s_lam2, s_nlam = sem("lam_sums"), sem("lam_bcast"), sem("lam_exp"), sem("lam_diff"), sem("nlam_ready")
        s_xps, s_xev, s_mps, s_mev, s_scl = sem("x_turned"), sem("x_copied"), sem("mod_summed"), sem("mod_ready"), sem("scales_ready")
        s_out = sem("xT_out")
        act_norm, pe_norm, dve_norm = stats_and_affine(nc, K, B1, rs, sq, psS, [(B1, M_A + 8, M_A)], 0)
        groups = [("ada_w_a", M_A // 8, 3), ("ada_w_kv", M_KV // 8, 2), ("ada_w_b", M_B // 8, 3)]

        with nc.Block() as block:
            @block.sync
            def _(sp):
                sp.dma_start(ident[:], A["ident"]).then_inc(s_const, 16)
                sp.dma_start(ones[:], A["ones"]).then_inc(s_const, 16)
                sp.sem_inc(s_wfree, 4)
                at = 0
                for name, n in (("ada_b_a", 24), ("ada_b_kv", 16), ("ada_b_b", 24), ("norm_a", 8), ("norm_kv", 8), ("norm_b", 8),
                                ("b_g_a", 4), ("onorm_a", 2), ("subln_b", 1)):
                    sp.dma_start(rows[at:at + n, :], A[name].rearrange("(r c) -> r c", c=P)).then_inc(s_rows, 16)
                    at += n
                for name in ("g_q", "g_k"):
                    for half in range(2):
                        sp.dma_start(rows[at:at + 1, DQ * half:DQ * (half + 1)], A[name].unsqueeze(0)).then_inc(s_rows, 16)
                    at += 1
                sp.dma_start(crow[0:1, :], A["c_prompt"]).then_inc(s_c, 16)
                sp.dma_start(crow[1:NC, :], A["c_sample"]).then_inc(s_c, 16)
                for j, name in enumerate(("lambda_q1", "lambda_k1", "lambda_q2", "lambda_k2")):
                    sp.dma_start(lam[0:1, j, :], A[name].unsqueeze(0)).then_inc(s_lam, 16)
                for name, first, n in groups:
                    wd = A[name].rearrange("(k p) n -> p k n", p=P)
                    with sp.Fori(0, n) as i:
                        for j in range(4):
                            sp.wait_ge(s_wfree, (i + first) * 4 + j + 1)
                            sp.dma_start(w[:, j], wd[:, :, bass.ds(i * 1024 + 256 * j, 256)]).then_inc(s_w[j], 16)

            @block.gpsimd
            def _(pool):
                nc.gpsimd.memset(K["eps"][:], EPS).then_inc(s_set, 1)

            @block.tensor
            def _(pe):
                pe.wait_ge(s_const, 32)
                pe.wait_ge(s_rows, 16 * 13)
                nc.tensor.transpose(psM[:, 0, 0:V_N], rows[:], ident[0:V_N, 0:V_N]).then_inc(s_vecT, 1)
                pe.wait_ge(s_csil, 1)
                for k in range(KC):
                    mm = nc.tensor.transpose(psM[:, 1, k * NC:(k + 1) * NC], crow[:, k * P:(k + 1) * P], ident[0:NC, 0:NC])
                mm.then_inc(s_cps, 1)
                pe.wait_ge(s_lsum, 2)
                pe.wait_ge(s_vec, 1)
                nc.tensor.matmul(psM[:, 0, 0:2], ones[0:1, :], lams[0:1, :], start=True, stop=True).then_inc(s_lps, 1)
                for t in range(NT + 1):
                    pe.wait_ge(s_x[t % 2], 16 * (t // 2 + 1))
                    n = P if t < NT else TS
                    for half in range(2):
                        u = 2 * t + half
                        if u >= 2:
                            pe.wait_ge(s_xev, u - 1)
                        for q in range(4):
                            k = 4 * half + q
                            mm = nc.tensor.transpose(psT[:, u % 2, q * P:q * P + n], xt[0:n, t % 2, k * P:(k + 1) * P], ident[0:n, 0:n])
                        mm.then_inc(s_xps, 1)
                pe_norm(pe)
                pe.wait_ge(s_cT, 1)
                pe.wait_ge(s_lexp, 1)
                for name, first, n in groups:
                    with pe.Fori(0, n) as i:
                        for j in range(4):
                            pe.wait_ge(s_w[j], (i + first + 1) * 16)
                            for m in range(2):
                                at = (2 * j + m) * NC
                                if j % 2 == 0 and m == 0:
                                    pe.wait_ge(s_mev, (i + first) * 2 + j // 2 + 1)
                                for k in range(KC):
                                    mm = nc.tensor.matmul(psM[:, j // 2, at:at + NC], w[:, j, k, m * P:(m + 1) * P], cT[:, k, :],
                                                          start=(k == 0), stop=(k == KC - 1))
                            mm.then_inc(s_wfree, 1)

            @block.scalar
            def _(act):
                for t in range(2):
                    act.dma_start(xt[:, t, :], A["x_prompt"][t * P:(t + 1) * P, :]).then_inc(s_x[t], 16)
                act.wait_ge(s_c, 32)
                nc.scalar.activation(cth[:], crow[:], ACT.Tanh, scale=0.5).then_inc(s_cth, 1)
                act.wait_ge(s_lps, 1)
                nc.scalar.activation(lame[:], psM[:, 0, 0:2], ACT.Exp).then_inc(s_lexp, 1)
                for t in range(2, NT + 1):
                    if t >= 2:
                        act.wait_ge(s_xps, 2 * (t - 1))
                    if t < NT:
                        act.dma_start(xt[:, t % 2, :], A["x_prompt"][t * P:(t + 1) * P, :]).then_inc(s_x[t % 2], 16)
                    else:
                        act.dma_start(xt[0:TS, t % 2, :], A["x_sample"]).then_inc(s_x[t % 2], 16)
                act.wait_ge(s_xev, 2 * (NT + 1))
                act.dma_start(SCR["xT"].rearrange("(k p) t -> p k t", p=P), B1[:]).then_inc(s_out, 16)
                act.wait_ge(s_set, 1)
                act_norm(act, lambda eng: eng.wait_ge(s_scl, 1))

            @block.vector
            def _(dve):
                dve.wait_ge(s_cth, 1)
                dve.wait_ge(s_c, 32)
                nc.vector.scalar_tensor_tensor(cth[:], cth[:], 1.0, crow[:], ALU.add, ALU.mult).then_inc(s_cth, 1)
                dve.wait_ge(s_cth, 2)
                nc.vector.tensor_scalar(crow[:], cth[:], 0.5, None, ALU.mult).then_inc(s_csil, 1)
                dve.wait_ge(s_lam, 64)
                for j in range(2):
                    if j:
                        dve.wait_ge(s_lsum, 1)
                    nc.vector.tensor_tensor_reduce(lamp[:], lam[0:1, 2 * j, :], lam[0:1, 2 * j + 1, :], 1.0, 0.0, ALU.mult, ALU.add,
                                                   lams[0:1, j:j + 1]).then_inc(s_lsum, 1)
                dve.wait_ge(s_vecT, 1)
                nc.vector.tensor_copy(vec[:], psM[:, 0, 0:V_N]).then_inc(s_vec, 1)
                dve.wait_ge(s_cps, 1)
                nc.vector.tensor_copy(cT[:].rearrange("p k c -> p (k c)"), psM[:, 1, 0:KC * NC]).then_inc(s_cT, 1)
                lam_init = 0.8 - 0.6 * float(np.exp(-0.3))
                dve.wait_ge(s_lexp, 1)
                nc.vector.tensor_tensor(K["nlam"][:], lame[:, 1:2], lame[:, 0:1], ALU.subtract).then_inc(s_lam2, 1)
                dve.wait_ge(s_lam2, 1)
                nc.vector.tensor_scalar(K["nlam"][:], K["nlam"][:], -lam_init, None, ALU.add)
                for u in range(2 * (NT + 1)):
                    dve.wait_ge(s_xps, u + 1)
                    t, half = u // 2, u % 2
                    n = P if t < NT else TS
                    nc.vector.tensor_copy(B1[:, 4 * half:4 * half + 4, t * P:t * P + n],
                                          psT[:, u % 2, :].rearrange("p (q t) -> p q t", q=4)[:, :, 0:n]).then_inc(s_xev, 1)
                dve.wait_ge(s_vec, 1)
                dve.sem_inc(s_mev, 2)
                for name, first, n in groups:
                    with dve.Fori(0, n) as i:
                        for b in range(2):
                            dve.wait_ge(s_wfree, (i + first) * 4 + 2 * b + 6)
                            at = (i + first) * 8 + 4 * b
                            nc.vector.tensor_tensor(mod[:, bass.ds(at, 4), :],
                                                    psM[:, b, b * 4 * NC:(b + 1) * 4 * NC].rearrange("p (m c) -> p m c", c=NC),
                                                    bcast(vec[:, bass.ds(at, 4)].unsqueeze(2), P, 4, NC), ALU.add).then_inc(s_mev, 1)
                dve.wait_ge(s_mev, 2 + 16)
                for col, gain in ((M_A + 8, V_NORM_A), (M_KV + 8, V_NORM_KV), (M_B + 8, V_NORM_B)):
                    ins = nc.vector.scalar_tensor_tensor(mod[:, col:col + 8, :], mod[:, col:col + 8, :], 1.0,
                                                         bcast(vec[:, gain:gain + 8].unsqueeze(2), P, 8, NC), ALU.add, ALU.mult)
                ins.then_inc(s_scl, 1)
                dve.wait_ge(s_scl, 1)
                dve.wait_ge(s_out, 16)
                dve_norm(dve, tmp)


def gla(nc, A, OUT, K):
    with ExitStack() as c:
        sem = lambda n: K["sem"]("gl_" + n)
        tile = lambda n, s: c.enter_context(nc.sbuf_tensor("gl_" + n, s, F32))
        psP = c.enter_context(nc.psum_tensor("gl_psP", [P, 2, 512], F32))
        psL = c.enter_context(nc.psum_tensor("gl_psL", [P, 4, 512], F32))
        psO = c.enter_context(nc.psum_tensor("gl_psO", [P, 512], F32))
        psK = c.enter_context(nc.psum_tensor("gl_psK", [P, 512], F32))
        w = {n: tile("w_" + n, [P, KC, s]) for n, s in (("q", P), ("k", P), ("v", DV), ("z", DV))}
        wlow = tile("wlow", [P, KC, RANK])
        wg2 = tile("wg2", [RANK, DK])
        low = tile("low", [RANK, T])
        masks = tile("masks", [P, NL + 1, P])
        smasks = tile("smasks", [TS, 3, TS])
        restart = tile("restart", [P, T])
        rowsel = tile("rowsel", [TS, SB])
        qT, kT, gk, cum, ec = (tile(n, [P, T]) for n in ("qT", "kT", "gk", "cum", "ec"))
        zs = tile("zs", [P, 2, T])
        th = tile("th", [P, 2, THIRD])
        v = tile("v", [P, NT + 1, DV])
        khT = tile("khT", [P, NT + 1, P])
        khm = tile("khm", [TS, SB, P])
        tmp = tile("tmp", [P, NL + 1, P])
        Am = tile("Am", [P, 2, P])
        As = tile("As", [TS, TS])
        state = tile("state", [P, DV])
        sst = tile("sst", [P, SB, DV])
        dec = tile("dec", [P, NT + SB])
        one = tile("one", [P, 1])
        X = K["B2"]
        h, G, ident, ones, vec = K["B1"], K["G"], K["ident"], K["ones"], K["vec"]

        passed = {"act": K["sem"]("passed_act")}
        s_const, s_g2in, s_low_in, s_set = sem("const_in"), sem("w_g2_in"), sem("low_in"), sem("one_set")
        s_w = {n: sem(f"w_{n}_in") for n in w}
        s_sin, s_sout, s_pout = sem("sstate_in"), sem("sstate_out"), sem("pstate_out")
        s_lowps, s_low = sem("low_summed"), sem("low_ready")
        s_proj, s_pfree = sem("proj_summed"), sem("proj_bank_free")
        s_v = sem("v_ready")
        s_zs = sem("z_ready")
        s_gm, s_ge, s_gl, s_lg, s_cum = sem("g_min"), sem("g_exp"), sem("g_log"), sem("logg"), sem("cum_ready")
        s_d, s_e, s_x = sem("level_diff"), sem("level_exp"), sem("level_ready")
        s_ece, s_dec, s_qh = sem("exp_cum"), sem("decay_kept"), sem("qhat_ready")
        s_kd, s_ke, s_kh = sem("khat_diff"), sem("khat_exp"), sem("khat_ready")
        s_kps, s_kT, s_khm = sem("khat_turned"), sem("khT_ready"), sem("khat_masked")
        s_lv, s_lm, s_A = sem("levels_summed"), sem("levels_masked"), sem("scores_ready")
        s_o, s_oev, s_up, s_st = sem("out_summed"), sem("out_copied"), sem("update_summed"), sem("state_ready")
        s_ups, s_sst = sem("supdate_summed"), sem("sstate_ready")
        s_osq, s_oss, s_oln, s_ors, s_g1, s_g2 = (sem("o_squares"), sem("o_sums"), sem("o_log"), sem("o_rstd"),
                                                   sem("o_normed"), sem("o_gated"))
        win = A["w_in_a"].rearrange("(k p) n -> p k n", p=P)
        CH = NT + 1
        UNITS = 20
        lvl = lambda ap, L: ap.rearrange("p (n a l) -> p n a l", a=2, l=L)

        with nc.Block() as block:
            @block.sync
            def _(sp):
                for dst, name in ((masks, "masks"), (smasks, "smasks"), (restart, "restart"), (rowsel, "rowsel")):
                    sp.dma_start(dst[:], A[name]).then_inc(s_const, 16)
                sp.dma_start(wlow[:], win[:, :, 3072:3088]).then_inc(s_low_in, 16)
                with sp.Fori(0, HA) as i:
                    for name, first, n, used in (("q", 0, P, 3), ("k", 512, P, 6), ("z", 2048, DV, 15), ("v", 1024, DV, UNITS)):
                        sp.wait_ge(s_proj, i * UNITS + used)
                        sp.dma_start(w[name][:], win[:, :, bass.ds(i * n + first, n)]).then_inc(s_w[name], 16)
                    sp.wait_ge(s_proj, i * UNITS + 9)
                    sp.dma_start(wg2[:], A["w_g2_a"][:, bass.ds(i * DK, DK)]).then_inc(s_g2in, 16)
                    sp.wait_ge(s_sout, 16 * i)
                    sp.dma_start(sst[:], A["state_gla"][:, bass.ds(i, 1), :, :].rearrange("b h k v -> k (b h) v")).then_inc(s_sin, 16)
                    sp.wait_ge(s_st, 8 * i + 8)
                    sp.dma_start(OUT["state_p"][bass.ds(i, 1), :, :].rearrange("h k v -> k (h v)"), state[:]).then_inc(s_pout, 16)
                    sp.wait_ge(s_sst, 8 * i + 8)
                    sp.dma_start(OUT["state_s"][:, bass.ds(i, 1), :, :].rearrange("b h k v -> k (b h) v"), sst[:]).then_inc(s_sout, 16)
                sp.wait_ge(s_pout, 16 * HA)
                sp.wait_ge(s_sout, 16 * HA)

            @block.gpsimd
            def _(pool):
                nc.gpsimd.memset(one[:], 1.0).then_inc(s_set, 1)

            @block.tensor
            def _(pe):
                pe.wait_ge(s_low_in, 16)
                for j, part in enumerate(thirds(low[:])):
                    for k in range(KC):
                        mm = nc.tensor.matmul(psL[0:RANK, j, 0:THIRD], wlow[:, k, :], thirds(h[:, k, :])[j], start=(k == 0), stop=(k == KC - 1))
                mm.then_inc(s_lowps, 1)
                pe.wait_ge(s_const, 16 * 4)
                pe.wait_ge(s_low, 1)
                pe.sem_inc(s_proj, UNITS)
                with pe.Fori(0, HA) as i:
                    unit = [0]

                    def bank():
                        pe.wait_ge(s_pfree, i * UNITS + unit[0] + 1)
                        b = unit[0] % 2
                        unit[0] += 1
                        return b

                    def features(wt, m):
                        for j in range(3):
                            b = bank()
                            for k in range(KC):
                                mm = nc.tensor.matmul(psP[:, b, 0:THIRD], wt[:, k, m * P:(m + 1) * P], thirds(h[:, k, :])[j],
                                                      start=(k == 0), stop=(k == KC - 1))
                            mm.then_inc(s_proj, 1)

                    pe.wait_ge(s_w["q"], 16 * (i + 1))
                    features(w["q"], 0)
                    pe.wait_ge(s_w["k"], 16 * (i + 1))
                    features(w["k"], 0)
                    pe.wait_ge(s_g2in, 16 * (i + 1))
                    for j in range(3):
                        b = bank()
                        nc.tensor.matmul(psP[:, b, 0:THIRD], wg2[:], thirds(low[:])[j], start=True, stop=True).then_inc(s_proj, 1)
                    pe.wait_ge(s_w["z"], 16 * (i + 1))
                    for m in range(2):
                        features(w["z"], m)
                    pe.wait_ge(s_w["v"], 16 * (i + 1))
                    for u in range(5):
                        b = bank()
                        for r in range(2 if u < 4 else 1):
                            t = 2 * u + r
                            n = P if t < NT else TS
                            for k in range(KC):
                                mm = nc.tensor.matmul(psP[0:n, b, r * DV:(r + 1) * DV], h[:, k, t * P:t * P + n], w["v"][:, k, :],
                                                      start=(k == 0), stop=(k == KC - 1))
                        mm.then_inc(s_proj, 1)
                    assert unit[0] == UNITS
                    pe.wait_ge(s_kh, i + 1)
                    for r in range(3):
                        if r:
                            pe.wait_ge(s_kT, 3 * i + r)
                        else:
                            pe.wait_ge(s_st, 8 * i)
                        for t in range(4 * r, min(4 * r + 4, CH)):
                            n = P if t < NT else TS
                            mm = nc.tensor.transpose(psK[0:n, (t % 4) * P:(t % 4) * P + P], gk[:, t * P:t * P + n], ident[:])
                        mm.then_inc(s_kps, 1)
                    pe.wait_ge(s_x, i + 1)
                    pe.wait_ge(s_qh, i + 1)
                    pe.wait_ge(s_v, 5 * (i + 1))

                    def levels(t):
                        if t >= 2:
                            pe.wait_ge(s_lm, CH * i + t - 1)
                        elif t == 0:
                            pe.wait_ge(s_ors, i)
                        lo, n = t * P, (P if t < NT else TS)
                        todo = [(X[:, L, lo:lo + n],) * 2 for L in (range(NL) if t < NT else SLEV)] + [(kT[:, lo:lo + n], qT[:, lo:lo + n])]
                        for r, (a, b) in enumerate(todo):
                            f = r * n
                            mm = nc.tensor.matmul(psL[0:n, 2 * (t % 2) + f // 512, f % 512:f % 512 + n], a, b, start=True, stop=True)
                        mm.then_inc(s_lv, 1)

                    def output(t):
                        pe.wait_ge(s_A, CH * i + t + 1)
                        if t:
                            pe.wait_ge(s_oev, CH * i + t)
                            if t < NT:
                                pe.wait_ge(s_st, 8 * i + t)
                        for half in range(2):
                            cols = slice(half * DK, (half + 1) * DK)
                            mm = nc.tensor.matmul(psO[:, half * P:(half + 1) * P], v[:, t, cols], Am[:, t % 2, :], start=True, stop=(t == 0))
                            if t:
                                mm = nc.tensor.matmul(psO[:, half * P:(half + 1) * P], state[:, cols], ec[:, t * P:(t + 1) * P], start=False, stop=True)
                        mm.then_inc(s_o, 1)

                    def update(t):
                        if t == 0:
                            pe.wait_ge(s_kT, 3 * i + 3)
                        else:
                            pe.wait_ge(s_st, 8 * i + t)
                        nc.tensor.matmul(psK[:, 0:DV], khT[:, t, :], v[:, t, :], start=True, stop=True).then_inc(s_up, 1)

                    levels(0)
                    for t in range(NT):
                        levels(t + 1)
                        output(t)
                        update(t)
                    pe.wait_ge(s_A, CH * i + CH)
                    pe.wait_ge(s_oev, CH * i + NT)
                    pe.wait_ge(s_sin, 16 * (i + 1))
                    for half in range(2):
                        cols = slice(half * DK, (half + 1) * DK)
                        for b in range(SB):
                            at = half * TS + b * SL
                            nc.tensor.matmul(psO[:, at:at + SL], sst[:, b, cols], ec[:, TP + b * SL:TP + (b + 1) * SL], start=(b == 0), stop=False)
                        mm = nc.tensor.matmul(psO[:, half * TS:(half + 1) * TS], v[0:TS, NT, cols], As[:], start=False, stop=True)
                    mm.then_inc(s_o, 1)
                    pe.wait_ge(s_khm, i + 1)
                    pe.wait_ge(s_lm, CH * i + CH)
                    for b in range(SB):
                        mm = nc.tensor.matmul(psL[:, b // 2, (b % 2) * DV:(b % 2 + 1) * DV], khm[:, b, :], v[0:TS, NT, :], start=True, stop=True)
                    mm.then_inc(s_ups, 1)
                    pe.wait_ge(s_osq, i + 1)
                    pe.wait_ge(s_sst, 8 * (i + 1))
                    for j in range(3):
                        for half in range(2):
                            mm = nc.tensor.matmul(psL[:, j, 0:THIRD], ones[:], thirds(X[:, half, :])[j], start=(half == 0), stop=(half == 1))
                    mm.then_inc(s_oss, 1)

            @block.scalar
            def _(act):
                A_ = nc.scalar.activation
                act.wait_ge(s_lowps, 1)
                A_(low[:].rearrange("p (j t) -> p j t", j=3), psL[0:RANK, 0:3, 0:THIRD], ACT.Copy).then_inc(s_low, 1)
                act.wait_ge(s_set, 1)
                act.sem_inc(s_pfree, 2)
                with act.Fori(0, HA) as i:
                    unit = [UNITS]

                    def done():
                        unit[0] += 1
                        act.wait_ge(s_proj, i * UNITS + unit[0])
                        return (unit[0] - 1) % 2

                    act.wait_ge(s_A, CH * i)
                    act.wait_ge(s_oss, i)
                    for j in range(3):
                        A_(thirds(qT[:])[j], psP[:, done(), 0:THIRD], ACT.Copy, scale=DK ** -0.5).then_inc(s_pfree, 1)
                    for j in range(3):
                        A_(thirds(kT[:])[j], psP[:, done(), 0:THIRD], ACT.Copy).then_inc(s_pfree, 1)
                    for j in range(3):
                        b = done()
                        apart(act, passed["act"])
                        A_(thirds(gk[:])[j], psP[:, b, 0:THIRD], ACT.Identity, bias=vec[:, bass.ds(i + V_BG, 1)])
                        A_(thirds(ec[:])[j], psP[:, b, 0:THIRD], ACT.Abs, bias=vec[:, bass.ds(i + V_BG, 1)]).then_inc(s_pfree, 1)
                    act.wait_ge(s_pfree, i * UNITS + 2 + 9)
                    A_(ec[:], ec[:], ACT.Exp, scale=-1.0).then_inc(s_ge, 1)
                    act.wait_ge(s_ge, i + 1)
                    A_(ec[:], ec[:], ACT.Ln, bias=one[:, 0:1]).then_inc(s_gl, 1)
                    act.wait_ge(s_g2, 2 * i)
                    for m in range(2):
                        for j in range(3):
                            u = 3 * m + j
                            b = done()
                            if u >= 2:
                                act.wait_ge(s_zs, 6 * i + u - 1)
                            A_(thirds(zs[:, m, :])[j], psP[:, b, 0:THIRD], ACT.Copy, scale=0.5)
                            A_(th[:, u % 2, :], psP[:, b, 0:THIRD], ACT.Tanh, scale=0.5).then_inc(s_pfree, 1)
                    act.wait_ge(s_cum, i + 1)
                    A_(ec[:], cum[:], ACT.Exp).then_inc(s_ece, 1)
                    for L in range(NL):
                        act.wait_ge(s_d, NL * i + L + 1)
                        n = T if L in SLEV else TP
                        A_(X[:, L, 0:n], X[:, L, 0:n], ACT.Exp).then_inc(s_e, 1)
                    act.wait_ge(s_kd, i + 1)
                    A_(gk[:], gk[:], ACT.Exp).then_inc(s_ke, 1)
                    for u in range(5):
                        b = done()
                        if u < 4:
                            A_(v[:, 2 * u:2 * u + 2, :].rearrange("p a d -> p (a d)"), psP[:, b, :], ACT.Copy).then_inc(s_v, 1)
                        else:
                            A_(v[0:TS, NT, :], psP[0:TS, b, 0:DV], ACT.Copy).then_inc(s_v, 1)
                        act.wait_ge(s_v, 5 * i + u + 1)
                        act.sem_inc(s_pfree, 1)
                    for r in range(3):
                        act.wait_ge(s_kps, 3 * i + r + 1)
                        if r < 2:
                            A_(khT[:, 4 * r:4 * r + 4, :].rearrange("p a d -> p (a d)"), psK[:], ACT.Copy).then_inc(s_kT, 1)
                        else:
                            A_(khT[0:TS, NT, :], psK[0:TS, 0:P], ACT.Copy).then_inc(s_kT, 1)
                    for t in range(CH):
                        act.wait_ge(s_o, CH * i + t + 1)
                        n = P if t < NT else TS
                        apart(act, passed["act"])
                        A_(G[:, bass.ds(2 * i, 2), t * P:t * P + n], psO[:, 0:2 * n].rearrange("p (a t) -> p a t", a=2), ACT.Copy).then_inc(s_oev, 1)
                    act.wait_ge(s_oev, CH * (i + 1))
                    act.wait_ge(s_lv, CH * (i + 1))
                    apart(act, passed["act"])
                    A_(X[:, 0:2, :], G[:, bass.ds(2 * i, 2), :], ACT.Square).then_inc(s_osq, 1)
                    act.wait_ge(s_oss, i + 1)
                    ecv = X[:, 2, :]
                    A_(ecv.rearrange("p (j t) -> p j t", j=3), psL[:, 0:3, 0:THIRD], ACT.Ln, scale=1.0 / DV, bias=K["eps"][:, 0:1]).then_inc(s_oln, 1)
                    act.wait_ge(s_oln, i + 1)
                    A_(ecv, ecv, ACT.Exp, scale=-0.5).then_inc(s_ors, 1)

            @block.vector
            def _(dve):
                V = nc.vector
                dve.wait_ge(s_const, 16 * 4)
                with dve.Fori(0, HA) as i:
                    dve.wait_ge(s_pfree, i * UNITS + 2 + 9)
                    V.tensor_scalar(gk[:], gk[:], 0.0, None, ALU.min).then_inc(s_gm, 1)
                    dve.wait_ge(s_gm, i + 1)
                    dve.wait_ge(s_gl, i + 1)
                    V.tensor_tensor(gk[:], gk[:], ec[:], ALU.subtract).then_inc(s_lg, 1)
                    dve.wait_ge(s_lg, 2 * i + 1)
                    V.tensor_scalar(gk[:], gk[:], 1.0 / 16.0, None, ALU.mult).then_inc(s_lg, 1)
                    dve.wait_ge(s_lg, 2 * i + 2)
                    V.tensor_tensor_scan(cum[:], restart[:], gk[:], 0.0, ALU.mult, ALU.add).then_inc(s_cum, 1)
                    dve.wait_ge(s_cum, i + 1)

                    def zgate(u):
                        dve.wait_ge(s_pfree, i * UNITS + 2 + 9 + u + 1)
                        dst = thirds(zs[:, u // 3, :])[u % 3]
                        V.scalar_tensor_tensor(dst, th[:, u % 2, :], 1.0, dst, ALU.add, ALU.mult).then_inc(s_zs, 1)

                    for L, size in enumerate(LEVELS):
                        parts = [(0, TP)] + ([(TP, T)] if L in SLEV else [])
                        for a, b in parts:
                            src, dst = lvl(cum[:, a:b], size), lvl(X[:, L, a:b], size)
                            m = src.shape[1]
                            ref = bcast(src[:, :, 0, size - 1:size], P, m, size)
                            V.tensor_tensor(dst[:, :, 0, :], ref, src[:, :, 0, :], ALU.subtract)
                            last = V.tensor_tensor(dst[:, :, 1, :], src[:, :, 1, :], ref, ALU.subtract)
                        last.then_inc(s_d, 1)
                        if L < 6:
                            zgate(L)
                    for a, b, size in ((0, TP, P), (TP, T, SL)):
                        src = cum[:, a:b].rearrange("p (n t) -> p n t", t=size)
                        last = V.tensor_tensor(gk[:, a:b].rearrange("p (n t) -> p n t", t=size), bcast(src[:, :, size - 1:size], P, (b - a) // size, size),
                                               src, ALU.subtract)
                    last.then_inc(s_kd, 1)
                    dve.wait_ge(s_ece, i + 1)
                    V.tensor_copy(dec[:, 0:NT], ec[:, P - 1:TP:P])
                    V.tensor_copy(dec[:, NT:NT + SB], ec[:, TP + SL - 1:T:SL]).then_inc(s_dec, 1)
                    dve.wait_ge(s_dec, i + 1)
                    V.tensor_tensor(ec[:], ec[:], qT[:], ALU.mult).then_inc(s_qh, 1)
                    for L, size in enumerate(LEVELS):
                        dve.wait_ge(s_e, NL * i + L + 1)
                        for a, b in [(0, TP)] + ([(TP, T)] if L in SLEV else []):
                            dst = lvl(X[:, L, a:b], size)
                            V.tensor_tensor(dst[:, :, 0, :], dst[:, :, 0, :], lvl(kT[:, a:b], size)[:, :, 0, :], ALU.mult)
                            last = V.tensor_tensor(dst[:, :, 1, :], dst[:, :, 1, :], lvl(qT[:, a:b], size)[:, :, 1, :], ALU.mult)
                    last.then_inc(s_x, 1)
                    dve.wait_ge(s_ke, i + 1)
                    V.tensor_tensor(gk[:], gk[:], kT[:], ALU.mult).then_inc(s_kh, 1)
                    dve.wait_ge(s_pout, 16 * i)
                    for t in range(NT):
                        dve.wait_ge(s_lv, CH * i + t + 1)
                        V.tensor_tensor(tmp[:].rearrange("p l t -> p (l t)"), psL[:, 2 * (t % 2):2 * (t % 2) + 2, :].rearrange("p a t -> p (a t)"),
                                        masks[:].rearrange("p l t -> p (l t)"), ALU.mult).then_inc(s_lm, 1)
                        dve.wait_ge(s_lm, CH * i + t + 1)
                        if t >= 2:
                            dve.wait_ge(s_o, CH * i + t - 1)
                        V.tensor_reduce(Am[:, t % 2, :], tmp[:].rearrange("p l t -> p t l"), AX.X, ALU.add).then_inc(s_A, 1)
                        dve.wait_ge(s_up, NT * i + t + 1)
                        if t == 0:
                            V.tensor_copy(state[:], psK[:, 0:DV]).then_inc(s_st, 1)
                        else:
                            dve.wait_ge(s_o, CH * i + t + 1)
                            V.scalar_tensor_tensor(state[:], state[:], dec[:, t:t + 1], psK[:, 0:DV], ALU.mult, ALU.add).then_inc(s_st, 1)
                        dve.wait_ge(s_st, 8 * i + t + 1)
                    dve.wait_ge(s_lv, CH * i + CH)
                    V.tensor_tensor(tmp[0:TS, 0:3, 0:TS], psL[0:TS, 0, 0:3 * TS].rearrange("p (l t) -> p l t", l=3), smasks[:], ALU.mult).then_inc(s_lm, 1)
                    dve.wait_ge(s_lm, CH * i + CH)
                    V.tensor_reduce(As[:], tmp[0:TS, 0:3, 0:TS].rearrange("p l t -> p t l"), AX.X, ALU.add).then_inc(s_A, 1)
                    dve.wait_ge(s_kT, 3 * i + 3)
                    V.tensor_tensor(khm[:], bcast(khT[0:TS, NT, :].unsqueeze(1), TS, SB, P), bcast(rowsel[:].unsqueeze(2), TS, SB, P), ALU.mult).then_inc(s_khm, 1)
                    dve.wait_ge(s_ups, i + 1)
                    for b in range(SB):
                        V.scalar_tensor_tensor(sst[:, b, :], sst[:, b, :], dec[:, NT + b:NT + b + 1], psL[:, b // 2, (b % 2) * DV:(b % 2 + 1) * DV],
                                               ALU.mult, ALU.add).then_inc(s_sst, 1)
                    dve.wait_ge(s_ors, i + 1)
                    for half in range(2):
                        o = G[:, bass.ds(2 * i + half, 1), :].rearrange("p a t -> p (a t)")
                        V.scalar_tensor_tensor(o, o, vec[:, V_ONORM + half:V_ONORM + half + 1], X[:, 2, :], ALU.mult, ALU.mult).then_inc(s_g1, 1)
                        dve.wait_ge(s_g1, 2 * i + half + 1)
                        dve.wait_ge(s_zs, 6 * i + 6)
                        V.tensor_tensor(o, o, zs[:, half, :], ALU.mult).then_inc(s_g2, 1)
                    dve.wait_ge(s_g2, 2 * (i + 1))


def out_proj(nc, W, resid, keep, dst, gate, K, use):
    with ExitStack() as c:
        sem = lambda n: K["sem"]("op_" + n)
        ps = c.enter_context(nc.psum_tensor(f"op{use}_ps", [P, 2, 512], F32))
        w = c.enter_context(nc.sbuf_tensor(f"op{use}_w", [P, 2, KC, P], F32))
        x = c.enter_context(nc.sbuf_tensor(f"op{use}_x", [P, 2, T], F32))
        sg = c.enter_context(nc.sbuf_tensor(f"op{use}_sg", [P, 2, TS], F32))
        s_w = [sem(f"w_in{b}") for b in range(2)]
        s_x = [sem(f"x_in{b}") for b in range(2)]
        s_mm, s_free, s_sg, s_out, s_kept = sem("summed"), sem("added"), sem("sample_gated"), sem("tile_ready"), sem("kept")
        G, mod = K["G"], K["mod"]
        wd = W.rearrange("(k p) n -> p k n", p=P)

        with nc.Block() as block:
            @block.sync
            def _(sp):
                if use == 0:
                    sp.sem_inc(s_mm, 6)
                    sp.sem_inc(s_out, 2)
                with sp.Fori(0, KC // 2) as i:
                    s = i + use * KC // 2
                    for b in range(2):
                        sp.wait_ge(s_mm, s * 6 + 3 * b + 3)
                        sp.dma_start(w[:, b], wd[:, :, bass.ds(i * 2 * P + b * P, P)]).then_inc(s_w[b], 16)
                        sp.wait_ge(s_out, s * 2 + b + 1)
                        sp.dma_start(x[:, b], resid[bass.ds(i * 2 * P + b * P, P), :]).then_inc(s_x[b], 16)
                if keep is not None:
                    with sp.Fori(0, KC) as m:
                        sp.wait_ge(s_out, m + 3)
                        sp.dma_start(keep[bass.ds(m * P, P), :], dst[:, bass.ds(m, 1), :].rearrange("p a t -> p (a t)")).then_inc(s_kept, 16)
                    sp.wait_ge(s_kept, 16 * KC)

            @block.tensor
            def _(pe):
                with pe.Fori(0, KC // 2) as i:
                    s = i + use * KC // 2
                    for b in range(2):
                        pe.wait_ge(s_w[b], 16 * (s + 1))
                        for j in range(3):
                            u = 3 * b + j
                            pe.wait_ge(s_free, s * 6 + u + 1)
                            for k in range(KC):
                                mm = nc.tensor.matmul(ps[:, u % 2, 0:THIRD], w[:, b, k, :], thirds(G[:, k, :])[j], start=(k == 0), stop=(k == KC - 1))
                            mm.then_inc(s_mm, 1)

            @block.vector
            def _(dve):
                V = nc.vector
                if use == 0:
                    dve.sem_inc(s_free, 2)
                with dve.Fori(0, KC // 2) as i:
                    s = i + use * KC // 2
                    for b in range(2):
                        dve.wait_ge(s_x[b], 16 * (s + 1))
                        gp = mod[:, bass.ds(i * 2 + b + gate, 1), 0:1].rearrange("p a c -> p (a c)")
                        gs = mod[:, bass.ds(i * 2 + b + gate, 1), 1:NC].rearrange("p a c -> p (a c)")
                        d = dst[:, bass.ds(i * 2 + b, 1), :].rearrange("p a t -> p (a t)")
                        for j in range(3):
                            u = 3 * b + j
                            dve.wait_ge(s_mm, s * 6 + u + 7)
                            n = THIRD if j < 2 else THIRD - TS
                            lo = THIRD * j
                            if j == 2:
                                V.tensor_tensor(sg[:, b, :].rearrange("p (s t) -> p s t", s=SB),
                                                ps[:, u % 2, n:THIRD].rearrange("p (s t) -> p s t", s=SB),
                                                bcast(gs.unsqueeze(2), P, SB, SL), ALU.mult).then_inc(s_sg, 1)
                            V.scalar_tensor_tensor(d[:, lo:lo + n], ps[:, u % 2, 0:n], gp, x[:, b, lo:lo + n], ALU.mult, ALU.add).then_inc(s_free, 1)
                        dve.wait_ge(s_sg, s * 2 + b + 1)
                        V.tensor_tensor(d[:, TP:T], sg[:, b, :], x[:, b, TP:T], ALU.add).then_inc(s_out, 1)


def normed(nc, K):
    with ExitStack() as c:
        tile = lambda n, s: c.enter_context(nc.sbuf_tensor("no_" + n, s, F32))
        ps = c.enter_context(nc.psum_tensor("no_ps", [P, 4, 512], F32))
        rs, sq, tmp = tile("rs", [P, T]), tile("sq", [P, 2, T]), tile("tmp", [P, KC, 2, SB, SL])
        a, p, v = stats_and_affine(nc, K, K["B2"], rs, sq, ps, [(K["B1"], M_KV + 8, M_KV), (K["B2"], M_B + 8, M_B)], 1)
        with nc.Block() as block:
            @block.scalar
            def _(act):
                a(act, lambda eng: None)

            @block.tensor
            def _(pe):
                p(pe)

            @block.vector
            def _(dve):
                v(dve, tmp)


def attention(nc, A, OUT, K):
    with ExitStack() as c:
        sem = lambda n: K["sem"]("at_" + n)
        tile = lambda n, s, dt=F32: c.enter_context(nc.sbuf_tensor("at_" + n, s, dt))
        psP = c.enter_context(nc.psum_tensor("at_psP", [P, 2, 512], F32))
        psS = c.enter_context(nc.psum_tensor("at_psS", [P, 4, 512], F32))
        psW = c.enter_context(nc.psum_tensor("at_psW", [P, 512], F32))
        psO = c.enter_context(nc.psum_tensor("at_psO", [P, 512], F32))
        w = {n: tile("w_" + n, [P, KC, P]) for n in "qkz"}
        w["v"] = w["q"]
        qT, kT, zs, rs = (tile(n, [P, T]) for n in ("qT", "kT", "zs", "rs"))
        v = tile("v", [P, NT + 1, DE])
        ko = tile("ko", [P, NT + 1, P])
        bias = tile("bias", [P, TP])
        sbias = tile("sbias", [SR, PAST + TS])
        bones = tile("bones", [P, P])
        comb, combr = tile("comb", [SR, TS]), tile("combr", [SR, TS])
        lamrow = tile("lamrow", [SR, 1])
        rowsel = tile("rowsel", [SR, 2])
        eps64, subg = tile("eps64", [P, 1]), tile("subg", [P, 1])
        S = tile("S", [P, 2, 2, TP])
        wT = tile("wT", [P, 2, TP])
        th = wT[:, 0, 0:2 * THIRD].rearrange("p (a t) -> p a t", a=2)
        sq = S[:, 1, :, :].rearrange("p c k -> p (c k)")[:, 0:T]
        kcT = S[:, 0, 0, :].rearrange("p (a k) -> p a k", a=2)
        SS = S[0:SR, 0, 1, 0:PAST + TS]
        nmx, rsum, rr = tile("nmx", [P, 2, 2]), tile("rsum", [P, 2, 2]), tile("rr", [P, 2, 2])
        QZ, QN = tile("QZ", [P, SB * (SR + SL)]), tile("QN", [P, SR])
        kc, vc = tile("kc", [P, SB * NPG, P]), tile("vc", [P, SB * NPG, DE])
        snm, ssum, srr = tile("snm", [SR, 2]), tile("ssum", [SR, 1]), tile("srr", [SR, 2])
        wsT = tile("wsT", [P, NPG + 1, TS])
        pt = tile("pt", [1, SB * NPG], I32)
        hk, hb, G, ident, ones, vec = K["B1"], K["B2"], K["G"], K["ident"], K["ones"], K["vec"]

        passed = {n: K["sem"]("passed_" + n) for n in ("sp", "pool", "act", "dve")}
        s_const, s_pt, s_set, s_init = sem("const_in"), sem("pages_in"), sem("set"), sem("init")
        s_w = {n: sem(f"w_{n}_in") for n in "qkzv"}
        s_kc, s_vc = sem("kcache_in"), sem("vcache_in")
        s_proj, s_pfree = sem("proj_summed"), sem("proj_bank_free")
        s_qk, s_sq, s_v = sem("qk_copied"), sem("qk_squares"), sem("v_ready")
        s_rs, s_qn, s_zs = sem("qk_rstd"), sem("qk_ready"), sem("z_ready")
        s_kops, s_ko, s_kst = sem("k_turned"), sem("k_out_ready"), sem("kv_stored")
        s_bias = sem("bias_ready")
        s_sc, s_min, s_exp, s_rec, s_r1, s_p1, s_wc = (sem("scores_summed"), sem("min_ready"), sem("exp_ready"), sem("recip"),
                                                       sem("recip_lam"), sem("p1_scaled"), sem("weights_ready"))
        s_wps, s_wT, s_pv, s_oev = sem("weights_turned"), sem("wT_ready"), sem("out_summed"), sem("out_copied")
        s_qz, s_kcps, s_kcT, s_ssc, s_smin, s_sexp = (sem("qz_ready"), sem("kcache_turned"), sem("kcT_ready"), sem("sscores_summed"),
                                                      sem("smin_ready"), sem("sexp_ready"))
        s_srec, s_comb, s_wsps, s_wsT, s_spv, s_soev = (sem("srecip"), sem("comb_ready"), sem("sweights_turned"), sem("wsT_ready"),
                                                        sem("sout_summed"), sem("sout_copied"))
        s_osq, s_oss, s_oln, s_ors, s_g1, s_g2 = (sem("o_squares"), sem("o_sums"), sem("o_log"), sem("o_rstd"),
                                                  sem("o_normed"), sem("o_gated"))
        UNITS = 18
        GROUPS = [(r, min(r + 4, NT + 1)) for r in range(0, NT + 1, 4)]
        WG = [(i + 4) // 4 for i in range(NT)]
        WB = [sum(WG[:i]) for i in range(NT + 1)]
        wd = {"q": A["w_in_b"].rearrange("(k p) n -> p k n", p=P)[:, :, 0:D], "z": A["w_in_b"].rearrange("(k p) n -> p k n", p=P)[:, :, D:2 * D],
              "k": A["w_k"].rearrange("(k p) n -> p k n", p=P), "v": A["w_v"].rearrange("(k p) n -> p k n", p=P)}

        with nc.Block() as block:
            @block.sync
            def _(sp):
                for dst, name in ((bias, "bias"), (sbias, "sbias"), (bones, "bones"), (comb, "comb"), (rowsel, "lamsel")):
                    sp.dma_start(dst[:], A[name]).then_inc(s_const, 16)
                sp.dma_start(pt[:], A["page_table"].rearrange("b n -> (b n)").unsqueeze(0)).then_inc(s_pt, 16)
                sp.sem_inc(s_proj, UNITS)
                sp.wait_ge(s_pt, 16)
                with sp.Fori(0, HB) as i:
                    for name, used in (("q", 12), ("k", 6), ("z", 9), ("v", UNITS + 3)):
                        sp.wait_ge(s_proj, i * UNITS + used)
                        sp.dma_start(w[name][:], wd[name][:, :, bass.ds(i * P, P)]).then_inc(s_w[name], 16)
                    sp.wait_ge(s_kcps, i * SB)
                    apart(sp, passed["sp"])
                    with sp.Fori(0, SB * NPG) as n:
                        page = sp.value_load(pt[0:1, bass.ds(n, 1)], min_val=0, max_val=A["cache_k"].shape[0] - 1)
                        sp.dma_start(kc[:, bass.ds(n, 1), :], A["cache_k"][bass.ds(page, 1), :, bass.ds(i, 1), :].rearrange("n p h d -> p (n h) d")).then_inc(s_kc, 16)
                    sp.wait_ge(s_spv, i)
                    apart(sp, passed["sp"])
                    with sp.Fori(0, SB * NPG) as n:
                        page = sp.value_load(pt[0:1, bass.ds(n, 1)], min_val=0, max_val=A["cache_v"].shape[0] - 1)
                        sp.dma_start(vc[:, bass.ds(n, 1), :], A["cache_v"][bass.ds(page, 1), :, bass.ds(i, 1), :].rearrange("n p h d -> p (n h) d")).then_inc(s_vc, 16)

            @block.gpsimd
            def _(pool):
                nc.gpsimd.memset(QZ[:], 0.0).then_inc(s_set, 1)
                nc.gpsimd.memset(QN[:], 0.0).then_inc(s_set, 1)
                nc.gpsimd.memset(eps64[:], EPS * DQ).then_inc(s_set, 1)
                with pool.Fori(0, HB) as i:
                    for t in range(NT):
                        n = P * (t + 1)
                        pool.wait_ge(s_r1, NT * i + t + 1)
                        apart(pool, passed["pool"])
                        nc.gpsimd.tensor_scalar(S[:, t % 2, 1, 0:n], S[:, t % 2, 1, 0:n], rr[:, t % 2, 1:2], None, ALU.mult).then_inc(s_p1, 1)

            @block.tensor
            def _(pe):
                pe.wait_ge(s_const, 16 * 5)
                with pe.Fori(0, HB) as i:
                    unit = [0]

                    def bank():
                        pe.wait_ge(s_pfree, i * UNITS + unit[0] + 1)
                        b = unit[0] % 2
                        unit[0] += 1
                        return b

                    for name, src in (("q", hb), ("k", hk), ("z", hb)):
                        pe.wait_ge(s_w[name], 16 * (i + 1))
                        for j in range(3):
                            b = bank()
                            for k in range(KC):
                                mm = nc.tensor.matmul(psP[:, b, 0:THIRD], w[name][:, k, :], thirds(src[:, k, :])[j], start=(k == 0), stop=(k == KC - 1))
                            mm.then_inc(s_proj, 1)
                    pe.wait_ge(s_w["v"], 16 * (i + 1))
                    for lo, hi in GROUPS:
                        b = bank()
                        for t in range(lo, hi):
                            n = P if t < NT else TS
                            for k in range(KC):
                                mm = nc.tensor.matmul(psP[0:n, b, (t - lo) * P:(t - lo + 1) * P], hk[:, k, t * P:t * P + n], w["v"][:, k, :],
                                                      start=(k == 0), stop=(k == KC - 1))
                        mm.then_inc(s_proj, 1)
                    for r in range(2):
                        pe.wait_ge(s_sq, 2 * i + r + 1)
                        for j in range(3):
                            b = bank()
                            nc.tensor.matmul(psP[:, b, 0:THIRD], bones[:], thirds(sq)[j], start=True, stop=True).then_inc(s_proj, 1)
                    assert unit[0] == UNITS
                    pe.wait_ge(s_qn, 2 * i + 2)
                    pe.wait_ge(s_v, 3 * i + 3)

                    def turn_k(r):
                        lo, hi = GROUPS[r]
                        pe.wait_ge(s_ko, 3 * i + r)
                        for t in range(lo, hi):
                            n = P if t < NT else TS
                            mm = nc.tensor.transpose(psW[0:n, (t - lo) * P:(t - lo + 1) * P], kT[:, t * P:t * P + n], ident[:])
                        mm.then_inc(s_kops, 1)

                    def scores(t):
                        for comp in range(2):
                            rows = slice(DQ * comp, DQ * (comp + 1))
                            if t:
                                pe.wait_ge(s_min, 2 * NT * i + 2 * (t - 1) + comp + 1)
                            for lo in range(0, P * (t + 1), 512):
                                hi = min(lo + 512, P * (t + 1))
                                mm = nc.tensor.matmul(psS[:, 2 * comp + lo // 512, 0:hi - lo], qT[rows, t * P:(t + 1) * P], kT[rows, lo:hi], start=True, stop=True)
                            mm.then_inc(s_sc, 1)

                    def weigh(t):
                        pe.wait_ge(s_wc, NT * i + t + 1)
                        for r in range(WG[t]):
                            lo, hi = 4 * r, min(4 * r + 4, t + 1)
                            pe.wait_ge(s_wT, WB[NT] * i + WB[t] + r)
                            for k in range(lo, hi):
                                mm = nc.tensor.transpose(psW[:, (k - lo) * P:(k - lo + 1) * P], S[:, t % 2, 0, k * P:(k + 1) * P], ident[:])
                            mm.then_inc(s_wps, 1)

                    def values(t):
                        pe.wait_ge(s_wT, WB[NT] * i + WB[t + 1])
                        if t:
                            pe.wait_ge(s_oev, NT * i + t)
                        for k in range(t + 1):
                            mm = nc.tensor.matmul(psO[:, (t % 2) * P:(t % 2 + 1) * P], v[:, k, :], wT[:, t % 2, k * P:(k + 1) * P], start=(k == 0), stop=(k == t))
                        mm.then_inc(s_pv, 1)

                    pe.wait_ge(s_ors, i)
                    for r in range(3):
                        turn_k(r)
                    scores(0)
                    pe.wait_ge(s_ko, 3 * i + 3)
                    for t in range(NT):
                        if t + 1 < NT:
                            scores(t + 1)
                        weigh(t)
                        if t:
                            values(t - 1)
                    values(NT - 1)
                    pe.wait_ge(s_qz, i + 1)
                    pe.wait_ge(s_kc, 16 * SB * NPG * (i + 1))
                    pe.wait_ge(s_min, 2 * NT * (i + 1))

                    def turn_cache(b):
                        if b:
                            pe.wait_ge(s_kcT, SB * i + b)
                        for g in range(NPG):
                            mm = nc.tensor.transpose(psW[:, g * PAGE:(g + 1) * PAGE], kc[:, b * NPG + g, :], ident[:])
                        mm.then_inc(s_kcps, 1)

                    turn_cache(0)
                    nc.tensor.matmul(psS[0:SR, 1, 0:TS], QN[:], kT[:, TP:T], start=True, stop=True)
                    for b in range(SB):
                        if b + 1 < SB:
                            turn_cache(b + 1)
                        pe.wait_ge(s_kcT, SB * i + b + 1)
                        mm = nc.tensor.matmul(psS[0:SR, 0, :], QZ[:, b * SR:(b + 1) * SR], kcT[:, b % 2, :], start=(b == 0), stop=(b == SB - 1))
                    mm.then_inc(s_ssc, 1)
                    pe.wait_ge(s_comb, i + 1)
                    for g in range(NPG):
                        nc.tensor.matmul(psW[:, g * TS:(g + 1) * TS], SS[:, g * PAGE:(g + 1) * PAGE], combr[:], start=True, stop=True)
                    nc.tensor.matmul(psW[0:TS, NPG * TS:(NPG + 1) * TS], SS[:, PAST:PAST + TS], combr[:], start=True, stop=True).then_inc(s_wsps, 1)
                    pe.wait_ge(s_wsT, 2 * (i + 1))
                    pe.wait_ge(s_vc, 16 * SB * NPG * (i + 1))
                    pe.wait_ge(s_oev, NT * (i + 1))
                    for b in range(SB):
                        for g in range(NPG):
                            nc.tensor.matmul(psO[:, b * SL:(b + 1) * SL], vc[:, b * NPG + g, :], wsT[:, g, b * SL:(b + 1) * SL], start=(b == 0 and g == 0), stop=False)
                    nc.tensor.matmul(psO[:, 0:TS], v[0:TS, NT, :], wsT[0:TS, NPG, :], start=False, stop=True).then_inc(s_spv, 1)
                    pe.wait_ge(s_osq, i + 1)
                    pe.wait_ge(s_smin, 2 * (i + 1))
                    for j in range(3):
                        mm = nc.tensor.matmul(psS[:, j, 0:THIRD], ones[:], thirds(sq)[j], start=True, stop=True)
                    mm.then_inc(s_oss, 1)

            @block.scalar
            def _(act):
                A_ = nc.scalar.activation
                act.sem_inc(s_pfree, 2)
                act.wait_ge(s_set, 3)
                with act.Fori(0, HB) as i:
                    unit = [UNITS]

                    def done():
                        unit[0] += 1
                        act.wait_ge(s_proj, i * UNITS + unit[0])
                        return (unit[0] - 1) % 2

                    act.wait_ge(s_g2, i)
                    act.wait_ge(s_kst, 64 * i)
                    for r, dst in enumerate((qT, kT)):
                        if r:
                            act.wait_ge(s_proj, i * UNITS + UNITS + 3)
                        for j in range(3):
                            A_(thirds(dst[:])[j], psP[:, done(), 0:THIRD], ACT.Copy).then_inc(s_qk, 1)
                            act.wait_ge(s_qk, 6 * i + 3 * r + j + 1)
                            act.sem_inc(s_pfree, 1)
                    A_(sq, qT[:], ACT.Square).then_inc(s_sq, 1)
                    for j in range(3):
                        b = done()
                        if j == 2:
                            act.wait_ge(s_zs, 3 * i + 1)
                        A_(thirds(zs[:])[j], psP[:, b, 0:THIRD], ACT.Copy, scale=0.5)
                        A_(th[:, j % 2, :], psP[:, b, 0:THIRD], ACT.Tanh, scale=0.5).then_inc(s_pfree, 1)
                    for lo, hi in GROUPS:
                        b = done()
                        n = P if lo < NT else TS
                        A_(v[0:n, lo:hi, :].rearrange("p a d -> p (a d)"), psP[0:n, b, 0:(hi - lo) * P], ACT.Copy).then_inc(s_v, 1)
                        act.wait_ge(s_v, 3 * i + lo // 4 + 1)
                        act.sem_inc(s_pfree, 1)
                    apart(act, passed["act"])
                    act.dma_start(OUT["v_p"][:, bass.ds(i, 1), :].rearrange("(t p) h e -> p t (h e)", p=P), v[:, 0:NT, :]).then_inc(s_kst, 16)
                    act.dma_start(OUT["v_s"][:, bass.ds(i, 1), :].rearrange("p h e -> p (h e)"), v[0:TS, NT, :]).then_inc(s_kst, 16)
                    for r, e in enumerate((eps64, K["eps"])):
                        if r:
                            act.wait_ge(s_qn, 2 * i + 1)
                        for j in range(3):
                            A_(thirds(rs[:])[j], psP[:, done(), 0:THIRD], ACT.Ln, scale=1.0 if r == 0 else 1.0 / DQ, bias=e[:, 0:1]).then_inc(s_pfree, 1)
                        if r == 0:
                            A_(sq, kT[:], ACT.Square).then_inc(s_sq, 1)
                        act.wait_ge(s_pfree, 2 + i * UNITS + 15 + 3 * r)
                        A_(rs[:], rs[:], ACT.Exp, scale=-0.5).then_inc(s_rs, 1)
                    for r, (lo, hi) in enumerate(GROUPS):
                        act.wait_ge(s_kops, 3 * i + r + 1)
                        n = P if lo < NT else TS
                        A_(ko[0:n, lo:hi, :].rearrange("p a d -> p (a d)"), psW[0:n, 0:(hi - lo) * P], ACT.Copy).then_inc(s_ko, 1)

                    act.wait_ge(s_ko, 3 * (i + 1))
                    act.dma_start(OUT["k_p"][:, bass.ds(i, 1), :].rearrange("(t p) h e -> p t (h e)", p=P), ko[:, 0:NT, :]).then_inc(s_kst, 16)
                    act.dma_start(OUT["k_s"][:, bass.ds(i, 1), :].rearrange("p h e -> p (h e)"), ko[0:TS, NT, :]).then_inc(s_kst, 16)

                    def exps(t):
                        n = P * (t + 1)
                        for comp in range(2):
                            act.wait_ge(s_min, 2 * NT * i + 2 * t + comp + 1)
                            s = S[:, t % 2, comp, 0:n]
                            A_(s, s, ACT.Exp, scale=-1.0, bias=nmx[:, t % 2, comp:comp + 1], accum_out=rsum[:, t % 2, comp:comp + 1]).then_inc(s_exp, 1)

                    def copies(t):
                        for r in range(WG[t]):
                            lo, hi = 4 * r, min(4 * r + 4, t + 1)
                            act.wait_ge(s_wps, WB[NT] * i + WB[t] + r + 1)
                            if t >= 2:
                                act.wait_ge(s_pv, NT * i + t - 1)
                            A_(wT[:, t % 2, lo * P:hi * P], psW[:, 0:(hi - lo) * P], ACT.Copy).then_inc(s_wT, 1)

                    def out(t):
                        act.wait_ge(s_pv, NT * i + t + 1)
                        apart(act, passed["act"])
                        A_(G[:, bass.ds(i, 1), t * P:(t + 1) * P].rearrange("p a t -> p (a t)"), psO[:, (t % 2) * P:(t % 2 + 1) * P], ACT.Copy).then_inc(s_oev, 1)

                    exps(0)
                    for t in range(NT):
                        if t + 1 < NT:
                            exps(t + 1)
                        copies(t)
                        if t:
                            out(t - 1)
                    out(NT - 1)
                    for b in range(SB):
                        act.wait_ge(s_kcps, SB * i + b + 1)
                        A_(kcT[:, b % 2, :], psW[:], ACT.Copy).then_inc(s_kcT, 1)
                    act.wait_ge(s_smin, 2 * (i + 1))
                    A_(SS, SS, ACT.Exp, scale=-1.0, bias=snm[:, 1:2], accum_out=ssum[:]).then_inc(s_sexp, 1)
                    act.wait_ge(s_wsps, i + 1)
                    A_(wsT[:, 0:NPG, :].rearrange("p a d -> p (a d)"), psW[:, 0:NPG * TS], ACT.Copy).then_inc(s_wsT, 1)
                    A_(wsT[0:TS, NPG, :], psW[0:TS, NPG * TS:(NPG + 1) * TS], ACT.Copy).then_inc(s_wsT, 1)
                    g = G[:, bass.ds(i, 1), :].rearrange("p a t -> p (a t)")
                    act.wait_ge(s_spv, i + 1)
                    apart(act, passed["act"])
                    A_(g[:, TP:T], psO[:, 0:TS], ACT.Copy).then_inc(s_soev, 1)
                    act.wait_ge(s_soev, i + 1)
                    act.wait_ge(s_oev, NT * (i + 1))
                    apart(act, passed["act"])
                    A_(sq, g, ACT.Square).then_inc(s_osq, 1)
                    act.wait_ge(s_oss, i + 1)
                    A_(rs[:].rearrange("p (j t) -> p j t", j=3), psS[:, 0:3, 0:THIRD], ACT.Ln, scale=1.0 / DE, bias=K["eps"][:, 0:1]).then_inc(s_oln, 1)
                    act.wait_ge(s_oln, i + 1)
                    A_(rs[:], rs[:], ACT.Exp, scale=-0.5).then_inc(s_ors, 1)
                act.wait_ge(s_kst, 64 * HB)

            @block.vector
            def _(dve):
                V = nc.vector
                lam_init = 0.8 - 0.6 * float(np.exp(-0.3))
                dve.wait_ge(s_const, 16 * 5)
                V.tensor_scalar(subg[:], vec[:, V_SUBLN:V_SUBLN + 1], 1.0 - lam_init, None, ALU.mult).then_inc(s_init, 1)
                V.scalar_tensor_tensor(lamrow[:], rowsel[:, 1:2], K["nlam"][0:SR, 0:1], rowsel[:, 0:1], ALU.mult, ALU.add).then_inc(s_init, 1)
                dve.wait_ge(s_init, 2)
                dve.wait_ge(s_set, 3)
                with dve.Fori(0, HB) as i:
                    V.tensor_scalar(bias[:], bias[:], 0.5, None, ALU.mult).then_inc(s_bias, 1)
                    V.tensor_scalar(sbias[:], sbias[:], 0.5, None, ALU.mult).then_inc(s_bias, 1)
                    for j in range(3):
                        dve.wait_ge(s_pfree, 2 + i * UNITS + 6 + j + 1)
                        z = thirds(zs[:])[j]
                        V.scalar_tensor_tensor(z, th[:, j % 2, :], 1.0, z, ALU.add, ALU.mult).then_inc(s_zs, 1)
                    for r, (dst, col) in enumerate(((qT, V_GQ), (kT, V_GK))):
                        dve.wait_ge(s_rs, 2 * i + r + 1)
                        dve.wait_ge(s_sq, 2 * i + r + 1)
                        V.scalar_tensor_tensor(dst[:], dst[:], vec[:, col:col + 1], rs[:], ALU.mult, ALU.mult).then_inc(s_qn, 1)
                    dve.wait_ge(s_qn, 2 * i + 2)
                    for comp in range(2):
                        rows = slice(DQ * comp, DQ * (comp + 1))
                        V.tensor_copy(QZ[rows, :].rearrange("p (b r) -> p b r", r=SR + SL)[:, :, comp * TS:comp * TS + SL],
                                      qT[rows, TP:T].rearrange("p (b t) -> p b t", b=SB))
                        last = V.tensor_copy(QN[rows, comp * TS:(comp + 1) * TS], qT[rows, TP:T])
                    last.then_inc(s_qz, 1)
                    dve.wait_ge(s_bias, 2 * (i + 1))

                    def mins(t):
                        n = P * (t + 1)
                        for comp in range(2):
                            dve.wait_ge(s_sc, 2 * NT * i + 2 * t + comp + 1)
                            if t >= 2:
                                dve.wait_ge(s_wps, WB[NT] * i + WB[t - 1])
                                dve.wait_ge(s_wc, NT * i + t - 1)
                            apart(dve, passed["dve"])
                            V.tensor_tensor_reduce(S[:, t % 2, comp, 0:n], psS[:, 2 * comp:2 * comp + 2, :].rearrange("p a k -> p (a k)")[:, 0:n],
                                                   bias[:, TP - n:TP], -1.0, 3.0e38, ALU.add, ALU.min, nmx[:, t % 2, comp:comp + 1]).then_inc(s_min, 1)

                    def combine(t):
                        n = P * (t + 1)
                        dve.wait_ge(s_exp, 2 * NT * i + 2 * t + 2)
                        V.reciprocal(rr[:, t % 2, :], rsum[:, t % 2, :]).then_inc(s_rec, 1)
                        dve.wait_ge(s_rec, NT * i + t + 1)
                        V.tensor_tensor(rr[:, t % 2, 1:2], rr[:, t % 2, 1:2], K["nlam"][:], ALU.mult).then_inc(s_r1, 1)
                        dve.wait_ge(s_p1, NT * i + t + 1)
                        V.scalar_tensor_tensor(S[:, t % 2, 0, 0:n], S[:, t % 2, 0, 0:n], rr[:, t % 2, 0:1], S[:, t % 2, 1, 0:n],
                                               ALU.mult, ALU.add).then_inc(s_wc, 1)

                    mins(0)
                    for t in range(NT):
                        if t + 1 < NT:
                            mins(t + 1)
                        combine(t)
                    dve.wait_ge(s_ssc, i + 1)
                    apart(dve, passed["dve"])
                    V.tensor_tensor_reduce(SS[:, 0:PAST], psS[0:SR, 0, :], sbias[:, 0:PAST], -1.0, 3.0e38, ALU.add, ALU.min, snm[:, 0:1]).then_inc(s_smin, 1)
                    dve.wait_ge(s_smin, 2 * i + 1)
                    apart(dve, passed["dve"])
                    V.tensor_tensor_reduce(SS[:, PAST:PAST + TS], psS[0:SR, 1, 0:TS], sbias[:, PAST:PAST + TS], -1.0, snm[:, 0:1], ALU.add, ALU.min,
                                           snm[:, 1:2]).then_inc(s_smin, 1)
                    dve.wait_ge(s_sexp, i + 1)
                    V.reciprocal(srr[:, 0:1], ssum[:]).then_inc(s_srec, 1)
                    dve.wait_ge(s_srec, 2 * i + 1)
                    V.tensor_tensor(srr[:, 1:2], srr[:, 0:1], lamrow[:], ALU.mult).then_inc(s_srec, 1)
                    dve.wait_ge(s_srec, 2 * i + 2)
                    V.tensor_scalar(combr[:], comb[:], srr[:, 1:2], None, ALU.mult).then_inc(s_comb, 1)
                    dve.wait_ge(s_ors, i + 1)
                    g = G[:, bass.ds(i, 1), :].rearrange("p a t -> p (a t)")
                    V.scalar_tensor_tensor(g, g, subg[:, 0:1], rs[:], ALU.mult, ALU.mult).then_inc(s_g1, 1)
                    dve.wait_ge(s_g1, i + 1)
                    dve.wait_ge(s_zs, 3 * i + 3)
                    V.tensor_tensor(g, g, zs[:], ALU.mult).then_inc(s_g2, 1)


def store_y(nc, OUT, K):
    with ExitStack() as c:
        sem = lambda n: K["sem"]("st_" + n)
        ps = c.enter_context(nc.psum_tensor("st_ps", [P, 4, 512], F32))
        y = c.enter_context(nc.sbuf_tensor("st_y", [P, NT + 1, D], F32))
        s_ps, s_y = sem("turned"), sem("copied")
        s_out = sem("y_out")
        B, ident = K["B1"], K["ident"]
        with nc.Block() as block:
            @block.tensor
            def _(pe):
                for u in range(2 * (NT + 1)):
                    t, half = u // 2, u % 2
                    n = P if t < NT else TS
                    if u >= 4:
                        pe.wait_ge(s_y, u - 3)
                    for q in range(4):
                        mm = nc.tensor.transpose(ps[0:n, u % 4, q * P:(q + 1) * P], B[:, 4 * half + q, t * P:t * P + n], ident[:])
                    mm.then_inc(s_ps, 1)

            @block.scalar
            def _(act):
                for u in range(2 * (NT + 1)):
                    t, half = u // 2, u % 2
                    n = P if t < NT else TS
                    act.wait_ge(s_ps, u + 1)
                    nc.scalar.activation(y[0:n, t, half * 512:(half + 1) * 512], ps[0:n, u % 4, :], ACT.Copy).then_inc(s_y, 1)

            @block.sync
            def _(sp):
                for t in range(NT + 1):
                    sp.wait_ge(s_y, 2 * t + 2)
                    if t < NT:
                        sp.dma_start(OUT["y_p"][t * P:(t + 1) * P, :], y[:, t, :]).then_inc(s_out, 16)
                    else:
                        sp.dma_start(OUT["y_s"], y[0:TS, t, :]).then_inc(s_out, 16)
                sp.wait_ge(s_out, 16 * (NT + 1))



def shape_constants():
    s, t = np.arange(P)[:, None], np.arange(P)[None, :]
    f = np.float32

    def level(L):
        return (s // (2 * L) == t // (2 * L)) & (s % (2 * L) < L) & (t % (2 * L) >= L)

    masks = np.stack([level(L) for L in LEVELS] + [s == t], 1).astype(f)
    seq = (s // SL == t // SL)[:TS, :TS]
    smasks = np.stack([level(2)[:TS, :TS] & seq, level(1)[:TS, :TS] & seq, (s == t)[:TS, :TS]], 1).astype(f)
    restart = np.ones((P, T), f)
    restart[:, 0:TP:P] = 0.0
    restart[:, TP:T:SL] = 0.0
    rowsel = (np.arange(TS)[:, None] // SL == np.arange(SB)[None, :]).astype(f)
    x = np.arange(TP)[None, :] - np.arange(P)[:, None] - (TP - P)
    bias = np.where(x <= 0, x, NEG).astype(f)
    r = np.arange(SR)
    seq_r, q_r = (r % TS) // SL, r % SL
    past = np.arange(PAST)[None, :] - (PAST + q_r)[:, None]
    n = np.arange(TS)
    new = np.where((seq_r[:, None] == n[None, :] // SL) & (n[None, :] % SL <= q_r[:, None]), n[None, :] % SL - q_r[:, None], NEG)
    sbias = np.concatenate([past, new], 1).astype(f)
    bones = (s // DQ == t // DQ).astype(f)
    comb = (r[:, None] % TS == n[None, :]).astype(f)
    lamsel = np.stack([r < TS, r >= TS], 1).astype(f)
    return {"ident": np.eye(P, dtype=f), "ones": np.ones((P, P), f), "masks": masks, "smasks": smasks, "restart": restart, "rowsel": rowsel,
            "bias": bias, "sbias": sbias, "bones": bones, "comb": comb, "lamsel": lamsel}


_OUTS = {"y_p": (TP, D), "y_s": (TS, D), "state_p": (HA, DK, DV), "state_s": (SB, HA, DK, DV), "k_p": (TP, HB, P), "v_p": (TP, HB, DE),
         "k_s": (TS, HB, P), "v_s": (TS, HB, DE)}


def kernel(**inputs):
    import concourse.bacc as bacc
    from concourse.bass_utils import run_bass_kernel_spmd

    a = {k: np.asarray(v) for k, v in inputs.items()}
    flat = {
        "x_prompt": a["x_prompt"].reshape(TP, D), "x_sample": a["x_sample"].reshape(TS, D),
        "cache_k": a["cache_k"].reshape(-1, PAGE, HB, P), "cache_v": a["cache_v"].reshape(-1, PAGE, HB, DE),
        "state_gla": a["state_gla"].reshape(SB, HA, DK, DV),
    }
    for k in ("norm_a", "ada_w_a", "ada_b_a", "w_in_a", "w_g2_a", "b_g_a", "onorm_a", "w_out_a", "norm_b", "ada_w_b", "ada_b_b", "w_in_b",
              "g_q", "lambda_q1", "lambda_k1", "lambda_q2", "lambda_k2", "subln_b", "w_out_b"):
        flat[k] = a[k][0]
    for k in ("c_prompt", "c_sample", "page_table", "norm_kv", "ada_w_kv", "ada_b_kv", "w_k", "w_v", "g_k"):
        flat[k] = a[k]
    flat.update(shape_constants())
    nc = bacc.Bacc("TRN2", target_bir_lowering=False, num_devices=1)
    arrays, ins = {}, {}
    for name, x in flat.items():
        arrays["in_" + name] = np.ascontiguousarray(x)
        ins[name] = nc.dram_tensor("in_" + name, x.shape, mybir.dt.from_np(x.dtype), kind="ExternalInput").ap()
    outs = {name: nc.dram_tensor("out_" + name, shape, F32, kind="ExternalOutput").ap() for name, shape in _OUTS.items()}
    scratch = {name: nc.dram_tensor("scr_" + name, (D, T), F32, kind="Internal").ap() for name in ("xT", "x1T")}
    build(nc, ins, outs, scratch)
    r = run_bass_kernel_spmd(nc, [arrays], core_ids=[0]).results[0]
    o = {name: r["out_" + name] for name in _OUTS}
    return (o["y_p"].reshape(1, TP, D), o["y_s"].reshape(SB, SL, D), o["state_p"].reshape(1, 1, HA, DK, DV),
            o["state_s"].reshape(1, SB, HA, DK, DV), o["k_p"].reshape(1, TP, HB, 2, DQ), o["v_p"].reshape(1, TP, HB, DE),
            o["k_s"].reshape(SB, SL, HB, 2, DQ), o["v_s"].reshape(SB, SL, HB, DE))
```

```python
from contextlib import ExitStack

import numpy as np

import concourse.bass as bass
from concourse import mybir

F32 = mybir.dt.float32
F32R = mybir.dt.float32r
I32 = mybir.dt.int32
ALU = mybir.AluOpType
ACT = mybir.ActivationFunctionType
AX = mybir.AxisListType

P = 128
D = 1024
KC = D // P
TP = 1024
NT = TP // P
SB, SL = 8, 4
TS = SB * SL
T = TP + TS
NC = SB + 1
THIRD = T // 3
HA, DK, DV = 4, 128, 256
RANK = 16
HB, DQ, DE = 8, 64, 128
PAST, PAGE = 512, 128
NPG = PAST // PAGE
EPS = 1e-6
LEVELS = [64, 32, 16, 8, 4, 2, 1]
NL = len(LEVELS)
SLEV = [5, 6]
SR = 2 * TS
NEG = -1.0e30

V_ADA, V_NORM_A, V_NORM_KV, V_NORM_B, V_BG, V_ONORM, V_SUBLN, V_GQ, V_GK, V_N = 0, 64, 72, 80, 88, 92, 94, 95, 96, 97
M_A, M_KV, M_B, M_N = 0, 24, 40, 64


class Chain:

    def __init__(self, eng, sem, base=0):
        self.eng, self.sem, self.base, self.n = eng, sem, base, 0

    def link(self, instruction):
        self.n += 1
        instruction.then_inc(self.sem, 1)
        self.eng.wait_ge(self.sem, self.base + self.n)


def apart(eng, passed):
    eng.sem_inc(passed, 1)


def thirds(ap):
    return [ap[:, THIRD * j:THIRD * (j + 1)] for j in range(3)]


def bcast(ap, *shape):
    return ap.broadcast_to(list(shape))


def build(nc, A, OUT, SCR):
    g = ExitStack()
    with g:
        def sb(name, shape, ctx=g, dt=F32):
            return ctx.enter_context(nc.sbuf_tensor(name, shape, dt))

        def sem(name, ctx=g):
            return ctx.enter_context(nc.semaphore(name))

        made = {}

        def shared(name):
            if name not in made:
                made[name] = sem(name)
            return made[name]

        K = {"sem": shared}
        K["ident"] = sb("ident", [P, P])
        K["ones"] = sb("ones", [P, P])
        K["vec"] = sb("vec", [P, V_N])
        K["mod"] = sb("mod", [P, M_N, NC])
        K["eps"] = sb("eps", [P, 1])
        K["nlam"] = sb("nlam", [P, 1])
        K["cT"] = sb("cT", [P, KC, NC])
        K["w0"] = sb("w0", [P, KC, P])
        K["w1"] = sb("w1", [P, KC, P])
        K["wlow"] = sb("wlow", [P, KC, RANK])
        K["B1"] = sb("B1", [P, KC, T])
        K["B2"] = sb("B2", [P, KC, T])
        K["G"] = sb("G", [P, KC, T])
        setup(nc, A, SCR, K)
        gla(nc, A, OUT, K)
        with ExitStack() as c:
            acc, tmp = sb("no_acc", [P, T], c), sb("no_tmp", [P, 2, KC, SB, SL], c)
            sq = K["B1"][:, 2:4, :]
            rs = acc
            ps = c.enter_context(nc.psum_tensor("no_ps", [P, 4, 512], F32))
            norm = Norm(nc, K, K["B2"], rs, sq, acc, ps, [(K["B1"], M_KV + 8, M_KV), (K["B2"], M_B + 8, M_B)], 1)
            out_proj(nc, A["w_out_a"], SCR["xT"], SCR["x1T"], K["B2"], M_A + 16, K, 0, norm)
            normed(nc, A, K, norm, tmp)
        attention(nc, A, OUT, K)
        out_proj(nc, A["w_out_b"], SCR["x1T"], None, K["B1"], M_B + 16, K, 1)
        store_y(nc, OUT, K)


class Norm:

    def __init__(self, nc, K, src, rs, sq, acc, ps, affine, use):
        self.nc, self.K, self.src, self.rs, self.sq, self.acc, self.ps, self.affine, self.use = nc, K, src, rs, sq, acc, ps, affine, use
        self.sq_ready, self.sq_used = K["sem"]("n_sq_ready"), K["sem"]("n_sq_used")
        self.summed, self.ln_ready, self.rs_ready = K["sem"]("n_summed"), K["sem"]("n_ln_ready"), K["sem"]("n_rs_ready")
        self.xr_ready, self.s_mul = K["sem"]("n_xr_ready"), K["sem"]("n_s_mul")

    def act_square(self, eng, k):
        if k >= 3:
            eng.wait_ge(self.sq_used, self.use * (KC - 1) + k - 2)
        self.nc.scalar.activation(self.acc[:] if k == 0 else self.sq[:, k % 2, :], self.src[:, k, :], ACT.Square).then_inc(self.sq_ready, 1)

    def dve_add(self, eng, k, slot, first=False):
        eng.wait_ge(self.sq_ready, k + (self.use * KC + 1))
        if not first:
            eng.wait_ge(self.sq_used, k + (self.use * (KC - 1) - 1))
        self.nc.vector.tensor_tensor(self.acc[:], self.acc[:], self.sq[:, slot, :], ALU.add).then_inc(self.sq_used, 1)

    def pe_sum(self, eng):
        eng.wait_ge(self.sq_used, (self.use + 1) * (KC - 1))
        for j, part in enumerate(thirds(self.acc[:])):
            mm = self.nc.tensor.matmul(self.ps[:, j, 0:THIRD], self.K["ones"][:], part, start=True, stop=True)
        mm.then_inc(self.summed, 1)

    def act_rstd(self, eng):
        eng.wait_ge(self.summed, self.use + 1)
        self.nc.scalar.activation(self.rs[:].rearrange("p (j t) -> p j t", j=3), self.ps[:, 0:3, 0:THIRD], ACT.Ln,
                                  scale=1.0 / D, bias=self.K["eps"][:, 0:1]).then_inc(self.ln_ready, 1)
        eng.wait_ge(self.ln_ready, self.use + 1)
        self.nc.scalar.activation(self.rs[:], self.rs[:], ACT.Exp, scale=-0.5).then_inc(self.rs_ready, 1)

    def dve_rstd(self, eng):
        eng.wait_ge(self.rs_ready, self.use + 1)
        for k in range(KC):
            self.nc.vector.tensor_tensor(self.src[:, k, :], self.src[:, k, :], self.rs[:], ALU.mult).then_inc(self.xr_ready, 1)

    def act_affine(self, eng):
        mod = self.K["mod"]
        for k in range(KC):
            eng.wait_ge(self.xr_ready, self.use * KC + k + 1)
            for dst, a, b in self.affine:
                self.nc.scalar.activation(dst[:, k, 0:TP], self.src[:, k, 0:TP], ACT.Identity, scale=mod[:, a + k, 0:1], bias=mod[:, b + k, 0:1])

    def dve_samples(self, eng, tmp):
        mod = self.K["mod"]
        xs = self.src[:, :, TP:T].rearrange("p k (b t) -> p k b t", b=SB)
        eng.wait_ge(self.xr_ready, (self.use + 1) * KC)
        for n, (dst, a, b) in enumerate(self.affine):
            av = bcast(mod[:, a:a + KC, 1:NC].unsqueeze(3), P, KC, SB, SL)
            self.nc.vector.tensor_tensor(tmp[:, n], xs, av, ALU.mult).then_inc(self.s_mul, 1)
        eng.wait_ge(self.s_mul, self.use + len(self.affine))
        for n, (dst, a, b) in enumerate(self.affine):
            bv = bcast(mod[:, b:b + KC, 1:NC].unsqueeze(3), P, KC, SB, SL)
            self.nc.vector.tensor_tensor(dst[:, :, TP:T].rearrange("p k (b t) -> p k b t", b=SB), tmp[:, n], bv, ALU.add)


def setup(nc, A, SCR, K):
    with ExitStack() as c:
        sem = lambda n: K["sem"]("su_" + n)
        tile = lambda n, s: c.enter_context(nc.sbuf_tensor("su_" + n, s, F32))
        psT = c.enter_context(nc.psum_tensor("su_psT", [P, 2, 512], F32))
        psM = c.enter_context(nc.psum_tensor("su_psM", [P, 2, 512], F32))
        psS = c.enter_context(nc.psum_tensor("su_psS", [P, 4, 512], F32))
        rows = tile("rows", [V_N, P])
        crow = tile("crow", [NC, D])
        cth = tile("cth", [NC, D])
        cT = K["cT"]
        lam = tile("lam", [1, 4, DQ])
        lamp = tile("lamp", [1, DQ])
        lams = tile("lams", [1, 2])
        lame = tile("lame", [P, 2])
        XB = 3
        xt = tile("xt", [P, XB, D])
        mrow = tile("mrow", [NC, 2, 512])
        w = tile("w", [P, 4, KC, 256])
        rs = tile("rs", [P, T])
        sq = tile("sq", [P, 2, T])
        acc = tile("acc", [P, T])
        tmp = tile("tmp", [P, 1, KC, SB, SL])
        B1, mod, vec, ident, ones = K["B1"], K["mod"], K["vec"], K["ident"], K["ones"]
        s_tab = sem("tables_in")
        s_x = [sem(f"x_in{j}") for j in range(XB)]
        s_id, s_mrow, s_mT = sem("ident_in"), sem("mod_rows"), sem("mod_turned")
        s_w = [sem(f"w_in{j}") for j in range(4)]
        s_wfree, s_set = sem("w_used"), sem("eps_set")
        s_vecT, s_vec = sem("vec_turned"), sem("vec_ready")
        s_cth, s_csil, s_cps, s_cT = sem("c_tanh"), sem("c_silu"), sem("c_turned"), sem("cT_ready")
        s_lsum, s_lps, s_lexp, s_lam2 = sem("lam_sums"), sem("lam_bcast"), sem("lam_exp"), sem("lam_diff")
        s_xps, s_xev, s_mev, s_scl = sem("x_turned"), sem("x_copied"), sem("mod_ready"), sem("scales_ready")
        s_out = sem("xT_out")
        norm = Norm(nc, K, B1, rs, sq, acc, psS, [(B1, M_A + 8, M_A)], 0)
        GROUPS = 3
        TABS = 20

        def load_mod(eng, slots):
            wd = A["ada_w_a"].rearrange("(k p) n -> p k n", p=P)
            with eng.Fori(0, GROUPS) as i:
                for j in slots:
                    eng.wait_ge(s_wfree, i * 4 + j + 1)
                    apart(eng, passed[slots[0]])
                    eng.dma_start(w[:, j], wd[:, :, bass.ds(i * 1024 + 256 * j, 256)]).then_inc(s_w[j], 16)

        passed = {0: K["sem"]("passed_sp"), 1: K["sem"]("passed_pool"), "pe": K["sem"]("passed_pe")}
        with nc.Block() as block:
            @block.sync
            def _(sp):
                sp.dma_start(ident[:], A["ident"]).then_inc(s_id, 16)
                sp.dma_start(ones[:], A["ones"]).then_inc(s_tab, 16)
                sp.sem_inc(s_wfree, 4)
                at = 0
                for name, n in (("ada_b_a", 24), ("ada_b_kv", 16), ("ada_b_b", 24), ("norm_a", 8), ("norm_kv", 8), ("norm_b", 8),
                                ("b_g_a", 4), ("onorm_a", 2), ("subln_b", 1)):
                    sp.dma_start(rows[at:at + n, :], A[name].rearrange("(r c) -> r c", c=P)).then_inc(s_tab, 16)
                    at += n
                for name in ("g_q", "g_k"):
                    for half in range(2):
                        sp.dma_start(rows[at:at + 1, DQ * half:DQ * (half + 1)], A[name].unsqueeze(0)).then_inc(s_tab, 16)
                    at += 1
                sp.dma_start(crow[0:1, :], A["c_prompt"]).then_inc(s_tab, 16)
                sp.dma_start(crow[1:NC, :], A["c_sample"]).then_inc(s_tab, 16)
                for j, name in enumerate(("lambda_q1", "lambda_k1", "lambda_q2", "lambda_k2")):
                    sp.dma_start(lam[0:1, j, :], A[name].unsqueeze(0)).then_inc(s_tab, 16)
                load_mod(sp, (0, 2))
                sp.dma_start(K["wlow"][:], A["w_in_a"].rearrange("(k p) n -> p k n", p=P)[:, :, 3072:3088]).then_inc(K["sem"]("gl_low_in"), 16)

            @block.gpsimd
            def _(pool):
                nc.gpsimd.memset(K["eps"][:], EPS).then_inc(s_set, 1)
                load_mod(pool, (1, 3))
                for n in range(2):
                    pool.dma_start(K[f"w{n}"][:], A["w_in_a"].rearrange("(k p) n -> p k n", p=P)[:, :, 512 * n:512 * n + P]).then_inc(
                        K["sem"](("gl_w_q_in", "gl_w_k_in")[n]), 16)

            @block.tensor
            def _(pe):
                pe.wait_ge(s_id, 16)
                for t in range(NT + 1):
                    pe.wait_ge(s_x[t % XB], 16 * (t // XB + 1))
                    n = P if t < NT else TS
                    for half in range(2):
                        u = 2 * t + half
                        if u >= 2:
                            pe.wait_ge(s_xev, u - 1)
                        for q in range(4):
                            k = 4 * half + q
                            mm = nc.tensor.transpose(psT[:, u % 2, q * P:q * P + n], xt[0:n, t % XB, k * P:(k + 1) * P], ident[0:n, 0:n])
                        mm.then_inc(s_xps, 1)
                    if t == 2:
                        pe.wait_ge(s_tab, 16 * TABS)
                        nc.tensor.transpose(psM[:, 0, 0:V_N], rows[:], ident[0:V_N, 0:V_N]).then_inc(s_vecT, 1)
                        pe.wait_ge(s_csil, 1)
                        for k in range(KC):
                            mm = nc.tensor.transpose(psM[:, 1, k * NC:(k + 1) * NC], crow[:, k * P:(k + 1) * P], ident[0:NC, 0:NC])
                        mm.then_inc(s_cps, 1)
                pe.wait_ge(s_lsum, 2)
                pe.wait_ge(s_vec, 1)
                nc.tensor.matmul(psM[:, 0, 0:2], ones[0:1, :], lams[0:1, :], start=True, stop=True).then_inc(s_lps, 1)
                pe.wait_ge(s_xev, 2 * (NT + 1))
                pe.wait_ge(s_cT, 1)
                pe.wait_ge(s_lexp, 1)
                def modulations(i):
                    for j in range(4):
                        pe.wait_ge(s_w[j], (i + 1) * 16)
                        for k in range(KC):
                            mm = nc.tensor.matmul(psM[0:NC, j // 2, (j % 2) * 256:(j % 2 + 1) * 256], cT[:, k, :], w[:, j, k, :],
                                                  start=(k == 0), stop=(k == KC - 1))
                        mm.then_inc(s_wfree, 1)
                    for b in range(2):
                        pe.wait_ge(s_mrow, 2 * i + b + 1)
                        pe.wait_ge(s_mev, 2 * i + b + 1)
                        apart(pe, passed["pe"])
                        for m in range(4):
                            mm = nc.tensor.transpose(psT[:, b, m * NC:(m + 1) * NC], mrow[:, b, m * P:(m + 1) * P], ident[0:NC, 0:NC])
                        mm.then_inc(s_mT, 1)

                modulations(0)
                norm.pe_sum(pe)
                with pe.Fori(1, GROUPS) as i:
                    modulations(i)

            @block.scalar
            def _(act):
                def load_x(t):
                    if t < NT:
                        act.dma_start(xt[:, t % XB, :], A["x_prompt"][t * P:(t + 1) * P, :]).then_inc(s_x[t % XB], 16)
                    else:
                        act.dma_start(xt[0:TS, t % XB, :], A["x_sample"]).then_inc(s_x[t % XB], 16)

                for t in range(XB):
                    load_x(t)
                act.wait_ge(s_tab, 16 * TABS)
                nc.scalar.activation(cth[:], crow[:], ACT.Tanh, scale=0.5).then_inc(s_cth, 1)
                for t in range(XB, NT + 1):
                    act.wait_ge(s_xps, 2 * (t - XB + 1))
                    load_x(t)
                act.wait_ge(s_lps, 1)
                nc.scalar.activation(lame[:], psM[:, 0, 0:2], ACT.Exp).then_inc(s_lexp, 1)
                act.wait_ge(s_xev, 2 * (NT + 1))
                act.dma_start(SCR["xT"].rearrange("(k p) t -> p k t", p=P), B1[:]).then_inc(s_out, 16)
                act.wait_ge(s_set, 1)
                for k in range(KC):
                    norm.act_square(act, k)
                norm.act_rstd(act)
                act.wait_ge(s_scl, 1)
                norm.act_affine(act)

            @block.vector
            def _(dve):
                for u in range(2 * (NT + 1)):
                    if u == 6:
                        dve.wait_ge(s_cth, 1)
                        dve.wait_ge(s_tab, 16 * TABS)
                        nc.vector.scalar_tensor_tensor(cth[:], cth[:], 1.0, crow[:], ALU.add, ALU.mult).then_inc(s_cth, 1)
                        dve.wait_ge(s_cth, 2)
                        nc.vector.tensor_scalar(crow[:], cth[:], 0.5, None, ALU.mult).then_inc(s_csil, 1)
                        dve.wait_ge(s_tab, 16 * TABS)
                        for j in range(2):
                            if j:
                                dve.wait_ge(s_lsum, 1)
                            nc.vector.tensor_tensor_reduce(lamp[:], lam[0:1, 2 * j, :], lam[0:1, 2 * j + 1, :], 1.0, 0.0, ALU.mult, ALU.add,
                                                           lams[0:1, j:j + 1]).then_inc(s_lsum, 1)
                        dve.wait_ge(s_vecT, 1)
                        nc.vector.tensor_copy(vec[:], psM[:, 0, 0:V_N]).then_inc(s_vec, 1)
                        dve.wait_ge(s_cps, 1)
                        nc.vector.tensor_copy(cT[:].rearrange("p k c -> p (k c)"), psM[:, 1, 0:KC * NC]).then_inc(s_cT, 1)
                    dve.wait_ge(s_xps, u + 1)
                    t, half = u // 2, u % 2
                    n = P if t < NT else TS
                    nc.vector.tensor_copy(B1[:, 4 * half:4 * half + 4, t * P:t * P + n],
                                          psT[:, u % 2, :].rearrange("p (q t) -> p q t", q=4)[:, :, 0:n]).then_inc(s_xev, 1)
                lam_init = 0.8 - 0.6 * float(np.exp(-0.3))
                dve.wait_ge(s_lexp, 1)
                nc.vector.tensor_tensor(K["nlam"][:], lame[:, 1:2], lame[:, 0:1], ALU.subtract).then_inc(s_lam2, 1)
                dve.wait_ge(s_lam2, 1)
                nc.vector.tensor_scalar(K["nlam"][:], K["nlam"][:], -lam_init, None, ALU.add)
                for k in range(1, KC):
                    norm.dve_add(dve, k, k % 2, k == 1)
                dve.wait_ge(s_vec, 1)
                dve.sem_inc(s_mev, 2)

                def modulations(i):
                    for b in range(2):
                        dve.wait_ge(s_wfree, i * 4 + 2 * b + 6)
                        nc.vector.tensor_copy(mrow[:, b, :], psM[0:NC, b, :]).then_inc(s_mrow, 1)
                    for b in range(2):
                        dve.wait_ge(s_mT, 2 * i + b + 1)
                        at = i * 8 + 4 * b
                        nc.vector.tensor_tensor(mod[:, bass.ds(at, 4), :], psT[:, b, 0:4 * NC].rearrange("p (m c) -> p m c", c=NC),
                                                bcast(vec[:, bass.ds(at, 4)].unsqueeze(2), P, 4, NC), ALU.add).then_inc(s_mev, 1)

                modulations(0)
                dve.wait_ge(s_out, 16)
                norm.dve_rstd(dve)
                modulations(1)
                dve.wait_ge(s_mev, 2 + 4)
                nc.vector.scalar_tensor_tensor(mod[:, M_A + 8:M_A + 16, :], mod[:, M_A + 8:M_A + 16, :], 1.0,
                                               bcast(vec[:, V_NORM_A:V_NORM_A + 8].unsqueeze(2), P, 8, NC), ALU.add, ALU.mult).then_inc(s_scl, 1)
                dve.wait_ge(s_scl, 1)
                norm.dve_samples(dve, tmp)
                modulations(2)


def gla(nc, A, OUT, K):
    MODS, MS = 10, 2
    with ExitStack() as c:
        sem = lambda n: K["sem"]("gl_" + n)
        tile = lambda n, s: c.enter_context(nc.sbuf_tensor("gl_" + n, s, F32))
        psP = c.enter_context(nc.psum_tensor("gl_psP", [P, 2, 512], F32))
        psL = c.enter_context(nc.psum_tensor("gl_psL", [P, 4, 512], F32))
        psO = c.enter_context(nc.psum_tensor("gl_psO", [P, 512], F32))
        psK = c.enter_context(nc.psum_tensor("gl_psK", [P, 512], F32))
        w = {n: tile("w_" + n, [P, KC, s]) for n, s in (("v", DV), ("z", DV))}
        w["q"], w["k"], wlow = K["w0"], K["w1"], K["wlow"]
        wg2 = tile("wg2", [RANK, DK])
        low = tile("low", [RANK, T])
        masks = tile("masks", [P, NL + 1, P])
        smasks = tile("smasks", [TS, 3, TS])
        restart = tile("restart", [P, T])
        rowsel = tile("rowsel", [TS, SB])
        qT, kT, gk, ec = (tile(n, [P, T]) for n in ("qT", "kT", "gk", "ec"))
        cum = K["B2"][:, NL, :]
        zs = tile("zs", [P, 2, T])
        v = tile("v", [P, NT + 1, DV])
        khT = tile("khT", [P, NT + 1, P])
        khm = tile("khm", [TS, SB, P])
        tmp = tile("tmp", [P, NL + 1, P])
        th = tmp[:].rearrange("p l t -> p (l t)")[:, 0:2 * THIRD].rearrange("p (a t) -> p a t", a=2)
        Am = tile("Am", [P, 2, P])
        As = tile("As", [TS, TS])
        state = tile("state", [P, 2, DV])
        wm = tile("wm", [P, MS, KC, P])
        sst = tile("sst", [P, SB, DV])
        dec = tile("dec", [P, NT + SB])
        one = tile("one", [P, 1])
        mod = K["mod"]
        X = K["B2"]
        h, G, ident, ones, vec = K["B1"], K["G"], K["ident"], K["ones"], K["vec"]

        passed = {n: K["sem"]("passed_" + n) for n in ("act", "pool", "sp")}
        s_const, s_g2in, s_low_in, s_set = sem("const_in"), sem("w_g2_in"), sem("low_in"), sem("one_set")
        s_w = {n: sem(f"w_{n}_in") for n in w}
        s_sin, s_sout, s_pout = sem("sstate_in"), sem("sstate_out"), sem("pstate_out")
        s_lowps, s_low = sem("low_summed"), sem("low_ready")
        s_proj, s_pfree = sem("proj_summed"), sem("proj_bank_free")
        s_v = sem("v_ready")
        s_zs = sem("z_ready")
        s_gm, s_ge, s_gl, s_lg, s_cum = sem("g_min"), sem("g_exp"), sem("g_log"), sem("logg"), sem("cum_ready")
        s_d, s_e, s_x = sem("level_diff"), sem("level_exp"), sem("level_ready")
        s_ece, s_dec, s_qh = sem("exp_cum"), sem("decay_kept"), sem("qhat_ready")
        s_kd, s_ke, s_kh = sem("khat_diff"), sem("khat_exp"), sem("khat_ready")
        s_kps, s_kT, s_khm = sem("khat_turned"), sem("khT_ready"), sem("khat_masked")
        s_lv, s_lm, s_A = sem("levels_summed"), sem("levels_masked"), sem("scores_ready")
        s_o, s_oev, s_up, s_st = sem("out_summed"), sem("out_copied"), sem("update_summed"), sem("state_ready")
        s_ups, s_sst = sem("supdate_summed"), sem("sstate_ready")
        s_osq, s_oss, s_oln, s_ors, s_g1, s_g2 = (sem("o_squares"), sem("o_sums"), sem("o_log"), sem("o_rstd"),
                                                   sem("o_normed"), sem("o_gated"))
        s_wm = [sem(f"w_mod_in{b}") for b in range(MS)]
        wkv, wb = A["ada_w_kv"].rearrange("(k p) n -> p k n", p=P), A["ada_w_b"].rearrange("(k p) n -> p k n", p=P)

        def mod_tile(i, n):
            return i * 4 + (M_KV + n) if n < 4 else i * 6 + (M_B + n - 4)

        win = A["w_in_a"].rearrange("(k p) n -> p k n", p=P)
        CH = NT + 1
        V_UNITS = {(0, 2): 15, (2, 4): 16, (4, 5): 17, (5, 6): 19, (6, 7): 21, (7, 8): 23, (8, 9): 25}
        M_UNITS = [18, 20, 22, 24, 26, 27, 28, 29, 30, 31]
        UNITS = 32
        lvl = lambda ap, L: ap.rearrange("p (n a l) -> p n a l", a=2, l=L)

        def over_heads(eng, head):
            with eng.Fori(0, HA - 1) as i:
                head(i, False)
            head(HA - 1, True)

        with nc.Block() as block:
            @block.sync
            def _(sp):
                for dst, name in ((masks, "masks"), (smasks, "smasks"), (restart, "restart"), (rowsel, "rowsel")):
                    sp.dma_start(dst[:], A[name]).then_inc(s_const, 16)
                with sp.Fori(0, HA) as i:
                    sp.dma_start(sst[:], A["state_gla"][:, bass.ds(i, 1), :, :].rearrange("b h k v -> k (b h) v")).then_inc(s_sin, 16)
                    sp.wait_ge(s_st, 8 * i + 8)
                    sp.dma_start(OUT["state_p"][bass.ds(i, 1), :, :].rearrange("h k v -> k (h v)"), state[:, (NT - 1) % 2, :]).then_inc(s_pout, 16)
                    sp.wait_ge(s_sst, 8 * i + 8)
                    sp.dma_start(OUT["state_s"][:, bass.ds(i, 1), :, :].rearrange("b h k v -> k (b h) v"), sst[:]).then_inc(s_sout, 16)
                    sp.wait_ge(s_sout, 16 * (i + 1))
                    apart(sp, passed["sp"])
                for b in range(2):
                    sp.wait_ge(s_proj, HA * UNITS + 6)
                    sp.dma_start(K[f"w{b}"][:], A["w_out_a"].rearrange("(k p) n -> p k n", p=P)[:, :, b * P:(b + 1) * P]).then_inc(
                        K["sem"](f"op_w_in{b}"), 16)
                sp.wait_ge(s_pout, 16 * HA)

            @block.gpsimd
            def _(pool):
                nc.gpsimd.memset(one[:], 1.0).then_inc(s_set, 1)

                def load(name, i, first, n, used):
                    pool.wait_ge(s_proj, i * UNITS + used)
                    apart(pool, passed["pool"])
                    pool.dma_start(w[name][:], win[:, :, bass.ds(i * n + first, n)]).then_inc(s_w[name], 16)

                def load_g2(i):
                    pool.wait_ge(s_proj, i * UNITS + 9)
                    apart(pool, passed["pool"])
                    pool.dma_start(wg2[:], A["w_g2_a"][:, bass.ds(i * DK, DK)]).then_inc(s_g2in, 16)

                def head(i, last):
                    load("z", i, 2048, DV, 15)
                    load("v", i, 1024, DV, V_UNITS[(8, 9)] + 1)
                    for n in range(MODS):
                        pool.wait_ge(s_proj, i * UNITS + (UNITS + M_UNITS[n - MS] if n >= MS else M_UNITS[n - MS]) + 1)
                        apart(pool, passed["pool"])
                        src = wkv[:, :, bass.ds(i * 4 * P + n * P, P)] if n < 4 else wb[:, :, bass.ds(i * 6 * P + (n - 4) * P, P)]
                        pool.dma_start(wm[:, n % MS], src).then_inc(s_wm[n % MS], 16)
                        if n == 3 and not last:
                            load("q", i + 1, 0, P, 3)
                            load("k", i + 1, 512, P, 6)
                            load_g2(i + 1)

                load_g2(0)
                over_heads(pool, head)

            @block.tensor
            def _(pe):
                pe.wait_ge(s_low_in, 16)
                for j, part in enumerate(thirds(low[:])):
                    for k in range(KC):
                        mm = nc.tensor.matmul(psL[0:RANK, j, 0:THIRD], wlow[:, k, :], thirds(h[:, k, :])[j], start=(k == 0), stop=(k == KC - 1))
                mm.then_inc(s_lowps, 1)
                pe.wait_ge(s_low, 1)
                pe.sem_inc(s_proj, UNITS)

                def bank(i, unit):
                    pe.wait_ge(s_pfree, i * UNITS + unit + 1)
                    return unit % 2

                def project(name, i, unit, m=0):
                    b = bank(i, unit)
                    for k in range(KC):
                        mm = nc.tensor.matmul(psP[:, b, 0:THIRD], w[name][:, k, m * P:(m + 1) * P], thirds(h[:, k, :])[unit % 3],
                                              start=(k == 0), stop=(k == KC - 1))
                    mm.then_inc(s_proj, 1)

                def head(i, last):
                    def project_v(lo, hi):
                        b = bank(i, V_UNITS[(lo, hi)])
                        for t in range(lo, hi):
                            n = P if t < NT else TS
                            for k in range(KC):
                                mm = nc.tensor.matmul(psP[0:n, b, (t - lo) * DV:(t - lo + 1) * DV], h[:, k, t * P:t * P + n], w["v"][:, k, :],
                                                      start=(k == 0), stop=(k == KC - 1))
                        mm.then_inc(s_proj, 1)

                    def turn_keys(r):
                        pe.wait_ge(s_kh, i + 1)
                        if r:
                            pe.wait_ge(s_kT, 3 * i + r)
                        for t in range(4 * r, min(4 * r + 4, CH)):
                            n = P if t < NT else TS
                            mm = nc.tensor.transpose(psK[0:n, (t % 4) * P:(t % 4) * P + P], gk[:, t * P:t * P + n], ident[:])
                        mm.then_inc(s_kps, 1)

                    def levels(t):
                        if t >= 2:
                            pe.wait_ge(s_lm, CH * i + t - 1)
                        elif t == 0:
                            pe.wait_ge(s_ors, i + 1)
                        lo, n = t * P, (P if t < NT else TS)
                        todo = [(X[:, L, lo:lo + n],) * 2 for L in (range(NL) if t < NT else SLEV)] + [(kT[:, lo:lo + n], qT[:, lo:lo + n])]
                        for r, (a, b) in enumerate(todo):
                            f = r * n
                            mm = nc.tensor.matmul(psL[0:n, 2 * (t % 2) + f // 512, f % 512:f % 512 + n], a, b, start=True, stop=True)
                        mm.then_inc(s_lv, 1)

                    def output(t):
                        pe.wait_ge(s_A, CH * i + t + 1)
                        if t:
                            pe.wait_ge(s_oev, CH * i + t)
                            if t < NT:
                                pe.wait_ge(s_st, 8 * i + t)
                        for half in range(2):
                            cols = slice(half * DK, (half + 1) * DK)
                            mm = nc.tensor.matmul(psO[:, half * P:(half + 1) * P], v[:, t, cols], Am[:, t % 2, :], start=True, stop=(t == 0))
                            if t:
                                mm = nc.tensor.matmul(psO[:, half * P:(half + 1) * P], state[:, (t - 1) % 2, cols], ec[:, t * P:(t + 1) * P], start=False, stop=True)
                        mm.then_inc(s_o, 1)

                    def update(t):
                        if t == 0:
                            pe.wait_ge(s_kT, 3 * i + 3)
                        else:
                            pe.wait_ge(s_st, 8 * i + t)
                        nc.tensor.matmul(psK[:, 0:DV], khT[:, t, :], v[:, t, :], start=True, stop=True).then_inc(s_up, 1)

                    def modulate(n):
                        pe.wait_ge(s_wm[n % MS], 16 * (MODS // MS * i + n // MS + 1))
                        b = bank(i, M_UNITS[n])
                        for k in range(KC):
                            mm = nc.tensor.matmul(psP[:, b, 0:NC], wm[:, n % MS, k, :], K["cT"][:, k, :], start=(k == 0), stop=(k == KC - 1))
                        mm.then_inc(s_proj, 1)

                    pe.wait_ge(s_w["k"], 16 * (i + 1))
                    for j in range(3):
                        project("k", i, 3 + j)
                    pe.wait_ge(s_g2in, 16 * (i + 1))
                    for j in range(3):
                        b = bank(i, 6 + j)
                        nc.tensor.matmul(psP[:, b, 0:THIRD], wg2[:], thirds(low[:])[j], start=True, stop=True).then_inc(s_proj, 1)
                    pe.wait_ge(s_w["z"], 16 * (i + 1))
                    for u in range(6):
                        project("z", i, 9 + u, u // 3)
                    pe.wait_ge(s_w["v"], 16 * (i + 1))
                    project_v(0, 2)
                    project_v(2, 4)
                    pe.wait_ge(s_x, i + 1)
                    levels(0)
                    turn_keys(0)
                    project_v(4, 5)
                    turn_keys(1)
                    levels(1)
                    turn_keys(2)
                    pe.wait_ge(s_v, 7 * i + 1)
                    update(0)
                    for t in range(NT):
                        if t:
                            levels(t + 1)
                            if t < 5:
                                project_v(t + 4, t + 5)
                        output(t)
                        modulate(t)
                        if t + 1 < NT:
                            pe.wait_ge(s_v, 7 * i + (1, 1, 2, 2, 3, 4, 5, 6)[t + 1])
                            update(t + 1)
                    pe.wait_ge(s_A, CH * i + CH)
                    pe.wait_ge(s_oev, CH * i + NT)
                    pe.wait_ge(s_v, 7 * i + 7)
                    pe.wait_ge(s_sin, 16 * (i + 1))
                    for half in range(2):
                        cols = slice(half * DK, (half + 1) * DK)
                        for b in range(SB):
                            at = half * TS + b * SL
                            nc.tensor.matmul(psO[:, at:at + SL], sst[:, b, cols], ec[:, TP + b * SL:TP + (b + 1) * SL], start=(b == 0), stop=False)
                        mm = nc.tensor.matmul(psO[:, half * TS:(half + 1) * TS], v[0:TS, NT, cols], As[:], start=False, stop=True)
                    mm.then_inc(s_o, 1)
                    modulate(NT)
                    pe.wait_ge(s_khm, i + 1)
                    pe.wait_ge(s_lm, CH * i + CH)
                    for b in range(SB):
                        mm = nc.tensor.matmul(psL[:, b // 2, (b % 2) * DV:(b % 2 + 1) * DV], khm[:, b, :], v[0:TS, NT, :], start=True, stop=True)
                    mm.then_inc(s_ups, 1)
                    modulate(NT + 1)
                    if not last:
                        pe.wait_ge(s_w["q"], 16 * (i + 2))
                        project("q", i + 1, 0)
                    pe.wait_ge(s_osq, i + 1)
                    pe.wait_ge(s_sst, 8 * (i + 1))
                    for j in range(3):
                        for half in range(2):
                            mm = nc.tensor.matmul(psL[:, j, 0:THIRD], ones[:], thirds(X[:, half, :])[j], start=(half == 0), stop=(half == 1))
                    mm.then_inc(s_oss, 1)
                    pe.wait_ge(s_st, 8 * (i + 1))
                    if not last:
                        project("q", i + 1, 1)
                        project("q", i + 1, 2)

                pe.wait_ge(s_w["q"], 16)
                for unit in range(3):
                    project("q", 0, unit)
                over_heads(pe, head)

            @block.scalar
            def _(act):
                A_ = nc.scalar.activation
                act.wait_ge(s_lowps, 1)
                A_(low[:].rearrange("p (j t) -> p j t", j=3), psL[0:RANK, 0:3, 0:THIRD], ACT.Copy).then_inc(s_low, 1)
                act.wait_ge(s_set, 1)
                act.sem_inc(s_pfree, 2)
                act.sem_inc(s_ors, 1)

                def done(i, unit):
                    act.wait_ge(s_proj, (i + 1) * UNITS + unit + 1)
                    return unit % 2

                def copy_q(i, unit):
                    A_(thirds(qT[:])[unit], psP[:, done(i, unit), 0:THIRD], ACT.Copy, scale=DK ** -0.5).then_inc(s_pfree, 1)

                def head(i, last):
                    def copy_v(lo, hi):
                        b = done(i, V_UNITS[(lo, hi)])
                        n = P if lo < NT else TS
                        A_(v[0:n, lo:hi, :].rearrange("p a d -> p (a d)"), psP[0:n, b, 0:(hi - lo) * DV], ACT.Copy).then_inc(s_v, 1)
                        act.wait_ge(s_v, 7 * i + list(V_UNITS).index((lo, hi)) + 1)
                        act.sem_inc(s_pfree, 1)

                    def copy_keys(r):
                        act.wait_ge(s_kps, 3 * i + r + 1)
                        if r < 2:
                            A_(khT[:, 4 * r:4 * r + 4, :].rearrange("p a d -> p (a d)"), psK[:], ACT.Copy).then_inc(s_kT, 1)
                        else:
                            A_(khT[0:TS, NT, :], psK[0:TS, 0:P], ACT.Copy).then_inc(s_kT, 1)

                    for j in range(3):
                        A_(thirds(kT[:])[j], psP[:, done(i, 3 + j), 0:THIRD], ACT.Copy).then_inc(s_pfree, 1)
                    for j in range(3):
                        b = done(i, 6 + j)
                        apart(act, passed["act"])
                        A_(thirds(gk[:])[j], psP[:, b, 0:THIRD], ACT.Identity, bias=vec[:, bass.ds(i + V_BG, 1)])
                        A_(thirds(ec[:])[j], psP[:, b, 0:THIRD], ACT.Abs, bias=vec[:, bass.ds(i + V_BG, 1)]).then_inc(s_pfree, 1)
                    act.wait_ge(s_pfree, i * UNITS + 2 + 9)
                    A_(ec[:], ec[:], ACT.Exp, scale=-1.0).then_inc(s_ge, 1)
                    act.wait_ge(s_ge, i + 1)
                    A_(ec[:], ec[:], ACT.Ln, bias=one[:, 0:1]).then_inc(s_gl, 1)
                    act.wait_ge(s_g2, 2 * i + 2)
                    for m in range(2):
                        for j in range(3):
                            u = 3 * m + j
                            b = done(i, 9 + u)
                            if u >= 2:
                                act.wait_ge(s_zs, 6 * i + u - 1)
                            A_(thirds(zs[:, m, :])[j], psP[:, b, 0:THIRD], ACT.Copy, scale=0.5)
                            A_(th[:, u % 2, :], psP[:, b, 0:THIRD], ACT.Tanh, scale=0.5).then_inc(s_pfree, 1)
                    act.wait_ge(s_cum, i + 1)
                    A_(ec[:], cum, ACT.Exp).then_inc(s_ece, 1)
                    for L in range(NL):
                        act.wait_ge(s_d, NL * i + L + 1)
                        n = T if L in SLEV else TP
                        A_(X[:, L, 0:n], X[:, L, 0:n], ACT.Exp).then_inc(s_e, 1)
                    act.wait_ge(s_kd, i + 1)
                    A_(gk[:], gk[:], ACT.Exp).then_inc(s_ke, 1)
                    copy_v(0, 2)
                    copy_v(2, 4)
                    copy_keys(0)
                    copy_v(4, 5)
                    copy_keys(1)
                    copy_keys(2)
                    for t in range(CH):
                        if 1 <= t < 5:
                            copy_v(t + 4, t + 5)
                        act.wait_ge(s_o, CH * i + t + 1)
                        n = P if t < NT else TS
                        apart(act, passed["act"])
                        A_(G[:, bass.ds(2 * i, 2), t * P:t * P + n], psO[:, 0:2 * n].rearrange("p (a t) -> p a t", a=2), ACT.Copy).then_inc(s_oev, 1)
                        for n in [t] if t < NT else [NT, NT + 1]:
                            b = done(i, M_UNITS[n])
                            apart(act, passed["act"])
                            A_(mod[:, bass.ds(mod_tile(i, n), 1), :].rearrange("p a c -> p (a c)"), psP[:, b, 0:NC], ACT.Identity,
                               bias=vec[:, bass.ds(mod_tile(i, n), 1)]).then_inc(s_pfree, 1)
                    act.wait_ge(s_oev, CH * (i + 1))
                    act.wait_ge(s_lv, CH * (i + 1))
                    apart(act, passed["act"])
                    A_(X[:, 0:2, :], G[:, bass.ds(2 * i, 2), :], ACT.Square).then_inc(s_osq, 1)
                    if not last:
                        copy_q(i + 1, 0)
                    act.wait_ge(s_oss, i + 1)
                    ecv = X[:, 2, :]
                    A_(ecv.rearrange("p (j t) -> p j t", j=3), psL[:, 0:3, 0:THIRD], ACT.Ln, scale=1.0 / DV, bias=K["eps"][:, 0:1]).then_inc(s_oln, 1)
                    act.wait_ge(s_oln, i + 1)
                    A_(ecv, ecv, ACT.Exp, scale=-0.5).then_inc(s_ors, 1)
                    if not last:
                        copy_q(i + 1, 1)
                        copy_q(i + 1, 2)

                for unit in range(3):
                    copy_q(0, unit)
                over_heads(act, head)

            @block.vector
            def _(dve):
                V = nc.vector
                dve.wait_ge(s_const, 16 * 4)
                dve.sem_inc(s_g2, 2)
                with dve.Fori(0, HA) as i:
                    dve.wait_ge(s_pfree, i * UNITS + 2 + 9)
                    V.tensor_scalar(gk[:], gk[:], 0.0, None, ALU.min).then_inc(s_gm, 1)
                    dve.wait_ge(s_gm, i + 1)
                    dve.wait_ge(s_gl, i + 1)
                    V.tensor_tensor(gk[:], gk[:], ec[:], ALU.subtract).then_inc(s_lg, 1)
                    dve.wait_ge(s_lg, 2 * i + 1)
                    V.tensor_scalar(gk[:], gk[:], 1.0 / 16.0, None, ALU.mult).then_inc(s_lg, 1)
                    dve.wait_ge(s_lg, 2 * i + 2)
                    V.tensor_tensor_scan(cum, restart[:], gk[:], 0.0, ALU.mult, ALU.add).then_inc(s_cum, 1)
                    dve.wait_ge(s_cum, i + 1)

                    def zgate(u):
                        dve.wait_ge(s_pfree, i * UNITS + 2 + 9 + u + 1)
                        dst = thirds(zs[:, u // 3, :])[u % 3]
                        V.scalar_tensor_tensor(dst, th[:, u % 2, :], 1.0, dst, ALU.add, ALU.mult).then_inc(s_zs, 1)

                    for L, size in enumerate(LEVELS):
                        parts = [(0, TP)] + ([(TP, T)] if L in SLEV else [])
                        for a, b in parts:
                            src, dst = lvl(cum[:, a:b], size), lvl(X[:, L, a:b], size)
                            m = src.shape[1]
                            ref = bcast(src[:, :, 0, size - 1:size], P, m, size)
                            V.tensor_tensor(dst[:, :, 0, :], ref, src[:, :, 0, :], ALU.subtract)
                            last = V.tensor_tensor(dst[:, :, 1, :], src[:, :, 1, :], ref, ALU.subtract)
                        last.then_inc(s_d, 1)
                        if L < 6:
                            zgate(L)
                    for a, b, size in ((0, TP, P), (TP, T, SL)):
                        src = cum[:, a:b].rearrange("p (n t) -> p n t", t=size)
                        last = V.tensor_tensor(gk[:, a:b].rearrange("p (n t) -> p n t", t=size), bcast(src[:, :, size - 1:size], P, (b - a) // size, size),
                                               src, ALU.subtract)
                    last.then_inc(s_kd, 1)
                    dve.wait_ge(s_ece, i + 1)
                    V.tensor_copy(dec[:, 0:NT], ec[:, P - 1:TP:P])
                    V.tensor_copy(dec[:, NT:NT + SB], ec[:, TP + SL - 1:T:SL]).then_inc(s_dec, 1)
                    dve.wait_ge(s_dec, i + 1)
                    V.tensor_tensor(ec[:], ec[:], qT[:], ALU.mult).then_inc(s_qh, 1)
                    for L, size in enumerate(LEVELS):
                        dve.wait_ge(s_e, NL * i + L + 1)
                        for a, b in [(0, TP)] + ([(TP, T)] if L in SLEV else []):
                            dst = lvl(X[:, L, a:b], size)
                            V.tensor_tensor(dst[:, :, 0, :], dst[:, :, 0, :], lvl(kT[:, a:b], size)[:, :, 0, :], ALU.mult)
                            last = V.tensor_tensor(dst[:, :, 1, :], dst[:, :, 1, :], lvl(qT[:, a:b], size)[:, :, 1, :], ALU.mult)
                    last.then_inc(s_x, 1)
                    dve.wait_ge(s_ke, i + 1)
                    V.tensor_tensor(gk[:], gk[:], kT[:], ALU.mult).then_inc(s_kh, 1)
                    for t in range(NT):
                        dve.wait_ge(s_lv, CH * i + t + 1)
                        if t:
                            dve.wait_ge(s_A, CH * i + t)
                        V.tensor_tensor(tmp[:].rearrange("p l t -> p (l t)"), psL[:, 2 * (t % 2):2 * (t % 2) + 2, :].rearrange("p a t -> p (a t)"),
                                        masks[:].rearrange("p l t -> p (l t)"), ALU.mult).then_inc(s_lm, 1)
                        dve.wait_ge(s_lm, CH * i + t + 1)
                        if t >= 2:
                            dve.wait_ge(s_o, CH * i + t - 1)
                        V.tensor_reduce(Am[:, t % 2, :], tmp[:].rearrange("p l t -> p t l"), AX.X, ALU.add).then_inc(s_A, 1)
                        dve.wait_ge(s_up, NT * i + t + 1)
                        if t == 0:
                            V.tensor_copy(state[:, 0, :], psK[:, 0:DV]).then_inc(s_st, 1)
                        else:
                            dve.wait_ge(s_o, CH * i + t)
                            dve.wait_ge(s_st, 8 * i + t)
                            V.scalar_tensor_tensor(state[:, t % 2, :], state[:, (t - 1) % 2, :], dec[:, t:t + 1], psK[:, 0:DV], ALU.mult, ALU.add).then_inc(s_st, 1)
                    dve.wait_ge(s_lv, CH * i + CH)
                    dve.wait_ge(s_A, CH * i + NT)
                    V.tensor_tensor(tmp[0:TS, 0:3, 0:TS], psL[0:TS, 0, 0:3 * TS].rearrange("p (l t) -> p l t", l=3), smasks[:], ALU.mult).then_inc(s_lm, 1)
                    dve.wait_ge(s_lm, CH * i + CH)
                    V.tensor_reduce(As[:], tmp[0:TS, 0:3, 0:TS].rearrange("p l t -> p t l"), AX.X, ALU.add).then_inc(s_A, 1)
                    dve.wait_ge(s_kT, 3 * i + 3)
                    V.tensor_tensor(khm[:], bcast(khT[0:TS, NT, :].unsqueeze(1), TS, SB, P), bcast(rowsel[:].unsqueeze(2), TS, SB, P), ALU.mult).then_inc(s_khm, 1)
                    dve.wait_ge(s_ups, i + 1)
                    for b in range(SB):
                        V.scalar_tensor_tensor(sst[:, b, :], sst[:, b, :], dec[:, NT + b:NT + b + 1], psL[:, b // 2, (b % 2) * DV:(b % 2 + 1) * DV],
                                               ALU.mult, ALU.add).then_inc(s_sst, 1)
                    dve.wait_ge(s_ors, i + 2)
                    for half in range(2):
                        o = G[:, bass.ds(2 * i + half, 1), :].rearrange("p a t -> p (a t)")
                        V.scalar_tensor_tensor(o, o, vec[:, V_ONORM + half:V_ONORM + half + 1], X[:, 2, :], ALU.mult, ALU.mult).then_inc(s_g1, 1)
                        dve.wait_ge(s_g1, 2 * i + half + 1)
                        dve.wait_ge(s_zs, 6 * i + 6)
                        V.tensor_tensor(o, o, zs[:, half, :], ALU.mult).then_inc(s_g2, 1)
                    dve.wait_ge(s_pout, 16 * (i + 1))
                    dve.wait_ge(s_g2, 2 * (i + 1) + 2)


def out_proj(nc, W, resid, keep, dst, gate, K, use, norm=None):
    with ExitStack() as c:
        sem = lambda n: K["sem"]("op_" + n)
        ps = c.enter_context(nc.psum_tensor(f"op{use}_ps", [P, 2, 512], F32))
        w = [K["w0"], K["w1"]]
        part = lambda n, s: c.enter_context(nc.sbuf_tensor(f"op{use}_{n}", s, F32R))
        wh, wl = part("w_high", [P, 2, KC, P]), part("w_low", [P, 2, KC, P])
        Gh, Gl = part("G_high", [P, KC, T]), part("G_low", [P, KC, T])
        x = K[("B1", "B2")[use]][:, 0:2, :]
        sg = c.enter_context(nc.sbuf_tensor(f"op{use}_sg", [P, 2, TS], F32))
        s_w = [sem(f"w_in{b}") for b in range(2)]
        s_x = [sem(f"x_in{b}") for b in range(2)]
        s_mm, s_free, s_sg, s_out, s_kept = sem("summed"), sem("added"), sem("sample_gated"), sem("tile_ready"), sem("kept")
        s_hi, s_lo = sem("high_ready"), sem("low_ready")
        G, mod = K["G"], K["mod"]
        base = use * (3 * KC + KC)
        third_split = lambda j: base + (1 + KC, 2 + 2 * KC, 2 + 3 * KC)[j]
        tile_split = lambda m: m + (base + 2 + 3 * KC - 1)

        def splits(weights, third):
            weights(0)
            for j in range(3):
                for k in range(KC):
                    third(j, k)
                if j == 0:
                    weights(1)
        wd = W.rearrange("(k p) n -> p k n", p=P)

        with nc.Block() as block:
            @block.sync
            def _(sp):
                if use == 0:
                    sp.sem_inc(s_out, 2)
                for b in range(2):
                    sp.wait_ge(s_out, use * KC + b + 1)
                    sp.dma_start(x[:, b], resid[b * P:(b + 1) * P, :]).then_inc(s_x[b], 16)

                def load(i, split):
                    for b in range(2):
                        sp.wait_ge(s_lo, split(b))
                        sp.dma_start(w[b][:], wd[:, :, bass.ds(i * 2 * P + b * P, P)]).then_inc(s_w[b], 16)
                        sp.wait_ge(s_out, i * 2 + (use * KC + b + 1))
                        sp.dma_start(x[:, b], resid[bass.ds(i * 2 * P + b * P, P), :]).then_inc(s_x[b], 16)

                load(1, lambda b: base + (1, 2 + KC)[b])
                with sp.Fori(2, KC // 2) as i:
                    load(i, lambda b: tile_split(i * 2 + (b - 2)))
                if keep is not None:
                    with sp.Fori(0, KC) as m:
                        sp.wait_ge(s_out, m + 3)
                        sp.dma_start(keep[bass.ds(m * P, P), :], dst[:, bass.ds(m, 1), :].rearrange("p a t -> p (a t)")).then_inc(s_kept, 16)
                    sp.wait_ge(s_kept, 16 * KC)

            @block.tensor
            def _(pe):
                def tiles(i, first):
                    s = i + use * KC // 2
                    for b in range(2):
                        if first:
                            pe.wait_ge(s_lo, base + (1, 2 + KC)[b])
                        else:
                            pe.wait_ge(s_lo, tile_split(i * 2 + b))
                        for j in range(3):
                            u = 3 * b + j
                            if first and b == 0:
                                pe.wait_ge(s_lo, third_split(j))
                            pe.wait_ge(s_free, s * 6 + u + 1)
                            for k in range(KC):
                                for n, (ws, gs) in enumerate(((wh, Gh), (wh, Gl), (wl, Gh))):
                                    mm = nc.tensor.matmul(ps[:, u % 2, 0:THIRD], ws[:, b, k, :], thirds(gs[:, k, :])[j],
                                                          start=(k == 0 and n == 0), stop=(k == KC - 1 and n == 2))
                            mm.then_inc(s_mm, 1)

                tiles(0, True)
                with pe.Fori(1, KC // 2) as i:
                    tiles(i, False)
                if norm is not None:
                    norm.pe_sum(pe)

            @block.scalar
            def _(act):
                def weights(m):
                    act.wait_ge(s_w[m % 2], 16 * ((use * KC + m) // 2 + 1))
                    if m >= 2:
                        act.wait_ge(s_mm, 3 * (use * KC + m - 1))
                    nc.scalar.activation(wh[:, m % 2], w[m % 2][:], ACT.Copy).then_inc(s_hi, 1)

                splits(weights, lambda j, k: nc.scalar.activation(thirds(Gh[:, k, :])[j], thirds(G[:, k, :])[j], ACT.Copy).then_inc(s_hi, 1))
                for m in range(KC):
                    if m + 2 < KC:
                        weights(m + 2)
                    if norm is not None:
                        act.wait_ge(s_out, use * KC + 2 + m + 1)
                        norm.act_square(act, m)
                if norm is not None:
                    norm.act_rstd(act)

            @block.vector
            def _(dve):
                V = nc.vector
                if use == 0:
                    dve.sem_inc(s_free, 2)

                done = [base]

                def low(dst, src, high):
                    done[0] += 1
                    dve.wait_ge(s_hi, done[0])
                    V.tensor_tensor(dst, src, high, ALU.subtract).then_inc(s_lo, 1)

                splits(lambda m: low(wl[:, m], w[m][:], wh[:, m]),
                       lambda j, k: low(thirds(Gl[:, k, :])[j], thirds(G[:, k, :])[j], thirds(Gh[:, k, :])[j]))

                def tiles(i, first, last):
                    s = i + use * KC // 2
                    for b in range(2):
                        if norm is not None and not first:
                            norm.dve_add(dve, i * 2 + b - 1, 1 - b)
                        dve.wait_ge(s_x[b], 16 * (s + 1))
                        gp = mod[:, bass.ds(i * 2 + b + gate, 1), 0:1].rearrange("p a c -> p (a c)")
                        gs = mod[:, bass.ds(i * 2 + b + gate, 1), 1:NC].rearrange("p a c -> p (a c)")
                        d = dst[:, bass.ds(i * 2 + b, 1), :].rearrange("p a t -> p (a t)")
                        for j in range(3):
                            u = 3 * b + j
                            dve.wait_ge(s_mm, s * 6 + u + 1)
                            n = THIRD if j < 2 else THIRD - TS
                            lo = THIRD * j
                            if j == 2:
                                V.tensor_tensor(sg[:, b, :].rearrange("p (s t) -> p s t", s=SB),
                                                ps[:, u % 2, n:THIRD].rearrange("p (s t) -> p s t", s=SB),
                                                bcast(gs.unsqueeze(2), P, SB, SL), ALU.mult).then_inc(s_sg, 1)
                            V.scalar_tensor_tensor(d[:, lo:lo + n], ps[:, u % 2, 0:n], gp, x[:, b, lo:lo + n], ALU.mult, ALU.add).then_inc(s_free, 1)
                        dve.wait_ge(s_sg, s * 2 + b + 1)
                        V.tensor_tensor(d[:, TP:T], sg[:, b, :], x[:, b, TP:T], ALU.add).then_inc(s_out, 1)
                        if not last:
                            dve.wait_ge(s_hi, tile_split(i * 2 + (b + 2)))
                            V.tensor_tensor(wl[:, b], w[b][:], wh[:, b], ALU.subtract).then_inc(s_lo, 1)

                tiles(0, True, False)
                with dve.Fori(1, KC // 2 - 1) as i:
                    tiles(i, False, False)
                tiles(KC // 2 - 1, False, True)
                if norm is not None:
                    norm.dve_add(dve, KC - 1, 1)


def normed(nc, A, K, norm, tmp):
    s_scl = K["sem"]("no_scales_ready")
    with nc.Block() as block:
        @block.gpsimd
        def _(pool):
            for n, (src, name) in enumerate(((A["w_in_b"], "at_w_q_in"), (A["w_k"], "at_w_k_in"))):
                pool.dma_start(K[f"w{n}"][:], src.rearrange("(k p) n -> p k n", p=P)[:, :, 0:P]).then_inc(K["sem"](name), 16)

        @block.scalar
        def _(act):
            act.wait_ge(s_scl, 1)
            norm.act_affine(act)

        @block.vector
        def _(dve):
            for col, gain in ((M_KV + 8, V_NORM_KV), (M_B + 8, V_NORM_B)):
                ins = nc.vector.scalar_tensor_tensor(K["mod"][:, col:col + 8, :], K["mod"][:, col:col + 8, :], 1.0,
                                                     bcast(K["vec"][:, gain:gain + 8].unsqueeze(2), P, 8, NC), ALU.add, ALU.mult)
            ins.then_inc(s_scl, 1)
            dve.wait_ge(s_scl, 1)
            norm.dve_rstd(dve)
            norm.dve_samples(dve, tmp)


def attention(nc, A, OUT, K):
    with ExitStack() as c:
        sem = lambda n: K["sem"]("at_" + n)
        tile = lambda n, s, dt=F32: c.enter_context(nc.sbuf_tensor("at_" + n, s, dt))
        psP = c.enter_context(nc.psum_tensor("at_psP", [P, 2, 512], F32))
        psS = c.enter_context(nc.psum_tensor("at_psS", [P, 4, 512], F32))
        psW = c.enter_context(nc.psum_tensor("at_psW", [P, 512], F32))
        psO = c.enter_context(nc.psum_tensor("at_psO", [P, 512], F32))
        w = {"q": K["w0"], "k": K["w1"], "z": tile("w_z", [P, KC, P])}
        w["v"] = w["q"]
        qT, kT, zs, rs = (tile(n, [P, T]) for n in ("qT", "kT", "zs", "rs"))
        v = tile("v", [P, NT + 1, DE])
        ko = tile("ko", [P, NT + 1, P])
        bias = tile("bias", [P, TP])
        sbias = tile("sbias", [SR, PAST + TS])
        bones = tile("bones", [P, P])
        comb, combr = tile("comb", [SR, TS]), tile("combr", [SR, TS])
        lamrow = tile("lamrow", [SR, 1])
        rowsel = tile("rowsel", [SR, 2])
        eps64, subg = tile("eps64", [P, 1]), tile("subg", [P, 1])
        S = tile("S", [P, 2, 2, TP])
        wT = tile("wT", [P, 2, TP])
        th = wT[:, 0, 0:2 * THIRD].rearrange("p (a t) -> p a t", a=2)
        sq = S[:, 1, :, :].rearrange("p c k -> p (c k)")[:, 0:T]
        kcT = ko[:].rearrange("p t k -> p (t k)")[:, 0:2 * PAST].rearrange("p (a k) -> p a k", a=2)
        SS = S[0:SR, 0, 1, 0:PAST + TS]
        nmx, rsum, rr = tile("nmx", [P, 2, 2]), tile("rsum", [P, 2, 2]), tile("rr", [P, 2, 2])
        QZ, QN = tile("QZ", [P, SB * (SR + SL)]), tile("QN", [P, SR])
        kc, vc = tile("kc", [P, SB * NPG, P]), tile("vc", [P, SB * NPG, DE])
        snm, ssum, srr = tile("snm", [SR, 2]), tile("ssum", [SR, 1]), tile("srr", [SR, 2])
        wsT = tile("wsT", [P, NPG + 1, TS])
        pt = tile("pt", [1, SB * NPG], I32)
        hk, hb, G, ident, ones, vec = K["B1"], K["B2"], K["G"], K["ident"], K["ones"], K["vec"]

        passed = {n: K["sem"]("passed_" + n) for n in ("sp", "pool", "act", "dve")}
        s_const, s_pt, s_set, s_init = sem("const_in"), sem("pages_in"), sem("set"), sem("init")
        s_w = {n: sem(f"w_{n}_in") for n in "qkzv"}
        s_kc, s_vc = sem("kcache_in"), sem("vcache_in")
        s_proj, s_pfree = sem("proj_summed"), sem("proj_bank_free")
        s_qk, s_sq, s_v = sem("qk_copied"), sem("qk_squares"), sem("v_ready")
        s_rs, s_qn, s_zs = sem("qk_rstd"), sem("qk_ready"), sem("z_ready")
        s_kops, s_ko, s_kst = sem("k_turned"), sem("k_out_ready"), sem("kv_stored")
        s_bias = sem("bias_ready")
        s_sc, s_min, s_exp, s_rec, s_r1, s_p1, s_wc = (sem("scores_summed"), sem("min_ready"), sem("exp_ready"), sem("recip"),
                                                       sem("recip_lam"), sem("p1_scaled"), sem("weights_ready"))
        s_wps, s_wT, s_pv, s_oev = sem("weights_turned"), sem("wT_ready"), sem("out_summed"), sem("out_copied")
        s_qz, s_kcps, s_kcT, s_ssc, s_smin, s_sexp = (sem("qz_ready"), sem("kcache_turned"), sem("kcT_ready"), sem("sscores_summed"),
                                                      sem("smin_ready"), sem("sexp_ready"))
        s_srec, s_comb, s_wsps, s_wsT, s_spv, s_soev = (sem("srecip"), sem("comb_ready"), sem("sweights_turned"), sem("wsT_ready"),
                                                        sem("sout_summed"), sem("sout_copied"))
        s_osq, s_oss, s_oln, s_ors, s_g1, s_g2 = (sem("o_squares"), sem("o_sums"), sem("o_log"), sem("o_rstd"),
                                                  sem("o_normed"), sem("o_gated"))
        UNITS = 12
        GROUPS = [(r, min(r + 4, NT + 1)) for r in range(0, NT + 1, 4)]
        WG = [(i + 4) // 4 for i in range(NT)]
        WB = [sum(WG[:i]) for i in range(NT + 1)]
        wd = {"q": A["w_in_b"].rearrange("(k p) n -> p k n", p=P)[:, :, 0:D], "z": A["w_in_b"].rearrange("(k p) n -> p k n", p=P)[:, :, D:2 * D],
              "k": A["w_k"].rearrange("(k p) n -> p k n", p=P), "v": A["w_v"].rearrange("(k p) n -> p k n", p=P)}

        def over_heads(eng, head):
            with eng.Fori(0, HB - 1) as i:
                head(i, False)
            head(HB - 1, True)

        with nc.Block() as block:
            @block.sync
            def _(sp):
                for dst, name in ((bias, "bias"), (sbias, "sbias"), (bones, "bones"), (comb, "comb"), (rowsel, "lamsel")):
                    sp.dma_start(dst[:], A[name]).then_inc(s_const, 16)
                sp.dma_start(pt[:], A["page_table"].rearrange("b n -> (b n)").unsqueeze(0)).then_inc(s_pt, 16)
                sp.wait_ge(s_pt, 16)
                with sp.Fori(0, HB) as i:
                    sp.wait_ge(s_kcps, i * SB + SB)
                    apart(sp, passed["sp"])
                    with sp.Fori(0, SB * NPG) as n:
                        page = sp.value_load(pt[0:1, bass.ds(n, 1)], min_val=0, max_val=A["cache_k"].shape[0] - 1)
                        sp.dma_start(kc[:, bass.ds(n, 1), :], A["cache_k"][bass.ds(page, 1), :, bass.ds(i, 1), :].rearrange("n p h d -> p (n h) d")).then_inc(s_kc, 16)
                    sp.wait_ge(s_ko, 3 * (i + 1))
                    apart(sp, passed["sp"])
                    sp.dma_start(OUT["k_p"][:, bass.ds(i, 1), :].rearrange("(t p) h e -> p t (h e)", p=P), ko[:, 0:NT, :]).then_inc(s_kst, 16)
                    sp.dma_start(OUT["k_s"][:, bass.ds(i, 1), :].rearrange("p h e -> p (h e)"), ko[0:TS, NT, :]).then_inc(s_kst, 16)
                    sp.wait_ge(s_v, 3 * (i + 1))
                    sp.wait_ge(s_kst, 64 * i + 32)
                    apart(sp, passed["sp"])
                    sp.dma_start(OUT["v_p"][:, bass.ds(i, 1), :].rearrange("(t p) h e -> p t (h e)", p=P), v[:, 0:NT, :]).then_inc(s_kst, 16)
                    sp.dma_start(OUT["v_s"][:, bass.ds(i, 1), :].rearrange("p h e -> p (h e)"), v[0:TS, NT, :]).then_inc(s_kst, 16)
                for b in range(2):
                    sp.wait_ge(s_proj, (HB + 1) * UNITS)
                    sp.dma_start(K[f"w{b}"][:], A["w_out_b"].rearrange("(k p) n -> p k n", p=P)[:, :, b * P:(b + 1) * P]).then_inc(
                        K["sem"](f"op_w_in{b}"), 16)

            @block.gpsimd
            def _(pool):
                nc.gpsimd.memset(QZ[:], 0.0).then_inc(s_set, 1)
                nc.gpsimd.memset(QN[:], 0.0).then_inc(s_set, 1)
                nc.gpsimd.memset(eps64[:], EPS * DQ).then_inc(s_set, 1)
                pool.sem_inc(s_proj, UNITS)
                pool.wait_ge(s_pt, 16)

                def load_weights(name, i, used):
                    pool.wait_ge(s_proj, i * UNITS + used)
                    apart(pool, passed["pool"])
                    pool.dma_start(w[name][:], wd[name][:, :, bass.ds(i * P, P)]).then_inc(s_w[name], 16)

                def head(i, last):
                    load_weights("z", i, 9)
                    load_weights("v", i, UNITS + 3)
                    pool.wait_ge(s_spv, i + 1)
                    apart(pool, passed["pool"])
                    with pool.Fori(0, SB * NPG) as n:
                        page = pool.value_load(pt[0:1, bass.ds(n, 1)], min_val=0, max_val=A["cache_v"].shape[0] - 1)
                        pool.dma_start(vc[:, bass.ds(n, 1), :], A["cache_v"][bass.ds(page, 1), :, bass.ds(i, 1), :].rearrange("n p h d -> p (n h) d")).then_inc(s_vc, 16)
                    if not last:
                        load_weights("q", i + 1, UNITS)
                        load_weights("k", i + 1, 6)

                over_heads(pool, head)

            @block.tensor
            def _(pe):
                pe.sem_inc(s_kcps, SB)
                pe.sem_inc(s_spv, 1)
                def project(name, i, unit, src):
                    pe.wait_ge(s_pfree, i * UNITS + unit + 1)
                    for k in range(KC):
                        mm = nc.tensor.matmul(psP[:, unit % 2, 0:THIRD], w[name][:, k, :], thirds(src[:, k, :])[unit % 3], start=(k == 0), stop=(k == KC - 1))
                    mm.then_inc(s_proj, 1)

                def project_v(r, i):
                    lo, hi = GROUPS[r]
                    pe.wait_ge(s_pfree, i * UNITS + 9 + r + 1)
                    for t in range(lo, hi):
                        n = P if t < NT else TS
                        for k in range(KC):
                            mm = nc.tensor.matmul(psP[0:n, (9 + r) % 2, (t - lo) * P:(t - lo + 1) * P], hk[:, k, t * P:t * P + n], w["v"][:, k, :],
                                                  start=(k == 0), stop=(k == KC - 1))
                    mm.then_inc(s_proj, 1)

                def head(i, last):
                    def squares(r):
                        pe.wait_ge(s_sq, 2 * i + r + 1)
                        for j in range(3):
                            mm = nc.tensor.matmul(psS[:, j, 0:THIRD], bones[:], thirds(sq)[j], start=True, stop=True)
                        mm.then_inc(s_oss, 1)

                    def turn_k(r):
                        lo, hi = GROUPS[r]
                        if r:
                            pe.wait_ge(s_ko, 3 * i + r)
                        for t in range(lo, hi):
                            n = P if t < NT else TS
                            mm = nc.tensor.transpose(psW[0:n, (t - lo) * P:(t - lo + 1) * P], kT[:, t * P:t * P + n], ident[:])
                        mm.then_inc(s_kops, 1)

                    def scores(t):
                        for comp in range(2):
                            rows = slice(DQ * comp, DQ * (comp + 1))
                            if t:
                                pe.wait_ge(s_min, 2 * NT * i + 2 * (t - 1) + comp + 1)
                            for lo in range(0, P * (t + 1), 512):
                                hi = min(lo + 512, P * (t + 1))
                                mm = nc.tensor.matmul(psS[:, 2 * comp + lo // 512, 0:hi - lo], qT[rows, t * P:(t + 1) * P], kT[rows, lo:hi], start=True, stop=True)
                            mm.then_inc(s_sc, 1)

                    def weigh(t, groups):
                        pe.wait_ge(s_wc, NT * i + t + 1)
                        for r in groups:
                            lo, hi = 4 * r, min(4 * r + 4, t + 1)
                            if t or r:
                                pe.wait_ge(s_wT, WB[NT] * i + WB[t] + r)
                            for k in range(lo, hi):
                                mm = nc.tensor.transpose(psW[:, (k - lo) * P:(k - lo + 1) * P], S[:, t % 2, 0, k * P:(k + 1) * P], ident[:])
                            mm.then_inc(s_wps, 1)

                    def values(t):
                        pe.wait_ge(s_wT, WB[NT] * i + WB[t + 1])
                        if t:
                            pe.wait_ge(s_oev, NT * i + t)
                        for k in range(t + 1):
                            mm = nc.tensor.matmul(psO[:, (t % 2) * P:(t % 2 + 1) * P], v[:, k, :], wT[:, t % 2, k * P:(k + 1) * P], start=(k == 0), stop=(k == t))
                        mm.then_inc(s_pv, 1)

                    def turn_cache(b):
                        if b:
                            pe.wait_ge(s_kcT, SB * i + b)
                        for n in range(NPG):
                            mm = nc.tensor.transpose(psP[:, 0, n * PAGE:(n + 1) * PAGE], kc[:, b * NPG + n, :], ident[:])
                        mm.then_inc(s_kcps, 1)

                    def cache_scores(b):
                        pe.wait_ge(s_kcT, SB * i + b + 1)
                        mm = nc.tensor.matmul(psP[0:SR, 1, :], QZ[:, b * SR:(b + 1) * SR], kcT[:, b % 2, :], start=(b == 0), stop=(b == SB - 1))
                        mm.then_inc(s_ssc, 1)

                    pe.wait_ge(s_w["k"], 16 * (i + 1))
                    project("k", i, 3, hk)
                    project("k", i, 4, hk)
                    pe.wait_ge(s_ors, i + 1)
                    squares(0)
                    project("k", i, 5, hk)
                    pe.wait_ge(s_w["z"], 16 * (i + 1))
                    for unit in range(6, 9):
                        project("z", i, unit, hb)
                    pe.wait_ge(s_rs, 2 * i + 1)
                    squares(1)
                    pe.wait_ge(s_w["v"], 16 * (i + 1))
                    project_v(0, i)
                    pe.wait_ge(s_qn, 2 * i + 2)
                    turn_k(0)
                    project_v(1, i)
                    turn_k(1)
                    scores(0)
                    project_v(2, i)
                    turn_k(2)
                    pe.wait_ge(s_ko, 3 * i + 3)
                    pe.wait_ge(s_v, 3 * i + 3)
                    pe.wait_ge(s_qz, i + 1)
                    pe.wait_ge(s_kc, 16 * SB * NPG * (i + 1))
                    for t in range(NT):
                        if t + 1 < NT:
                            scores(t + 1)
                        if t:
                            turn_cache(t - 1)
                            values(t - 1)
                        if t == NT - 1:
                            pe.wait_ge(s_min, 2 * NT * (i + 1))
                            nc.tensor.matmul(psS[0:SR, 1, 0:TS], QN[:], kT[:, TP:T], start=True, stop=True).then_inc(s_ssc, 1)
                            cache_scores(t - 1)
                            turn_cache(SB - 1)
                        weigh(t, [0])
                        if 0 < t < NT - 1:
                            cache_scores(t - 1)
                        if t == NT - 1:
                            cache_scores(SB - 1)
                        weigh(t, range(1, WG[t]))
                    if not last:
                        pe.wait_ge(s_w["q"], 16 * (i + 2))
                        project("q", i, UNITS, hb)
                    values(NT - 1)
                    pe.wait_ge(s_wT, WB[NT] * (i + 1))
                    pe.wait_ge(s_comb, i + 1)
                    for g in range(NPG):
                        nc.tensor.matmul(psW[:, g * TS:(g + 1) * TS], SS[:, g * PAGE:(g + 1) * PAGE], combr[:], start=True, stop=True)
                    nc.tensor.matmul(psW[0:TS, NPG * TS:(NPG + 1) * TS], SS[:, PAST:PAST + TS], combr[:], start=True, stop=True).then_inc(s_wsps, 1)
                    if not last:
                        project("q", i, UNITS + 1, hb)
                    pe.wait_ge(s_wsT, 2 * (i + 1))
                    pe.wait_ge(s_vc, 16 * SB * NPG * (i + 1))
                    pe.wait_ge(s_oev, NT * (i + 1))
                    for b in range(SB):
                        for g in range(NPG):
                            nc.tensor.matmul(psO[:, b * SL:(b + 1) * SL], vc[:, b * NPG + g, :], wsT[:, g, b * SL:(b + 1) * SL], start=(b == 0 and g == 0), stop=False)
                    nc.tensor.matmul(psO[:, 0:TS], v[0:TS, NT, :], wsT[0:TS, NPG, :], start=False, stop=True).then_inc(s_spv, 1)
                    if not last:
                        project("q", i, UNITS + 2, hb)
                    pe.wait_ge(s_osq, i + 1)
                    pe.wait_ge(s_smin, 2 * (i + 1))
                    for j in range(3):
                        mm = nc.tensor.matmul(psS[:, j, 0:THIRD], ones[:], thirds(sq)[j], start=True, stop=True)
                    mm.then_inc(s_oss, 1)

                pe.wait_ge(s_w["q"], 16)
                for unit in range(3):
                    project("q", 0, unit, hb)
                pe.wait_ge(s_const, 16 * 5)
                over_heads(pe, head)

            @block.scalar
            def _(act):
                A_ = nc.scalar.activation
                act.sem_inc(s_pfree, 2)
                act.sem_inc(s_ors, 1)
                act.wait_ge(s_set, 3)

                def done(i, unit):
                    act.wait_ge(s_proj, (i + 1) * UNITS + unit + 1)
                    return unit % 2

                def copy_out(dst, i, unit):
                    b = done(i, unit)
                    A_(thirds(dst[:])[unit % 3], psP[:, b, 0:THIRD], ACT.Copy).then_inc(s_qk, 1)
                    act.wait_ge(s_qk, 6 * i + (unit if unit < 6 else unit - UNITS + 6) + 1)
                    act.sem_inc(s_pfree, 1)

                def head(i, last):
                    def rstd(r):
                        act.wait_ge(s_oss, 3 * i + r + 1)
                        A_(rs[:].rearrange("p (j t) -> p j t", j=3), psS[:, 0:3, 0:THIRD], ACT.Ln, scale=(1.0, 1.0 / DQ)[r],
                           bias=(eps64, K["eps"])[r][:, 0:1]).then_inc(s_oln, 1)
                        act.wait_ge(s_oln, 3 * i + r + 1)
                        A_(rs[:], rs[:], ACT.Exp, scale=-0.5).then_inc(s_rs, 1)

                    act.wait_ge(s_qk, 6 * i + 3)
                    A_(sq, qT[:], ACT.Square).then_inc(s_sq, 1)
                    copy_out(kT, i, 3)
                    copy_out(kT, i, 4)
                    act.wait_ge(s_g2, i + 1)
                    rstd(0)
                    copy_out(kT, i, 5)
                    A_(sq, kT[:], ACT.Square).then_inc(s_sq, 1)
                    for j in range(3):
                        b = done(i, 6 + j)
                        if j == 2:
                            act.wait_ge(s_zs, 3 * i + 1)
                        A_(thirds(zs[:])[j], psP[:, b, 0:THIRD], ACT.Copy, scale=0.5)
                        A_(th[:, j % 2, :], psP[:, b, 0:THIRD], ACT.Tanh, scale=0.5).then_inc(s_pfree, 1)
                    act.wait_ge(s_qn, 2 * i + 1)
                    rstd(1)
                    for r, (lo, hi) in enumerate(GROUPS):
                        b = done(i, 9 + r)
                        n = P if lo < NT else TS
                        A_(v[0:n, lo:hi, :].rearrange("p a d -> p (a d)"), psP[0:n, b, 0:(hi - lo) * P], ACT.Copy).then_inc(s_v, 1)
                        act.wait_ge(s_v, 3 * i + r + 1)
                        act.sem_inc(s_pfree, 1)
                        act.wait_ge(s_kops, 3 * i + r + 1)
                        A_(ko[0:n, lo:hi, :].rearrange("p a d -> p (a d)"), psW[0:n, 0:(hi - lo) * P], ACT.Copy).then_inc(s_ko, 1)

                    def exps(t):
                        n = P * (t + 1)
                        for comp in range(2):
                            act.wait_ge(s_min, 2 * NT * i + 2 * t + comp + 1)
                            s = S[:, t % 2, comp, 0:n]
                            A_(s, s, ACT.Exp, scale=-1.0, bias=nmx[:, t % 2, comp:comp + 1], accum_out=rsum[:, t % 2, comp:comp + 1]).then_inc(s_exp, 1)

                    def copies(t):
                        for r in range(WG[t]):
                            lo, hi = 4 * r, min(4 * r + 4, t + 1)
                            act.wait_ge(s_wps, WB[NT] * i + WB[t] + r + 1)
                            if t >= 2:
                                act.wait_ge(s_pv, NT * i + t - 1)
                            A_(wT[:, t % 2, lo * P:hi * P], psW[:, 0:(hi - lo) * P], ACT.Copy).then_inc(s_wT, 1)

                    def out(t):
                        act.wait_ge(s_pv, NT * i + t + 1)
                        apart(act, passed["act"])
                        A_(G[:, bass.ds(i, 1), t * P:(t + 1) * P].rearrange("p a t -> p (a t)"), psO[:, (t % 2) * P:(t % 2 + 1) * P], ACT.Copy).then_inc(s_oev, 1)

                    exps(0)

                    def cached(b):
                        act.wait_ge(s_kcps, SB * i + SB + b + 1)
                        if b >= 2:
                            act.wait_ge(s_ssc, (SB + 1) * i + b - 1)
                        A_(kcT[:, b % 2, :], psP[:, 0, :], ACT.Copy).then_inc(s_kcT, 1)

                    for t in range(NT):
                        if t == 1:
                            act.wait_ge(s_kst, 64 * i + 32)
                        if t:
                            cached(t - 1)
                        if t == NT - 1:
                            cached(SB - 1)
                        copies(t)
                        if t + 1 < NT:
                            exps(t + 1)
                        if t:
                            out(t - 1)
                    act.wait_ge(s_smin, 2 * (i + 1))
                    A_(SS, SS, ACT.Exp, scale=-1.0, bias=snm[:, 1:2], accum_out=ssum[:]).then_inc(s_sexp, 1)
                    if not last:
                        copy_out(qT, i, UNITS)
                    out(NT - 1)
                    act.wait_ge(s_kst, 64 * (i + 1))
                    act.wait_ge(s_wsps, i + 1)
                    A_(wsT[:, 0:NPG, :].rearrange("p a d -> p (a d)"), psW[:, 0:NPG * TS], ACT.Copy).then_inc(s_wsT, 1)
                    A_(wsT[0:TS, NPG, :], psW[0:TS, NPG * TS:(NPG + 1) * TS], ACT.Copy).then_inc(s_wsT, 1)
                    if not last:
                        copy_out(qT, i, UNITS + 1)
                    g = G[:, bass.ds(i, 1), :].rearrange("p a t -> p (a t)")
                    act.wait_ge(s_spv, i + 2)
                    apart(act, passed["act"])
                    A_(g[:, TP:T], psO[:, 0:TS], ACT.Copy).then_inc(s_soev, 1)
                    act.wait_ge(s_soev, i + 1)
                    act.wait_ge(s_oev, NT * (i + 1))
                    apart(act, passed["act"])
                    A_(sq, g, ACT.Square).then_inc(s_osq, 1)
                    if not last:
                        copy_out(qT, i, UNITS + 2)
                    act.wait_ge(s_oss, 3 * i + 3)
                    A_(rs[:].rearrange("p (j t) -> p j t", j=3), psS[:, 0:3, 0:THIRD], ACT.Ln, scale=1.0 / DE, bias=K["eps"][:, 0:1]).then_inc(s_oln, 1)
                    act.wait_ge(s_oln, 3 * i + 3)
                    A_(rs[:], rs[:], ACT.Exp, scale=-0.5).then_inc(s_ors, 1)

                for unit in range(3):
                    copy_out(qT, 0, unit)
                over_heads(act, head)

            @block.vector
            def _(dve):
                V = nc.vector
                lam_init = 0.8 - 0.6 * float(np.exp(-0.3))
                dve.wait_ge(s_const, 16 * 5)
                V.tensor_scalar(subg[:], vec[:, V_SUBLN:V_SUBLN + 1], 1.0 - lam_init, None, ALU.mult).then_inc(s_init, 1)
                V.scalar_tensor_tensor(lamrow[:], rowsel[:, 1:2], K["nlam"][0:SR, 0:1], rowsel[:, 0:1], ALU.mult, ALU.add).then_inc(s_init, 1)
                dve.wait_ge(s_init, 2)
                dve.wait_ge(s_set, 3)
                dve.sem_inc(s_g2, 1)
                with dve.Fori(0, HB) as i:
                    V.tensor_scalar(bias[:], bias[:], 0.5, None, ALU.mult).then_inc(s_bias, 1)
                    V.tensor_scalar(sbias[:], sbias[:], 0.5, None, ALU.mult).then_inc(s_bias, 1)
                    def norm(r, dst, col):
                        dve.wait_ge(s_rs, 2 * i + r + 1)
                        V.scalar_tensor_tensor(dst[:], dst[:], vec[:, col:col + 1], rs[:], ALU.mult, ALU.mult).then_inc(s_qn, 1)

                    dve.wait_ge(s_sq, 2 * i + 1)
                    norm(0, qT, V_GQ)
                    for j in range(3):
                        dve.wait_ge(s_pfree, 2 + i * UNITS + 6 + j + 1)
                        z = thirds(zs[:])[j]
                        V.scalar_tensor_tensor(z, th[:, j % 2, :], 1.0, z, ALU.add, ALU.mult).then_inc(s_zs, 1)
                    dve.wait_ge(s_sq, 2 * i + 2)
                    norm(1, kT, V_GK)
                    dve.wait_ge(s_qn, 2 * i + 2)
                    for comp in range(2):
                        rows = slice(DQ * comp, DQ * (comp + 1))
                        V.tensor_copy(QZ[rows, :].rearrange("p (b r) -> p b r", r=SR + SL)[:, :, comp * TS:comp * TS + SL],
                                      qT[rows, TP:T].rearrange("p (b t) -> p b t", b=SB))
                        last = V.tensor_copy(QN[rows, comp * TS:(comp + 1) * TS], qT[rows, TP:T])
                    last.then_inc(s_qz, 1)
                    dve.wait_ge(s_bias, 2 * (i + 1))

                    def mins(t):
                        n = P * (t + 1)
                        for comp in range(2):
                            dve.wait_ge(s_sc, 2 * NT * i + 2 * t + comp + 1)
                            if t >= 2:
                                dve.wait_ge(s_wps, WB[NT] * i + WB[t - 1])
                                dve.wait_ge(s_wc, NT * i + t - 1)
                            apart(dve, passed["dve"])
                            V.tensor_tensor_reduce(S[:, t % 2, comp, 0:n], psS[:, 2 * comp:2 * comp + 2, :].rearrange("p a k -> p (a k)")[:, 0:n],
                                                   bias[:, TP - n:TP], -1.0, 3.0e38, ALU.add, ALU.min, nmx[:, t % 2, comp:comp + 1]).then_inc(s_min, 1)

                    def combine(t):
                        n = P * (t + 1)
                        dve.wait_ge(s_exp, 2 * NT * i + 2 * t + 2)
                        V.reciprocal(rr[:, t % 2, :], rsum[:, t % 2, :]).then_inc(s_rec, 1)
                        dve.wait_ge(s_rec, NT * i + t + 1)
                        V.tensor_tensor(rr[:, t % 2, 1:2], rr[:, t % 2, 1:2], K["nlam"][:], ALU.mult).then_inc(s_r1, 1)
                        dve.wait_ge(s_r1, NT * i + t + 1)
                        V.tensor_scalar(S[:, t % 2, 1, 0:n], S[:, t % 2, 1, 0:n], rr[:, t % 2, 1:2], None, ALU.mult).then_inc(s_p1, 1)
                        dve.wait_ge(s_p1, NT * i + t + 1)
                        V.scalar_tensor_tensor(S[:, t % 2, 0, 0:n], S[:, t % 2, 0, 0:n], rr[:, t % 2, 0:1], S[:, t % 2, 1, 0:n],
                                               ALU.mult, ALU.add).then_inc(s_wc, 1)

                    mins(0)
                    for t in range(NT):
                        combine(t)
                        if t + 1 < NT:
                            mins(t + 1)
                    dve.wait_ge(s_ssc, (SB + 1) * (i + 1))
                    apart(dve, passed["dve"])
                    V.tensor_tensor_reduce(SS[:, 0:PAST], psP[0:SR, 1, :], sbias[:, 0:PAST], -1.0, 3.0e38, ALU.add, ALU.min, snm[:, 0:1]).then_inc(s_smin, 1)
                    dve.wait_ge(s_smin, 2 * i + 1)
                    apart(dve, passed["dve"])
                    V.tensor_tensor_reduce(SS[:, PAST:PAST + TS], psS[0:SR, 1, 0:TS], sbias[:, PAST:PAST + TS], -1.0, snm[:, 0:1], ALU.add, ALU.min,
                                           snm[:, 1:2]).then_inc(s_smin, 1)
                    dve.wait_ge(s_sexp, i + 1)
                    V.reciprocal(srr[:, 0:1], ssum[:]).then_inc(s_srec, 1)
                    dve.wait_ge(s_srec, 2 * i + 1)
                    V.tensor_tensor(srr[:, 1:2], srr[:, 0:1], lamrow[:], ALU.mult).then_inc(s_srec, 1)
                    dve.wait_ge(s_srec, 2 * i + 2)
                    V.tensor_scalar(combr[:], comb[:], srr[:, 1:2], None, ALU.mult).then_inc(s_comb, 1)
                    dve.wait_ge(s_ors, i + 2)
                    g = G[:, bass.ds(i, 1), :].rearrange("p a t -> p (a t)")
                    V.scalar_tensor_tensor(g, g, subg[:, 0:1], rs[:], ALU.mult, ALU.mult).then_inc(s_g1, 1)
                    dve.wait_ge(s_g1, i + 1)
                    dve.wait_ge(s_zs, 3 * i + 3)
                    V.tensor_tensor(g, g, zs[:], ALU.mult).then_inc(s_g2, 1)
                    dve.wait_ge(s_g2, i + 2)


def store_y(nc, OUT, K):
    with ExitStack() as c:
        sem = lambda n: K["sem"]("st_" + n)
        ps = c.enter_context(nc.psum_tensor("st_ps", [P, 4, 512], F32))
        y = c.enter_context(nc.sbuf_tensor("st_y", [P, NT + 1, D], F32))
        s_ps, s_y = sem("turned"), sem("copied")
        s_out = sem("y_out")
        B, ident = K["B1"], K["ident"]
        with nc.Block() as block:
            @block.tensor
            def _(pe):
                for u in range(2 * (NT + 1)):
                    t, half = u // 2, u % 2
                    n = P if t < NT else TS
                    if u >= 4:
                        pe.wait_ge(s_y, u - 3)
                    for q in range(4):
                        mm = nc.tensor.transpose(ps[0:n, u % 4, q * P:(q + 1) * P], B[:, 4 * half + q, t * P:t * P + n], ident[:])
                    mm.then_inc(s_ps, 1)

            @block.scalar
            def _(act):
                for u in range(2 * (NT + 1)):
                    t, half = u // 2, u % 2
                    n = P if t < NT else TS
                    act.wait_ge(s_ps, u + 1)
                    nc.scalar.activation(y[0:n, t, half * 512:(half + 1) * 512], ps[0:n, u % 4, :], ACT.Copy).then_inc(s_y, 1)

            @block.sync
            def _(sp):
                for t in range(NT + 1):
                    sp.wait_ge(s_y, 2 * t + 2)
                    if t < NT:
                        sp.dma_start(OUT["y_p"][t * P:(t + 1) * P, :], y[:, t, :]).then_inc(s_out, 16)
                    else:
                        sp.dma_start(OUT["y_s"], y[0:TS, t, :]).then_inc(s_out, 16)
                sp.wait_ge(s_out, 16 * (NT + 1))



def shape_constants():
    s, t = np.arange(P)[:, None], np.arange(P)[None, :]
    f = np.float32

    def level(L):
        return (s // (2 * L) == t // (2 * L)) & (s % (2 * L) < L) & (t % (2 * L) >= L)

    masks = np.stack([level(L) for L in LEVELS] + [s == t], 1).astype(f)
    seq = (s // SL == t // SL)[:TS, :TS]
    smasks = np.stack([level(2)[:TS, :TS] & seq, level(1)[:TS, :TS] & seq, (s == t)[:TS, :TS]], 1).astype(f)
    restart = np.ones((P, T), f)
    restart[:, 0:TP:P] = 0.0
    restart[:, TP:T:SL] = 0.0
    rowsel = (np.arange(TS)[:, None] // SL == np.arange(SB)[None, :]).astype(f)
    x = np.arange(TP)[None, :] - np.arange(P)[:, None] - (TP - P)
    bias = np.where(x <= 0, x, NEG).astype(f)
    r = np.arange(SR)
    seq_r, q_r = (r % TS) // SL, r % SL
    past = np.arange(PAST)[None, :] - (PAST + q_r)[:, None]
    n = np.arange(TS)
    new = np.where((seq_r[:, None] == n[None, :] // SL) & (n[None, :] % SL <= q_r[:, None]), n[None, :] % SL - q_r[:, None], NEG)
    sbias = np.concatenate([past, new], 1).astype(f)
    bones = (s // DQ == t // DQ).astype(f)
    comb = (r[:, None] % TS == n[None, :]).astype(f)
    lamsel = np.stack([r < TS, r >= TS], 1).astype(f)
    return {"ident": np.eye(P, dtype=f), "ones": np.ones((P, P), f), "masks": masks, "smasks": smasks, "restart": restart, "rowsel": rowsel,
            "bias": bias, "sbias": sbias, "bones": bones, "comb": comb, "lamsel": lamsel}


_OUTS = {"y_p": (TP, D), "y_s": (TS, D), "state_p": (HA, DK, DV), "state_s": (SB, HA, DK, DV), "k_p": (TP, HB, P), "v_p": (TP, HB, DE),
         "k_s": (TS, HB, P), "v_s": (TS, HB, DE)}


def kernel(**inputs):
    import concourse.bacc as bacc
    from concourse.bass_utils import run_bass_kernel_spmd

    a = {k: np.asarray(v) for k, v in inputs.items()}
    flat = {
        "x_prompt": a["x_prompt"].reshape(TP, D), "x_sample": a["x_sample"].reshape(TS, D),
        "cache_k": a["cache_k"].reshape(-1, PAGE, HB, P), "cache_v": a["cache_v"].reshape(-1, PAGE, HB, DE),
        "state_gla": a["state_gla"].reshape(SB, HA, DK, DV),
    }
    for k in ("norm_a", "ada_w_a", "ada_b_a", "w_in_a", "w_g2_a", "b_g_a", "onorm_a", "w_out_a", "norm_b", "ada_w_b", "ada_b_b", "w_in_b",
              "g_q", "lambda_q1", "lambda_k1", "lambda_q2", "lambda_k2", "subln_b", "w_out_b"):
        flat[k] = a[k][0]
    for k in ("c_prompt", "c_sample", "page_table", "norm_kv", "ada_w_kv", "ada_b_kv", "w_k", "w_v", "g_k"):
        flat[k] = a[k]
    flat.update(shape_constants())
    nc = bacc.Bacc("TRN2", target_bir_lowering=False, num_devices=1)
    arrays, ins = {}, {}
    for name, x in flat.items():
        arrays["in_" + name] = np.ascontiguousarray(x)
        ins[name] = nc.dram_tensor("in_" + name, x.shape, mybir.dt.from_np(x.dtype), kind="ExternalInput").ap()
    outs = {name: nc.dram_tensor("out_" + name, shape, F32, kind="ExternalOutput").ap() for name, shape in _OUTS.items()}
    scratch = {name: nc.dram_tensor("scr_" + name, (D, T), F32, kind="Internal").ap() for name in ("xT", "x1T")}
    build(nc, ins, outs, scratch)
    r = run_bass_kernel_spmd(nc, [arrays], core_ids=[0]).results[0]
    o = {name: r["out_" + name] for name in _OUTS}
    return (o["y_p"].reshape(1, TP, D), o["y_s"].reshape(SB, SL, D), o["state_p"].reshape(1, 1, HA, DK, DV),
            o["state_s"].reshape(1, SB, HA, DK, DV), o["k_p"].reshape(1, TP, HB, 2, DQ), o["v_p"].reshape(1, TP, HB, DE),
            o["k_s"].reshape(SB, SL, HB, 2, DQ), o["v_s"].reshape(SB, SL, HB, DE))
```

```python
from contextlib import ExitStack

import numpy as np

import concourse.bass as bass
from concourse import mybir

F32 = mybir.dt.float32
F32R = mybir.dt.float32r
I32 = mybir.dt.int32
ALU = mybir.AluOpType
ACT = mybir.ActivationFunctionType
AX = mybir.AxisListType

P = 128
D = 1024
KC = D // P
TP = 1024
NT = TP // P
SB, SL = 8, 4
TS = SB * SL
T = TP + TS
NC = SB + 1
THIRD = T // 3
HA, DK, DV = 4, 128, 256
RANK = 16
HB, DQ, DE = 8, 64, 128
PAST, PAGE = 512, 128
NPG = PAST // PAGE
EPS = 1e-6
LEVELS = [64, 32, 16, 8, 4, 2, 1]
NL = len(LEVELS)
SLEV = [5, 6]
SR = 2 * TS
NEG = -1.0e30

V_ADA, V_NORM_A, V_NORM_KV, V_NORM_B, V_BG, V_ONORM, V_SUBLN, V_GQ, V_GK, V_N = 0, 64, 72, 80, 88, 92, 94, 95, 96, 97
M_A, M_KV, M_B, M_N = 0, 24, 40, 64


def apart(eng, passed):
    eng.sem_inc(passed, 1)


def thirds(ap):
    return [ap[:, THIRD * j:THIRD * (j + 1)] for j in range(3)]


def bcast(ap, *shape):
    return ap.broadcast_to(list(shape))


def build(nc, A, OUT, SCR):
    g = ExitStack()
    with g:
        def sb(name, shape, ctx=g, dt=F32):
            return ctx.enter_context(nc.sbuf_tensor(name, shape, dt))

        def sem(name, ctx=g):
            return ctx.enter_context(nc.semaphore(name))

        made = {}

        def shared(name):
            if name not in made:
                made[name] = sem(name)
            return made[name]

        K = {"sem": shared}
        K["ident"] = sb("ident", [P, P])
        K["ones"] = sb("ones", [P, P])
        K["vec"] = sb("vec", [P, V_N])
        K["mod"] = sb("mod", [P, M_N, NC])
        K["eps"] = sb("eps", [P, 1])
        K["nlam"] = sb("nlam", [P, 1])
        K["cT"] = sb("cT", [P, KC, NC])
        K["w0"] = sb("w0", [P, KC, P])
        K["w1"] = sb("w1", [P, KC, P])
        K["wlow"] = sb("wlow", [P, KC, RANK])
        K["B2"] = sb("B2", [P, KC, T])
        with ExitStack() as c:
            K["Hh"], K["Hl"] = sb("Hh", [P, KC, T], c, F32R), sb("Hl", [P, KC, T], c, F32R)
            setup(nc, A, SCR, K)
            gla(nc, A, OUT, SCR, K)
        K["B1"] = sb("B1", [P, KC, T])
        K["G"] = sb("G", [P, KC, T])
        with ExitStack() as c:
            acc, tmp = sb("no_acc", [P, T], c), sb("no_tmp", [P, 2, KC, SB, SL], c)
            sq = K["B1"][:, 2:4, :]
            rs = acc
            ps = c.enter_context(nc.psum_tensor("no_ps", [P, 4, 512], F32))
            norm = Norm(nc, K, K["B2"], rs, sq, acc, ps, [(K["B1"], M_B + 8, M_B), (K["B2"], M_KV + 8, M_KV)], 1)
            out_proj(nc, A["w_out_a"], SCR["xT"], SCR["x1T"], K["B2"], M_A + 16, K, 0, norm, SCR["G"].rearrange("(k p) t -> p k t", p=P))
            normed(nc, A, K, norm, tmp)
        attention(nc, A, OUT, K, norm)
        out_proj(nc, A["w_out_b"], SCR["x1T"], None, K["B1"], M_B + 16, K, 1, OUT=OUT)


class Norm:

    def __init__(self, nc, K, src, rs, sq, acc, ps, affine, use):
        self.nc, self.K, self.src, self.rs, self.sq, self.acc, self.ps, self.affine, self.use = nc, K, src, rs, sq, acc, ps, affine, use
        self.sq_ready, self.sq_used = K["sem"]("n_sq_ready"), K["sem"]("n_sq_used")
        self.summed, self.ln_ready, self.rs_ready = K["sem"]("n_summed"), K["sem"]("n_ln_ready"), K["sem"]("n_rs_ready")
        self.xr_ready, self.s_mul = K["sem"]("n_xr_ready"), K["sem"]("n_s_mul")

    def act_square(self, eng, k):
        if k >= 3:
            eng.wait_ge(self.sq_used, self.use * (KC - 1) + k - 2)
        self.nc.scalar.activation(self.acc[:] if k == 0 else self.sq[:, k % 2, :], self.src[:, k, :], ACT.Square).then_inc(self.sq_ready, 1)

    def dve_add(self, eng, k, slot, first=False):
        eng.wait_ge(self.sq_ready, k + (self.use * KC + 1))
        if not first:
            eng.wait_ge(self.sq_used, k + (self.use * (KC - 1) - 1))
        self.nc.vector.tensor_tensor(self.acc[:], self.acc[:], self.sq[:, slot, :], ALU.add).then_inc(self.sq_used, 1)

    def pe_sum(self, eng):
        eng.wait_ge(self.sq_used, (self.use + 1) * (KC - 1))
        for j, part in enumerate(thirds(self.acc[:])):
            mm = self.nc.tensor.matmul(self.ps[:, j, 0:THIRD], self.K["ones"][:], part, start=True, stop=True)
        mm.then_inc(self.summed, 1)

    def act_rstd(self, eng):
        eng.wait_ge(self.summed, self.use + 1)
        self.nc.scalar.activation(self.rs[:].rearrange("p (j t) -> p j t", j=3), self.ps[:, 0:3, 0:THIRD], ACT.Ln,
                                  scale=1.0 / D, bias=self.K["eps"][:, 0:1]).then_inc(self.ln_ready, 1)
        eng.wait_ge(self.ln_ready, self.use + 1)
        self.nc.scalar.activation(self.rs[:], self.rs[:], ACT.Exp, scale=-0.5).then_inc(self.rs_ready, 1)

    def dve_rstd(self, eng):
        eng.wait_ge(self.rs_ready, self.use + 1)
        for k in range(KC):
            self.nc.vector.tensor_tensor(self.src[:, k, :], self.src[:, k, :], self.rs[:], ALU.mult).then_inc(self.xr_ready, 1)

    def act_affine(self, eng, affine, done):
        mod = self.K["mod"]
        for k in range(KC):
            eng.wait_ge(self.xr_ready, self.use * KC + k + 1)
            for dst, a, b in affine:
                last = self.nc.scalar.activation(dst[:, k, 0:TP], self.src[:, k, 0:TP], ACT.Identity, scale=mod[:, a + k, 0:1],
                                                 bias=mod[:, b + k, 0:1])
            if done is not None:
                last.then_inc(done, 1)

    def dve_samples(self, eng, tmp):
        mod = self.K["mod"]
        xs = self.src[:, :, TP:T].rearrange("p k (b t) -> p k b t", b=SB)
        eng.wait_ge(self.xr_ready, (self.use + 1) * KC)
        for n, (dst, a, b) in enumerate(self.affine):
            av = bcast(mod[:, a:a + KC, 1:NC].unsqueeze(3), P, KC, SB, SL)
            self.nc.vector.tensor_tensor(tmp[:, n], xs, av, ALU.mult).then_inc(self.s_mul, 1)
        eng.wait_ge(self.s_mul, self.use * 4 + 2)
        for n, (dst, a, b) in enumerate(self.affine):
            bv = bcast(mod[:, b:b + KC, 1:NC].unsqueeze(3), P, KC, SB, SL)
            self.nc.vector.tensor_tensor(dst[:, :, TP:T].rearrange("p k (b t) -> p k b t", b=SB), tmp[:, n], bv, ALU.add).then_inc(self.s_mul, 1)


def setup(nc, A, SCR, K):
    with ExitStack() as c:
        sem = lambda n: K["sem"]("su_" + n)
        tile = lambda n, s: c.enter_context(nc.sbuf_tensor("su_" + n, s, F32))
        psT = c.enter_context(nc.psum_tensor("su_psT", [P, 2, 512], F32))
        psM = c.enter_context(nc.psum_tensor("su_psM", [P, 2, 512], F32))
        psS = c.enter_context(nc.psum_tensor("su_psS", [P, 4, 512], F32))
        rows = tile("rows", [V_N, P])
        crow = tile("crow", [NC, D])
        cth = tile("cth", [NC, D])
        cT = K["cT"]
        lam = tile("lam", [1, 4, DQ])
        lamp = tile("lamp", [1, DQ])
        lams = tile("lams", [1, 2])
        lame = tile("lame", [P, 2])
        XB = 3
        xt = tile("xt", [P, XB, D])
        mrow = tile("mrow", [NC, 2, 512])
        w = tile("w", [P, 4, KC, 256])
        rs = tile("rs", [P, T])
        sq = tile("sq", [P, 2, T])
        acc = tile("acc", [P, T])
        tmp = tile("tmp", [P, 2, KC, SB, SL])
        xT, mod, vec, ident, ones = K["B2"], K["mod"], K["vec"], K["ident"], K["ones"]
        s_tab = sem("tables_in")
        s_x = [sem(f"x_in{j}") for j in range(XB)]
        s_id, s_mrow, s_mT = sem("ident_in"), sem("mod_rows"), sem("mod_turned")
        s_w = [sem(f"w_in{j}") for j in range(4)]
        s_wfree, s_set = sem("w_used"), sem("eps_set")
        s_vecT, s_vec = sem("vec_turned"), sem("vec_ready")
        s_cth, s_csil, s_cps, s_cT = sem("c_tanh"), sem("c_silu"), sem("c_turned"), sem("cT_ready")
        s_lsum, s_lps, s_lexp, s_lam2 = sem("lam_sums"), sem("lam_bcast"), sem("lam_exp"), sem("lam_diff")
        s_xps, s_xev, s_mev, s_scl = sem("x_turned"), sem("x_copied"), sem("mod_ready"), K["sem"]("scales_ready")
        s_out = sem("xT_out")
        norm = Norm(nc, K, xT, rs, sq, acc, psS, [(K["Hh"], M_A + 8, M_A), (xT, M_A + 8, M_A)], 0)
        s_hi, s_lo = K["sem"]("gl_high"), K["sem"]("gl_low")
        GROUPS = 3
        TABS = 20

        def load_mod(eng, slots):
            wd = A["ada_w_a"].rearrange("(k p) n -> p k n", p=P)
            with eng.Fori(0, GROUPS) as i:
                for j in slots:
                    eng.wait_ge(s_wfree, i * 4 + j + 1)
                    apart(eng, passed[slots[0]])
                    eng.dma_start(w[:, j], wd[:, :, bass.ds(i * 1024 + 256 * j, 256)]).then_inc(s_w[j], 16)

        passed = {0: K["sem"]("passed_sp"), 1: K["sem"]("passed_pool"), "pe": K["sem"]("passed_pe")}
        with nc.Block() as block:
            @block.sync
            def _(sp):
                sp.dma_start(ident[:], A["ident"]).then_inc(s_id, 16)
                sp.dma_start(ones[:], A["ones"]).then_inc(s_tab, 16)
                sp.sem_inc(s_wfree, 4)
                at = 0
                for name, n in (("ada_b_a", 24), ("ada_b_kv", 16), ("ada_b_b", 24), ("norm_a", 8), ("norm_kv", 8), ("norm_b", 8),
                                ("b_g_a", 4), ("onorm_a", 2), ("subln_b", 1)):
                    sp.dma_start(rows[at:at + n, :], A[name].rearrange("(r c) -> r c", c=P)).then_inc(s_tab, 16)
                    at += n
                for name in ("g_q", "g_k"):
                    for half in range(2):
                        sp.dma_start(rows[at:at + 1, DQ * half:DQ * (half + 1)], A[name].unsqueeze(0)).then_inc(s_tab, 16)
                    at += 1
                sp.dma_start(crow[0:1, :], A["c_prompt"]).then_inc(s_tab, 16)
                sp.dma_start(crow[1:NC, :], A["c_sample"]).then_inc(s_tab, 16)
                for j, name in enumerate(("lambda_q1", "lambda_k1", "lambda_q2", "lambda_k2")):
                    sp.dma_start(lam[0:1, j, :], A[name].unsqueeze(0)).then_inc(s_tab, 16)
                load_mod(sp, (0, 2))
                sp.dma_start(K["wlow"][:], A["w_in_a"].rearrange("(k p) n -> p k n", p=P)[:, :, 3072:3088]).then_inc(K["sem"]("gl_low_in"), 16)

            @block.gpsimd
            def _(pool):
                nc.gpsimd.memset(K["eps"][:], EPS).then_inc(s_set, 1)
                load_mod(pool, (1, 3))
                for n in range(2):
                    pool.dma_start(K[f"w{n}"][:], A["w_in_a"].rearrange("(k p) n -> p k n", p=P)[:, :, 512 * n:512 * n + P]).then_inc(
                        K["sem"](f"gl_w_in{n}"), 16)

            @block.tensor
            def _(pe):
                pe.wait_ge(s_id, 16)
                for t in range(NT + 1):
                    pe.wait_ge(s_x[t % XB], 16 * (t // XB + 1))
                    n = P if t < NT else TS
                    for half in range(2):
                        u = 2 * t + half
                        if u >= 2:
                            pe.wait_ge(s_xev, u - 1)
                        for q in range(4):
                            k = 4 * half + q
                            mm = nc.tensor.transpose(psT[:, u % 2, q * P:q * P + n], xt[0:n, t % XB, k * P:(k + 1) * P], ident[0:n, 0:n])
                        mm.then_inc(s_xps, 1)
                    if t == 2:
                        pe.wait_ge(s_tab, 16 * TABS)
                        nc.tensor.transpose(psM[:, 0, 0:V_N], rows[:], ident[0:V_N, 0:V_N]).then_inc(s_vecT, 1)
                        pe.wait_ge(s_csil, 1)
                        for k in range(KC):
                            mm = nc.tensor.transpose(psM[:, 1, k * NC:(k + 1) * NC], crow[:, k * P:(k + 1) * P], ident[0:NC, 0:NC])
                        mm.then_inc(s_cps, 1)
                pe.wait_ge(s_lsum, 2)
                pe.wait_ge(s_vec, 1)
                nc.tensor.matmul(psM[:, 0, 0:2], ones[0:1, :], lams[0:1, :], start=True, stop=True).then_inc(s_lps, 1)
                pe.wait_ge(s_xev, 2 * (NT + 1))
                pe.wait_ge(s_cT, 1)
                pe.wait_ge(s_lexp, 1)
                def modulations(i):
                    for j in range(4):
                        pe.wait_ge(s_w[j], (i + 1) * 16)
                        for k in range(KC):
                            mm = nc.tensor.matmul(psM[0:NC, j // 2, (j % 2) * 256:(j % 2 + 1) * 256], cT[:, k, :], w[:, j, k, :],
                                                  start=(k == 0), stop=(k == KC - 1))
                        mm.then_inc(s_wfree, 1)
                    for b in range(2):
                        pe.wait_ge(s_mrow, 2 * i + b + 1)
                        pe.wait_ge(s_mev, 2 * i + b + 1)
                        apart(pe, passed["pe"])
                        for m in range(4):
                            mm = nc.tensor.transpose(psT[:, b, m * NC:(m + 1) * NC], mrow[:, b, m * P:(m + 1) * P], ident[0:NC, 0:NC])
                        mm.then_inc(s_mT, 1)

                modulations(0)
                norm.pe_sum(pe)
                with pe.Fori(1, GROUPS) as i:
                    modulations(i)

            @block.scalar
            def _(act):
                def load_x(t):
                    if t < NT:
                        act.dma_start(xt[:, t % XB, :], A["x_prompt"][t * P:(t + 1) * P, :]).then_inc(s_x[t % XB], 16)
                    else:
                        act.dma_start(xt[0:TS, t % XB, :], A["x_sample"]).then_inc(s_x[t % XB], 16)

                for t in range(XB):
                    load_x(t)
                act.wait_ge(s_tab, 16 * TABS)
                nc.scalar.activation(cth[:], crow[:], ACT.Tanh, scale=0.5).then_inc(s_cth, 1)
                for t in range(XB, NT + 1):
                    act.wait_ge(s_xps, 2 * (t - XB + 1))
                    load_x(t)
                act.wait_ge(s_lps, 1)
                nc.scalar.activation(lame[:], psM[:, 0, 0:2], ACT.Exp).then_inc(s_lexp, 1)
                act.wait_ge(s_xev, 2 * (NT + 1))
                act.dma_start(SCR["xT"].rearrange("(k p) t -> p k t", p=P), xT[:]).then_inc(s_out, 16)
                act.wait_ge(s_set, 1)
                for k in range(KC):
                    norm.act_square(act, k)
                norm.act_rstd(act)
                act.wait_ge(s_scl, 1)
                norm.act_affine(act, norm.affine, s_hi)

            @block.vector
            def _(dve):
                for u in range(2 * (NT + 1)):
                    if u == 6:
                        dve.wait_ge(s_cth, 1)
                        dve.wait_ge(s_tab, 16 * TABS)
                        nc.vector.scalar_tensor_tensor(cth[:], cth[:], 1.0, crow[:], ALU.add, ALU.mult).then_inc(s_cth, 1)
                        dve.wait_ge(s_cth, 2)
                        nc.vector.tensor_scalar(crow[:], cth[:], 0.5, None, ALU.mult).then_inc(s_csil, 1)
                        dve.wait_ge(s_tab, 16 * TABS)
                        for j in range(2):
                            if j:
                                dve.wait_ge(s_lsum, 1)
                            nc.vector.tensor_tensor_reduce(lamp[:], lam[0:1, 2 * j, :], lam[0:1, 2 * j + 1, :], 1.0, 0.0, ALU.mult, ALU.add,
                                                           lams[0:1, j:j + 1]).then_inc(s_lsum, 1)
                        dve.wait_ge(s_vecT, 1)
                        nc.vector.tensor_copy(vec[:], psM[:, 0, 0:V_N]).then_inc(s_vec, 1)
                        dve.wait_ge(s_cps, 1)
                        nc.vector.tensor_copy(cT[:].rearrange("p k c -> p (k c)"), psM[:, 1, 0:KC * NC]).then_inc(s_cT, 1)
                    dve.wait_ge(s_xps, u + 1)
                    t, half = u // 2, u % 2
                    n = P if t < NT else TS
                    nc.vector.tensor_copy(xT[:, 4 * half:4 * half + 4, t * P:t * P + n],
                                          psT[:, u % 2, :].rearrange("p (q t) -> p q t", q=4)[:, :, 0:n]).then_inc(s_xev, 1)
                lam_init = 0.8 - 0.6 * float(np.exp(-0.3))
                dve.wait_ge(s_lexp, 1)
                nc.vector.tensor_tensor(K["nlam"][:], lame[:, 1:2], lame[:, 0:1], ALU.subtract).then_inc(s_lam2, 1)
                dve.wait_ge(s_lam2, 1)
                nc.vector.tensor_scalar(K["nlam"][:], K["nlam"][:], -lam_init, None, ALU.add)
                for k in range(1, KC):
                    norm.dve_add(dve, k, k % 2, k == 1)
                dve.wait_ge(s_vec, 1)
                dve.sem_inc(s_mev, 2)

                def modulations(i):
                    for b in range(2):
                        dve.wait_ge(s_wfree, i * 4 + 2 * b + 6)
                        nc.vector.tensor_copy(mrow[:, b, :], psM[0:NC, b, :]).then_inc(s_mrow, 1)
                    for b in range(2):
                        dve.wait_ge(s_mT, 2 * i + b + 1)
                        at = i * 8 + 4 * b
                        nc.vector.tensor_tensor(mod[:, bass.ds(at, 4), :], psT[:, b, 0:4 * NC].rearrange("p (m c) -> p m c", c=NC),
                                                bcast(vec[:, bass.ds(at, 4)].unsqueeze(2), P, 4, NC), ALU.add).then_inc(s_mev, 1)

                modulations(0)
                dve.wait_ge(s_out, 16)
                norm.dve_rstd(dve)
                modulations(1)
                dve.wait_ge(s_mev, 2 + 4)
                nc.vector.scalar_tensor_tensor(mod[:, M_A + 8:M_A + 16, :], mod[:, M_A + 8:M_A + 16, :], 1.0,
                                               bcast(vec[:, V_NORM_A:V_NORM_A + 8].unsqueeze(2), P, 8, NC), ALU.add, ALU.mult).then_inc(s_scl, 1)
                dve.wait_ge(s_scl, 1)
                norm.dve_samples(dve, tmp)

                def low(k):
                    if k == 0:
                        dve.wait_ge(norm.s_mul, 4)
                    dve.wait_ge(s_hi, k + 1)
                    nc.vector.tensor_tensor(K["Hl"][:, k, :], xT[:, k, :], K["Hh"][:, k, :], ALU.subtract).then_inc(s_lo, 1)

                for k in range(KC - 2):
                    low(k)
                modulations(2)
                for k in range(KC - 2, KC):
                    low(k)


def gla(nc, A, OUT, SCR, K):
    MODS, MS = 10, 2
    with ExitStack() as c:
        sem = lambda n: K["sem"]("gl_" + n)
        tile = lambda n, s: c.enter_context(nc.sbuf_tensor("gl_" + n, s, F32))
        psP = c.enter_context(nc.psum_tensor("gl_psP", [P, 2, 512], F32))
        psL = c.enter_context(nc.psum_tensor("gl_psL", [P, 4, 512], F32))
        psO = c.enter_context(nc.psum_tensor("gl_psO", [P, 512], F32))
        psK = c.enter_context(nc.psum_tensor("gl_psK", [P, 512], F32))
        part = lambda n, s: c.enter_context(nc.sbuf_tensor("gl_" + n, s, F32R))
        raw, wh, wl = [K["w0"], K["w1"]], part("w_high", [P, 2, KC, P]), part("w_low", [P, 2, KC, P])
        wlow, lowh, lowl = K["wlow"], part("wlow_high", [P, KC, RANK]), part("wlow_low", [P, KC, RANK])
        Q_TILE, K_TILE, Z_TILE, V_TILE, TILES = 0, 1, 2, 4, 6
        SPLITS = KC + 1
        wg2 = tile("wg2", [RANK, DK])
        low = tile("low", [RANK, T])
        masks = tile("masks", [P, NL + 1, P])
        smasks = tile("smasks", [TS, 3, TS])
        restart = tile("restart", [P, T])
        rowsel = tile("rowsel", [TS, SB])
        qT, kT, gk, ec = (tile(n, [P, T]) for n in ("qT", "kT", "gk", "ec"))
        cum = K["B2"][:, NL, :]
        zs = tile("zs", [P, 2, T])
        v = tile("v", [P, NT + 1, DV])
        khT = tile("khT", [P, NT + 1, P])
        tmp = tile("tmp", [P, NL + 1, P])
        th = tmp[:].rearrange("p l t -> p (l t)")[:, 0:2 * THIRD].rearrange("p (a t) -> p a t", a=2)
        khm = tmp[0:TS, :, :]
        Am = tile("Am", [P, 2, P])
        As = tile("As", [TS, TS])
        state = tile("state", [P, 2, DV])
        wm = tile("wm", [P, MS, KC, P])
        sst = tile("sst", [P, SB, DV])
        dec = tile("dec", [P, NT + SB])
        one = tile("one", [P, 1])
        mod = K["mod"]
        X = K["B2"]
        Gs, osq, ors = X[:, 0:2, :], X[:, 2:4, :], X[:, 4, :]
        Hh, Hl, ident, ones, vec = K["Hh"], K["Hl"], K["ident"], K["ones"], K["vec"]

        passed = {n: K["sem"]("passed_" + n) for n in ("act", "pool", "sp")}
        s_const, s_g2in, s_low_in, s_set = sem("const_in"), sem("w_g2_in"), sem("low_in"), K["sem"]("su_eps_set")
        s_w = [sem(f"w_in{b}") for b in range(2)]
        s_hi, s_lo = sem("high"), sem("low")
        s_sin, s_sout, s_pout = sem("sstate_in"), sem("sstate_out"), sem("pstate_out")
        s_lowps, s_low = sem("low_summed"), sem("low_ready")
        s_proj, s_pfree = sem("proj_summed"), sem("proj_bank_free")
        s_v = sem("v_ready")
        s_zs = sem("z_ready")
        s_gm, s_ge, s_gl, s_lg, s_cum = sem("g_min"), sem("g_exp"), sem("g_log"), sem("logg"), sem("cum_ready")
        s_d, s_e, s_x = sem("level_diff"), sem("level_exp"), sem("level_ready")
        s_ece, s_dec, s_qh = sem("exp_cum"), sem("decay_kept"), sem("qhat_ready")
        s_kd, s_ke, s_kh = sem("khat_diff"), sem("khat_exp"), sem("khat_ready")
        s_kps, s_kT, s_khm = sem("khat_turned"), sem("khT_ready"), sem("khat_masked")
        s_lv, s_lm, s_A = sem("levels_summed"), sem("levels_masked"), sem("scores_ready")
        s_o, s_oev, s_up, s_st = sem("out_summed"), sem("out_copied"), sem("update_summed"), sem("state_ready")
        s_ups, s_sst = sem("supdate_summed"), sem("sstate_ready")
        s_osq, s_oss, s_oln, s_ors, s_g1, s_g2 = (sem("o_squares"), sem("o_sums"), sem("o_log"), sem("o_rstd"),
                                                   sem("o_normed"), sem("o_gated"))
        s_wm = [sem(f"w_mod_in{b}") for b in range(MS)]
        wkv, wb = A["ada_w_kv"].rearrange("(k p) n -> p k n", p=P), A["ada_w_b"].rearrange("(k p) n -> p k n", p=P)

        def mod_tile(i, n):
            return i * 4 + (M_KV + n) if n < 4 else i * 6 + (M_B + n - 4)

        win = A["w_in_a"].rearrange("(k p) n -> p k n", p=P)
        CH = NT + 1
        V_UNITS = {(0, 2): 17, (2, 4): 18, (4, 5): 19, (5, 6): 20, (6, 7): 22, (7, 8): 24, (8, 9): 26}
        M_UNITS = [15, 16, 21, 23, 25, 27, 28, 29, 30, 31]
        M_CHUNK = [[], [2], [3], [4], [5], [6], [7], [], [8, 9]]
        UNITS = 32
        lvl = lambda ap, L: ap.rearrange("p (n a l) -> p n a l", a=2, l=L)

        def over_heads(eng, head):
            with eng.Fori(0, HA - 1) as i:
                head(i, False)
            head(HA - 1, True)

        with nc.Block() as block:
            @block.sync
            def _(sp):
                for dst, name in ((masks, "masks"), (smasks, "smasks"), (restart, "restart"), (rowsel, "rowsel")):
                    sp.dma_start(dst[:], A[name]).then_inc(s_const, 16)

                def head(i, last):
                    sp.dma_start(sst[:], A["state_gla"][:, bass.ds(i, 1), :, :].rearrange("b h k v -> k (b h) v")).then_inc(s_sin, 16)
                    sp.wait_ge(s_st, 8 * i + 8)
                    sp.dma_start(OUT["state_p"][bass.ds(i, 1), :, :].rearrange("h k v -> k (h v)"), state[:, (NT - 1) % 2, :]).then_inc(s_pout, 16)
                    sp.wait_ge(s_sst, 8 * i + 8)
                    sp.dma_start(OUT["state_s"][:, bass.ds(i, 1), :, :].rearrange("b h k v -> k (b h) v"), sst[:]).then_inc(s_sout, 16)
                    sp.wait_ge(s_sout, 16 * (i + 1))
                    if last:
                        return
                    sp.wait_ge(s_g2, 2 * i + 4)
                    apart(sp, passed["sp"])
                    sp.dma_start(SCR["G"].rearrange("(k p) t -> p k t", p=P)[:, bass.ds(2 * i, 2), :], Gs).then_inc(s_pout, 16)

                over_heads(sp, head)
                for b in range(2):
                    sp.wait_ge(s_lo, SPLITS + TILES * HA)
                    sp.dma_start(K[f"w{b}"][:], A["w_out_a"].rearrange("(k p) n -> p k n", p=P)[:, :, b * P:(b + 1) * P]).then_inc(
                        K["sem"](f"op_w_in{b}"), 16)
                sp.wait_ge(s_pout, 32 * HA - 16)

            @block.gpsimd
            def _(pool):
                nc.gpsimd.memset(one[:], 1.0).then_inc(s_set, 1)

                def load(i, n):
                    pool.wait_ge(s_lo, TILES * i + (SPLITS + n - 1))
                    apart(pool, passed["pool"])
                    first, step = ((0, P), (512, P), (2048, DV), (2048 + P, DV), (1024, DV), (1024 + P, DV))[n]
                    pool.dma_start(raw[n % 2][:], win[:, :, bass.ds(i * step + first, P)]).then_inc(s_w[n % 2], 16)

                def load_g2(i):
                    pool.wait_ge(s_proj, i * UNITS + 9)
                    apart(pool, passed["pool"])
                    pool.dma_start(wg2[:], A["w_g2_a"][:, bass.ds(i * DK, DK)]).then_inc(s_g2in, 16)

                def head(i, last):
                    for n in range(Z_TILE, TILES):
                        load(i, n)
                    for n in range(MODS):
                        pool.wait_ge(s_proj, i * UNITS + (UNITS + M_UNITS[n - MS] if n >= MS else M_UNITS[n - MS]) + 1)
                        apart(pool, passed["pool"])
                        src = wkv[:, :, bass.ds(i * 4 * P + n * P, P)] if n < 4 else wb[:, :, bass.ds(i * 6 * P + (n - 4) * P, P)]
                        pool.dma_start(wm[:, n % MS], src).then_inc(s_wm[n % MS], 16)
                        if n == 3 and not last:
                            load(i + 1, Q_TILE)
                            load(i + 1, K_TILE)
                            load_g2(i + 1)

                load_g2(0)
                over_heads(pool, head)

            @block.tensor
            def _(pe):
                def products(out, stationary, moving):
                    for k in range(KC):
                        for n, (a, b) in enumerate(((0, 0), (0, 1), (1, 0))):
                            mm = nc.tensor.matmul(out, stationary(a, k), moving(b, k), start=(k == 0 and n == 0), stop=(k == KC - 1 and n == 2))
                    return mm

                H, W = (Hh, Hl), (wh, wl)
                pe.wait_ge(s_lo, SPLITS)
                for j in range(3):
                    mm = products(psL[0:RANK, j, 0:THIRD], lambda a, k: (lowh, lowl)[a][:, k, :], lambda b, k: thirds(H[b][:, k, :])[j])
                mm.then_inc(s_lowps, 1)
                pe.wait_ge(s_low, 1)
                pe.sem_inc(s_proj, UNITS)

                def bank(i, unit):
                    pe.wait_ge(s_pfree, i * UNITS + unit + 1)
                    return unit % 2

                def weights(i, n):
                    pe.wait_ge(s_lo, TILES * i + (SPLITS + n + 1))

                def project(i, unit, n):
                    mm = products(psP[:, bank(i, unit), 0:THIRD], lambda a, k: W[a][:, n % 2, k, :], lambda b, k: thirds(H[b][:, k, :])[unit % 3])
                    mm.then_inc(s_proj, 1)

                def head(i, last):
                    def project_v(lo, hi):
                        b = bank(i, V_UNITS[(lo, hi)])
                        for t in range(lo, hi):
                            n = P if t < NT else TS
                            mm = products(psP[0:n, b, (t - lo) * DV:(t - lo + 1) * DV], lambda a, k: H[a][:, k, t * P:t * P + n],
                                          lambda b, k: W[b][:, :, k, :])
                        mm.then_inc(s_proj, 1)

                    def turn_keys(r):
                        pe.wait_ge(s_kh, i + 1)
                        if r:
                            pe.wait_ge(s_kT, 3 * i + r)
                        for t in range(4 * r, min(4 * r + 4, CH)):
                            n = P if t < NT else TS
                            mm = nc.tensor.transpose(psK[0:n, (t % 4) * P:(t % 4) * P + P], gk[:, t * P:t * P + n], ident[:])
                        mm.then_inc(s_kps, 1)

                    def levels(t):
                        if t >= 2:
                            pe.wait_ge(s_lm, CH * i + t - 1)
                        elif t == 0:
                            pe.wait_ge(s_ors, i + 1)
                        lo, n = t * P, (P if t < NT else TS)
                        todo = [(X[:, L, lo:lo + n],) * 2 for L in (range(NL) if t < NT else SLEV)] + [(kT[:, lo:lo + n], qT[:, lo:lo + n])]
                        for r, (a, b) in enumerate(todo):
                            f = r * n
                            mm = nc.tensor.matmul(psL[0:n, 2 * (t % 2) + f // 512, f % 512:f % 512 + n], a, b, start=True, stop=True)
                        mm.then_inc(s_lv, 1)

                    def output(t):
                        pe.wait_ge(s_A, CH * i + t + 1)
                        if t:
                            pe.wait_ge(s_oev, CH * i + t)
                            if t < NT:
                                pe.wait_ge(s_st, 8 * i + t)
                        for half in range(2):
                            cols = slice(half * DK, (half + 1) * DK)
                            mm = nc.tensor.matmul(psO[:, half * P:(half + 1) * P], v[:, t, cols], Am[:, t % 2, :], start=True, stop=(t == 0))
                            if t:
                                mm = nc.tensor.matmul(psO[:, half * P:(half + 1) * P], state[:, (t - 1) % 2, cols], ec[:, t * P:(t + 1) * P], start=False, stop=True)
                        mm.then_inc(s_o, 1)

                    def update(t):
                        if t == 0:
                            pe.wait_ge(s_kT, 3 * i + 3)
                        else:
                            pe.wait_ge(s_st, 8 * i + t)
                        nc.tensor.matmul(psK[:, 0:DV], khT[:, t, :], v[:, t, :], start=True, stop=True).then_inc(s_up, 1)

                    def modulate(n):
                        pe.wait_ge(s_wm[n % MS], 16 * (MODS // MS * i + n // MS + 1))
                        b = bank(i, M_UNITS[n])
                        for k in range(KC):
                            mm = nc.tensor.matmul(psP[:, b, 0:NC], wm[:, n % MS, k, :], K["cT"][:, k, :], start=(k == 0), stop=(k == KC - 1))
                        mm.then_inc(s_proj, 1)

                    weights(i, K_TILE)
                    for j in range(3):
                        project(i, 3 + j, K_TILE)
                    pe.wait_ge(s_g2in, 16 * (i + 1))
                    for j in range(3):
                        b = bank(i, 6 + j)
                        nc.tensor.matmul(psP[:, b, 0:THIRD], wg2[:], thirds(low[:])[j], start=True, stop=True).then_inc(s_proj, 1)
                    for u in range(6):
                        if u % 3 == 0:
                            weights(i, Z_TILE + u // 3)
                        project(i, 9 + u, Z_TILE + u // 3)
                    modulate(0)
                    modulate(1)
                    weights(i, V_TILE + 1)
                    project_v(0, 2)
                    project_v(2, 4)
                    pe.wait_ge(s_x, i + 1)
                    levels(0)
                    turn_keys(0)
                    project_v(4, 5)
                    turn_keys(1)
                    levels(1)
                    turn_keys(2)
                    pe.wait_ge(s_v, 7 * i + 1)
                    update(0)
                    for t in range(NT):
                        if t:
                            levels(t + 1)
                            if t < 5:
                                project_v(t + 4, t + 5)
                        output(t)
                        for n in M_CHUNK[t]:
                            modulate(n)
                        if t + 1 < NT:
                            pe.wait_ge(s_v, 7 * i + (1, 1, 2, 2, 3, 4, 5, 6)[t + 1])
                            update(t + 1)
                    pe.wait_ge(s_A, CH * i + CH)
                    pe.wait_ge(s_oev, CH * i + NT)
                    pe.wait_ge(s_v, 7 * i + 7)
                    pe.wait_ge(s_sin, 16 * (i + 1))
                    for half in range(2):
                        cols = slice(half * DK, (half + 1) * DK)
                        for b in range(SB):
                            at = half * TS + b * SL
                            nc.tensor.matmul(psO[:, at:at + SL], sst[:, b, cols], ec[:, TP + b * SL:TP + (b + 1) * SL], start=(b == 0), stop=False)
                        mm = nc.tensor.matmul(psO[:, half * TS:(half + 1) * TS], v[0:TS, NT, cols], As[:], start=False, stop=True)
                    mm.then_inc(s_o, 1)
                    modulate(NT)
                    pe.wait_ge(s_khm, i + 1)
                    pe.wait_ge(s_lm, CH * i + CH)
                    for b in range(SB):
                        mm = nc.tensor.matmul(psL[:, b // 2, (b % 2) * DV:(b % 2 + 1) * DV], khm[:, b, :], v[0:TS, NT, :], start=True, stop=True)
                    mm.then_inc(s_ups, 1)
                    modulate(NT + 1)
                    if not last:
                        weights(i + 1, Q_TILE)
                        project(i + 1, 0, Q_TILE)
                    pe.wait_ge(s_osq, i + 1)
                    pe.wait_ge(s_sst, 8 * (i + 1))
                    for j in range(3):
                        for half in range(2):
                            mm = nc.tensor.matmul(psL[:, j, 0:THIRD], ones[:], thirds(osq[:, half, :])[j], start=(half == 0), stop=(half == 1))
                    mm.then_inc(s_oss, 1)
                    pe.wait_ge(s_st, 8 * (i + 1))
                    if not last:
                        project(i + 1, 1, Q_TILE)
                        project(i + 1, 2, Q_TILE)

                weights(0, Q_TILE)
                for unit in range(3):
                    project(0, unit, Q_TILE)
                over_heads(pe, head)

            @block.scalar
            def _(act):
                A_ = nc.scalar.activation
                def high(i, n, unit):
                    act.wait_ge(s_w[n % 2], i * 48 + 16 * (n // 2 + 1))
                    if unit is not None:
                        act.wait_ge(s_proj, (i + 1) * UNITS + (unit + 1))
                        apart(act, passed["act"])
                    A_(wh[:, n % 2], raw[n % 2][:], ACT.Copy).then_inc(s_hi, 1)

                act.wait_ge(s_low_in, 16)
                A_(lowh[:], wlow[:], ACT.Copy).then_inc(s_hi, 1)
                high(0, Q_TILE, None)
                high(0, K_TILE, None)
                act.wait_ge(s_lowps, 1)
                A_(low[:].rearrange("p (j t) -> p j t", j=3), psL[0:RANK, 0:3, 0:THIRD], ACT.Copy).then_inc(s_low, 1)
                act.wait_ge(s_set, 2)
                act.sem_inc(s_pfree, 2)
                act.sem_inc(s_ors, 1)

                def done(i, unit):
                    act.wait_ge(s_proj, (i + 1) * UNITS + unit + 1)
                    return unit % 2

                def copy_q(i, unit):
                    A_(thirds(qT[:])[unit], psP[:, done(i, unit), 0:THIRD], ACT.Copy, scale=DK ** -0.5).then_inc(s_pfree, 1)

                def head(i, last):
                    def copy_v(lo, hi):
                        b = done(i, V_UNITS[(lo, hi)])
                        n = P if lo < NT else TS
                        A_(v[0:n, lo:hi, :].rearrange("p a d -> p (a d)"), psP[0:n, b, 0:(hi - lo) * DV], ACT.Copy).then_inc(s_v, 1)
                        act.wait_ge(s_v, 7 * i + list(V_UNITS).index((lo, hi)) + 1)
                        act.sem_inc(s_pfree, 1)

                    def modulation(n):
                        b = done(i, M_UNITS[n])
                        apart(act, passed["act"])
                        A_(mod[:, bass.ds(mod_tile(i, n), 1), :].rearrange("p a c -> p (a c)"), psP[:, b, 0:NC], ACT.Identity,
                           bias=vec[:, bass.ds(mod_tile(i, n), 1)]).then_inc(s_pfree, 1)

                    def copy_keys(r):
                        act.wait_ge(s_kps, 3 * i + r + 1)
                        if r < 2:
                            A_(khT[:, 4 * r:4 * r + 4, :].rearrange("p a d -> p (a d)"), psK[:], ACT.Copy).then_inc(s_kT, 1)
                        else:
                            A_(khT[0:TS, NT, :], psK[0:TS, 0:P], ACT.Copy).then_inc(s_kT, 1)

                    high(i, Z_TILE, 2)
                    for j in range(3):
                        A_(thirds(kT[:])[j], psP[:, done(i, 3 + j), 0:THIRD], ACT.Copy).then_inc(s_pfree, 1)
                    high(i, Z_TILE + 1, 5)
                    for j in range(3):
                        b = done(i, 6 + j)
                        apart(act, passed["act"])
                        A_(thirds(gk[:])[j], psP[:, b, 0:THIRD], ACT.Identity, bias=vec[:, bass.ds(i + V_BG, 1)])
                        A_(thirds(ec[:])[j], psP[:, b, 0:THIRD], ACT.Abs, bias=vec[:, bass.ds(i + V_BG, 1)]).then_inc(s_pfree, 1)
                    act.wait_ge(s_pfree, i * UNITS + 2 + 9)
                    A_(ec[:], ec[:], ACT.Exp, scale=-1.0).then_inc(s_ge, 1)
                    act.wait_ge(s_ge, i + 1)
                    A_(ec[:], ec[:], ACT.Ln, bias=one[:, 0:1]).then_inc(s_gl, 1)
                    act.wait_ge(s_g2, 2 * i + 2)
                    for m in range(2):
                        for j in range(3):
                            u = 3 * m + j
                            b = done(i, 9 + u)
                            if u >= 2:
                                act.wait_ge(s_zs, 6 * i + u - 1)
                            A_(thirds(zs[:, m, :])[j], psP[:, b, 0:THIRD], ACT.Copy, scale=0.5)
                            A_(th[:, u % 2, :], psP[:, b, 0:THIRD], ACT.Tanh, scale=0.5).then_inc(s_pfree, 1)
                        high(i, V_TILE + m, 11 + 3 * m)
                    modulation(0)
                    modulation(1)
                    act.wait_ge(s_cum, i + 1)
                    A_(ec[:], cum, ACT.Exp).then_inc(s_ece, 1)
                    for L in range(NL):
                        act.wait_ge(s_d, NL * i + L + 1)
                        n = T if L in SLEV else TP
                        A_(X[:, L, 0:n], X[:, L, 0:n], ACT.Exp).then_inc(s_e, 1)
                    act.wait_ge(s_kd, i + 1)
                    A_(gk[:], gk[:], ACT.Exp).then_inc(s_ke, 1)
                    copy_v(0, 2)
                    copy_v(2, 4)
                    copy_keys(0)
                    copy_v(4, 5)
                    copy_keys(1)
                    copy_keys(2)
                    for t in range(CH):
                        if 1 <= t < 5:
                            copy_v(t + 4, t + 5)
                        act.wait_ge(s_o, CH * i + t + 1)
                        n = P if t < NT else TS
                        apart(act, passed["act"])
                        A_(Gs[:, :, t * P:t * P + n], psO[:, 0:2 * n].rearrange("p (a t) -> p a t", a=2), ACT.Copy).then_inc(s_oev, 1)
                        for m in M_CHUNK[t]:
                            modulation(m)
                        if t == 5 and not last:
                            high(i + 1, Q_TILE, V_UNITS[(8, 9)] - UNITS)
                    act.wait_ge(s_oev, CH * (i + 1))
                    act.wait_ge(s_lv, CH * (i + 1))
                    apart(act, passed["act"])
                    A_(osq, Gs, ACT.Square).then_inc(s_osq, 1)
                    if not last:
                        high(i + 1, K_TILE, V_UNITS[(8, 9)] - UNITS)
                        copy_q(i + 1, 0)
                    act.wait_ge(s_oss, i + 1)
                    A_(ors.rearrange("p (j t) -> p j t", j=3), psL[:, 0:3, 0:THIRD], ACT.Ln, scale=1.0 / DV, bias=K["eps"][:, 0:1]).then_inc(s_oln, 1)
                    act.wait_ge(s_oln, i + 1)
                    A_(ors, ors, ACT.Exp, scale=-0.5).then_inc(s_ors, 1)
                    if not last:
                        copy_q(i + 1, 1)
                        copy_q(i + 1, 2)

                for unit in range(3):
                    copy_q(0, unit)
                over_heads(act, head)

            @block.vector
            def _(dve):
                V = nc.vector
                def low_part(i, n):
                    dve.wait_ge(s_hi, TILES * i + (SPLITS + n + 1))
                    V.tensor_tensor(wl[:, n % 2], raw[n % 2][:], wh[:, n % 2], ALU.subtract).then_inc(s_lo, 1)

                dve.wait_ge(s_hi, SPLITS)
                V.tensor_tensor(lowl[:], wlow[:], lowh[:], ALU.subtract).then_inc(s_lo, 1)
                low_part(0, Q_TILE)
                low_part(0, K_TILE)
                dve.wait_ge(s_const, 16 * 4)
                dve.sem_inc(s_g2, 2)

                def head(i, final):
                    low_part(i, Z_TILE)
                    low_part(i, Z_TILE + 1)
                    dve.wait_ge(s_pfree, i * UNITS + 2 + 9)
                    V.tensor_scalar(gk[:], gk[:], 0.0, None, ALU.min).then_inc(s_gm, 1)
                    dve.wait_ge(s_gm, i + 1)
                    dve.wait_ge(s_gl, i + 1)
                    V.tensor_tensor(gk[:], gk[:], ec[:], ALU.subtract).then_inc(s_lg, 1)
                    dve.wait_ge(s_lg, 2 * i + 1)
                    V.tensor_scalar(gk[:], gk[:], 1.0 / 16.0, None, ALU.mult).then_inc(s_lg, 1)
                    dve.wait_ge(s_lg, 2 * i + 2)
                    V.tensor_tensor_scan(cum, restart[:], gk[:], 0.0, ALU.mult, ALU.add).then_inc(s_cum, 1)
                    dve.wait_ge(s_cum, i + 1)

                    def zgate(u):
                        dve.wait_ge(s_pfree, i * UNITS + 2 + 9 + u + 1)
                        dst = thirds(zs[:, u // 3, :])[u % 3]
                        V.scalar_tensor_tensor(dst, th[:, u % 2, :], 1.0, dst, ALU.add, ALU.mult).then_inc(s_zs, 1)

                    for L, size in enumerate(LEVELS):
                        parts = [(0, TP)] + ([(TP, T)] if L in SLEV else [])
                        for a, b in parts:
                            src, dst = lvl(cum[:, a:b], size), lvl(X[:, L, a:b], size)
                            m = src.shape[1]
                            ref = bcast(src[:, :, 0, size - 1:size], P, m, size)
                            V.tensor_tensor(dst[:, :, 0, :], ref, src[:, :, 0, :], ALU.subtract)
                            last = V.tensor_tensor(dst[:, :, 1, :], src[:, :, 1, :], ref, ALU.subtract)
                        last.then_inc(s_d, 1)
                        if L < 6:
                            zgate(L)
                        if L in (2, 5):
                            low_part(i, V_TILE + L // 3)
                    for a, b, size in ((0, TP, P), (TP, T, SL)):
                        src = cum[:, a:b].rearrange("p (n t) -> p n t", t=size)
                        last = V.tensor_tensor(gk[:, a:b].rearrange("p (n t) -> p n t", t=size), bcast(src[:, :, size - 1:size], P, (b - a) // size, size),
                                               src, ALU.subtract)
                    last.then_inc(s_kd, 1)
                    dve.wait_ge(s_ece, i + 1)
                    V.tensor_copy(dec[:, 0:NT], ec[:, P - 1:TP:P])
                    V.tensor_copy(dec[:, NT:NT + SB], ec[:, TP + SL - 1:T:SL]).then_inc(s_dec, 1)
                    dve.wait_ge(s_dec, i + 1)
                    V.tensor_tensor(ec[:], ec[:], qT[:], ALU.mult).then_inc(s_qh, 1)
                    for L, size in enumerate(LEVELS):
                        dve.wait_ge(s_e, NL * i + L + 1)
                        for a, b in [(0, TP)] + ([(TP, T)] if L in SLEV else []):
                            dst = lvl(X[:, L, a:b], size)
                            V.tensor_tensor(dst[:, :, 0, :], dst[:, :, 0, :], lvl(kT[:, a:b], size)[:, :, 0, :], ALU.mult)
                            last = V.tensor_tensor(dst[:, :, 1, :], dst[:, :, 1, :], lvl(qT[:, a:b], size)[:, :, 1, :], ALU.mult)
                    last.then_inc(s_x, 1)
                    dve.wait_ge(s_ke, i + 1)
                    V.tensor_tensor(gk[:], gk[:], kT[:], ALU.mult).then_inc(s_kh, 1)
                    for t in range(NT):
                        dve.wait_ge(s_lv, CH * i + t + 1)
                        if t:
                            dve.wait_ge(s_A, CH * i + t)
                        V.tensor_tensor(tmp[:].rearrange("p l t -> p (l t)"), psL[:, 2 * (t % 2):2 * (t % 2) + 2, :].rearrange("p a t -> p (a t)"),
                                        masks[:].rearrange("p l t -> p (l t)"), ALU.mult).then_inc(s_lm, 1)
                        dve.wait_ge(s_lm, CH * i + t + 1)
                        if t >= 2:
                            dve.wait_ge(s_o, CH * i + t - 1)
                        V.tensor_reduce(Am[:, t % 2, :], tmp[:].rearrange("p l t -> p t l"), AX.X, ALU.add).then_inc(s_A, 1)
                        dve.wait_ge(s_up, NT * i + t + 1)
                        if t == 0:
                            V.tensor_copy(state[:, 0, :], psK[:, 0:DV]).then_inc(s_st, 1)
                        else:
                            dve.wait_ge(s_o, CH * i + t)
                            dve.wait_ge(s_st, 8 * i + t)
                            V.scalar_tensor_tensor(state[:, t % 2, :], state[:, (t - 1) % 2, :], dec[:, t:t + 1], psK[:, 0:DV], ALU.mult, ALU.add).then_inc(s_st, 1)
                        if t == 5 and not final:
                            low_part(i + 1, Q_TILE)
                    dve.wait_ge(s_lv, CH * i + CH)
                    dve.wait_ge(s_A, CH * i + NT)
                    V.tensor_tensor(tmp[0:TS, 0:3, 0:TS], psL[0:TS, 0, 0:3 * TS].rearrange("p (l t) -> p l t", l=3), smasks[:], ALU.mult).then_inc(s_lm, 1)
                    dve.wait_ge(s_lm, CH * i + CH)
                    V.tensor_reduce(As[:], tmp[0:TS, 0:3, 0:TS].rearrange("p l t -> p t l"), AX.X, ALU.add).then_inc(s_A, 1)
                    dve.wait_ge(s_kT, 3 * i + 3)
                    dve.wait_ge(s_A, CH * (i + 1))
                    V.tensor_tensor(khm, bcast(khT[0:TS, NT, :].unsqueeze(1), TS, SB, P), bcast(rowsel[:].unsqueeze(2), TS, SB, P), ALU.mult).then_inc(s_khm, 1)
                    dve.wait_ge(s_ups, i + 1)
                    for b in range(SB):
                        V.scalar_tensor_tensor(sst[:, b, :], sst[:, b, :], dec[:, NT + b:NT + b + 1], psL[:, b // 2, (b % 2) * DV:(b % 2 + 1) * DV],
                                               ALU.mult, ALU.add).then_inc(s_sst, 1)
                    if not final:
                        low_part(i + 1, K_TILE)
                    dve.wait_ge(s_ors, i + 2)
                    for half in range(2):
                        o = Gs[:, half, :]
                        V.scalar_tensor_tensor(o, o, vec[:, V_ONORM + half:V_ONORM + half + 1], ors, ALU.mult, ALU.mult).then_inc(s_g1, 1)
                        dve.wait_ge(s_g1, 2 * i + half + 1)
                        dve.wait_ge(s_zs, 6 * i + 6)
                        V.tensor_tensor(o, o, zs[:, half, :], ALU.mult).then_inc(s_g2, 1)
                    dve.wait_ge(s_pout, 32 * (i + 1) - (16 if final else 0))
                    dve.wait_ge(s_g2, 2 * (i + 1) + 2)

                over_heads(dve, head)


def out_proj(nc, W, resid, keep, dst, gate, K, use, norm=None, Gin=None, OUT=None):
    with ExitStack() as c:
        sem = lambda n: K["sem"]("op_" + n)
        ps = c.enter_context(nc.psum_tensor(f"op{use}_ps", [P, 2, 512], F32))
        w = [K["w0"], K["w1"]]
        part = lambda n, s: c.enter_context(nc.sbuf_tensor(f"op{use}_{n}", s, F32R))
        wh, wl = part("w_high", [P, 2, KC, P]), part("w_low", [P, 2, KC, P])
        Gh, Gl = part("G_high", [P, KC, T]), part("G_low", [P, KC, T])
        x = K[("B1", "B2")[use]][:, 0:2, :]
        sg = c.enter_context(nc.sbuf_tensor(f"op{use}_sg", [P, 2, TS], F32))
        s_w = [sem(f"w_in{b}") for b in range(2)]
        s_x = [sem(f"x_in{b}") for b in range(2)]
        s_mm, s_free, s_sg, s_out, s_kept = sem("summed"), sem("added"), sem("sample_gated"), sem("tile_ready"), sem("kept")
        G, mod, ident = K["G"], K["mod"], K["ident"]
        LEFT = KC if Gin is None else KC - 2
        source = lambda k: G[:, k, :] if k < LEFT else dst[:, k - LEFT, :]
        s_hi, s_lo, s_gin = sem("high_ready"), sem("low_ready"), sem("G_in")
        if OUT is not None:
            psY = c.enter_context(nc.psum_tensor("op_psY", [P, 3, 512], F32))
            ys = c.enter_context(nc.sbuf_tensor("op_ys", [P, 2, NT + 1, P], F32))
            s_turned, s_y, s_yout = sem("y_turned"), sem("y_copied"), [sem(f"y_out{b}") for b in range(2)]
        GROUPS = [(r, min(r + 4, NT + 1)) for r in range(0, NT + 1, 4)]
        base = use * (3 * KC + KC)
        third_split = lambda j: base + (1 + KC, 2 + 2 * KC, 2 + 3 * KC)[j]
        tile_split = lambda m: m + (base + 2 + 3 * KC - 1)

        def splits(weights, third):
            weights(0)
            for j in range(3):
                for k in range(KC):
                    third(j, k)
                if j == 0:
                    weights(1)
        wd = W.rearrange("(k p) n -> p k n", p=P)

        with nc.Block() as block:
            @block.sync
            def _(sp):
                if use == 0:
                    sp.dma_start(G[:, 0:LEFT, 0:THIRD], Gin[:, 0:LEFT, 0:THIRD]).then_inc(s_kept, 16)
                    sp.dma_start(G[:, 0:LEFT, THIRD:T], Gin[:, 0:LEFT, THIRD:T]).then_inc(s_gin, 16)
                    sp.sem_inc(s_out, 2)
                for b in range(2):
                    sp.wait_ge(s_out, use * KC + b + 1)
                    sp.dma_start(x[:, b], resid[b * P:(b + 1) * P, :]).then_inc(s_x[b], 16)

                def load(i, split):
                    for b in range(2):
                        sp.wait_ge(s_lo, split(b))
                        sp.dma_start(w[b][:], wd[:, :, bass.ds(i * 2 * P + b * P, P)]).then_inc(s_w[b], 16)
                        sp.wait_ge(s_out, i * 2 + (use * KC + b + 1))
                        sp.dma_start(x[:, b], resid[bass.ds(i * 2 * P + b * P, P), :]).then_inc(s_x[b], 16)

                load(1, lambda b: base + (1, 2 + KC)[b])
                with sp.Fori(2, KC // 2) as i:
                    load(i, lambda b: tile_split(i * 2 + (b - 2)))
                if keep is not None:
                    with sp.Fori(0, KC) as m:
                        sp.wait_ge(s_out, m + 3)
                        sp.dma_start(keep[bass.ds(m * P, P), :], dst[:, bass.ds(m, 1), :].rearrange("p a t -> p (a t)")).then_inc(s_kept, 16)
                    sp.wait_ge(s_kept, 16 * KC + 16)

            @block.tensor
            def _(pe):
                def turn(m, slot, first=False):
                    pe.wait_ge(s_out, m + (use * KC + 3))
                    for r, (lo, hi) in enumerate(GROUPS):
                        if not first:
                            pe.wait_ge(s_y, m * 3 + (r - 2))
                            apart(pe, K["sem"]("passed_pe"))
                        for t in range(lo, hi):
                            n = P if t < NT else TS
                            mm = nc.tensor.transpose(psY[0:n, r, (t - lo) * P:(t - lo + 1) * P], dst[:, slot, t * P:t * P + n], ident[:])
                        mm.then_inc(s_turned, 1)

                def tiles(i, first):
                    s = i + use * KC // 2
                    for b in range(2):
                        if first:
                            pe.wait_ge(s_lo, base + (1, 2 + KC)[b])
                        else:
                            pe.wait_ge(s_lo, tile_split(i * 2 + b))
                        for j in range(3):
                            u = 3 * b + j
                            pe.wait_ge(s_free, s * 6 + u + 1)
                            for k in range(KC):
                                if first and b == 0:
                                    pe.wait_ge(s_lo, third_split(j) - KC + k + 1)
                                for n, (ws, gs) in enumerate(((wh, Gh), (wh, Gl), (wl, Gh))):
                                    mm = nc.tensor.matmul(ps[:, u % 2, 0:THIRD], ws[:, b, k, :], thirds(gs[:, k, :])[j],
                                                          start=(k == 0 and n == 0), stop=(k == KC - 1 and n == 2))
                            mm.then_inc(s_mm, 1)
                        if OUT is not None and not (first and b == 0):
                            turn(i * 2 + (b - 1), 1 - b, first)

                tiles(0, True)
                with pe.Fori(1, KC // 2) as i:
                    tiles(i, False)
                if norm is not None:
                    norm.pe_sum(pe)
                if OUT is not None:
                    turn(KC - 1, 1)

            @block.scalar
            def _(act):
                def weights(m):
                    act.wait_ge(s_w[m % 2], 16 * ((use * KC + m) // 2 + 1))
                    if m >= 2:
                        act.wait_ge(s_mm, 3 * (use * KC + m - 1))
                    nc.scalar.activation(wh[:, m % 2], w[m % 2][:], ACT.Copy).then_inc(s_hi, 1)

                def third(j, k):
                    if Gin is not None and k == 0 and j < 2:
                        act.wait_ge((s_kept, s_gin)[j], 16)
                    nc.scalar.activation(thirds(Gh[:, k, :])[j], thirds(source(k))[j], ACT.Copy).then_inc(s_hi, 1)

                splits(weights, third)

                def store(m):
                    if m >= 2:
                        act.wait_ge(s_yout[m % 2], 32 * (m // 2))
                    for r, (lo, hi) in enumerate(GROUPS):
                        act.wait_ge(s_turned, 3 * m + r + 1)
                        n = P if lo < NT else TS
                        nc.scalar.activation(ys[0:n, m % 2, lo:hi, :].rearrange("p t d -> p (t d)"), psY[0:n, r, 0:(hi - lo) * P],
                                             ACT.Copy).then_inc(s_y, 1)
                    act.wait_ge(s_y, 3 * m + 3)
                    cols = slice(m * P, (m + 1) * P)
                    act.dma_start(OUT["y_p"][:, cols].rearrange("(t p) d -> p t d", p=P), ys[:, m % 2, 0:NT, :]).then_inc(s_yout[m % 2], 16)
                    act.dma_start(OUT["y_s"][:, cols], ys[0:TS, m % 2, NT, :]).then_inc(s_yout[m % 2], 16)

                for m in range(KC):
                    if m + 2 < KC:
                        weights(m + 2)
                    if OUT is not None and m:
                        store(m - 1)
                    if norm is not None:
                        act.wait_ge(s_out, use * KC + 2 + m + 1)
                        norm.act_square(act, m)
                if norm is not None:
                    norm.act_rstd(act)
                if OUT is not None:
                    store(KC - 1)
                    for b in range(2):
                        act.wait_ge(s_yout[b], 16 * KC)

            @block.vector
            def _(dve):
                V = nc.vector
                if use == 0:
                    dve.sem_inc(s_free, 2)

                done = [base]

                def low(dst, src, high):
                    done[0] += 1
                    dve.wait_ge(s_hi, done[0])
                    V.tensor_tensor(dst, src, high, ALU.subtract).then_inc(s_lo, 1)

                splits(lambda m: low(wl[:, m], w[m][:], wh[:, m]),
                       lambda j, k: low(thirds(Gl[:, k, :])[j], thirds(source(k))[j], thirds(Gh[:, k, :])[j]))

                def tiles(i, first, last):
                    s = i + use * KC // 2
                    for b in range(2):
                        if norm is not None and not first:
                            norm.dve_add(dve, i * 2 + b - 1, 1 - b)
                        dve.wait_ge(s_x[b], 16 * (s + 1))
                        gp = mod[:, bass.ds(i * 2 + b + gate, 1), 0:1].rearrange("p a c -> p (a c)")
                        gs = mod[:, bass.ds(i * 2 + b + gate, 1), 1:NC].rearrange("p a c -> p (a c)")
                        if OUT is None:
                            d = dst[:, bass.ds(i * 2 + b, 1), :].rearrange("p a t -> p (a t)")
                        else:
                            d = dst[:, b, :]
                            if not first:
                                dve.wait_ge(s_turned, i * 6 + (3 * b - 3))
                        for j in range(3):
                            u = 3 * b + j
                            dve.wait_ge(s_mm, s * 6 + u + 1)
                            n = THIRD if j < 2 else THIRD - TS
                            lo = THIRD * j
                            if j == 2:
                                V.tensor_tensor(sg[:, b, :].rearrange("p (s t) -> p s t", s=SB),
                                                ps[:, u % 2, n:THIRD].rearrange("p (s t) -> p s t", s=SB),
                                                bcast(gs.unsqueeze(2), P, SB, SL), ALU.mult).then_inc(s_sg, 1)
                            V.scalar_tensor_tensor(d[:, lo:lo + n], ps[:, u % 2, 0:n], gp, x[:, b, lo:lo + n], ALU.mult, ALU.add).then_inc(s_free, 1)
                        dve.wait_ge(s_sg, s * 2 + b + 1)
                        V.tensor_tensor(d[:, TP:T], sg[:, b, :], x[:, b, TP:T], ALU.add).then_inc(s_out, 1)
                        if not last:
                            dve.wait_ge(s_hi, tile_split(i * 2 + (b + 2)))
                            V.tensor_tensor(wl[:, b], w[b][:], wh[:, b], ALU.subtract).then_inc(s_lo, 1)

                tiles(0, True, False)
                with dve.Fori(1, KC // 2 - 1) as i:
                    tiles(i, False, False)
                tiles(KC // 2 - 1, False, True)
                if norm is not None:
                    norm.dve_add(dve, KC - 1, 1)


def normed(nc, A, K, norm, tmp):
    s_scl = K["sem"]("scales_ready")
    with nc.Block() as block:
        @block.gpsimd
        def _(pool):
            for n, (src, name) in enumerate(((A["w_in_b"], "at_w_q_in"), (A["w_k"], "at_w_k_in"))):
                pool.dma_start(K[f"w{n}"][:], src.rearrange("(k p) n -> p k n", p=P)[:, :, 0:P]).then_inc(K["sem"](name), 16)

        @block.scalar
        def _(act):
            act.wait_ge(s_scl, 2)
            norm.act_affine(act, norm.affine[:1], None)

        @block.vector
        def _(dve):
            for col, gain in ((M_KV + 8, V_NORM_KV), (M_B + 8, V_NORM_B)):
                ins = nc.vector.scalar_tensor_tensor(K["mod"][:, col:col + 8, :], K["mod"][:, col:col + 8, :], 1.0,
                                                     bcast(K["vec"][:, gain:gain + 8].unsqueeze(2), P, 8, NC), ALU.add, ALU.mult)
            ins.then_inc(s_scl, 1)
            dve.wait_ge(s_scl, 2)
            norm.dve_rstd(dve)
            norm.dve_samples(dve, tmp)


def attention(nc, A, OUT, K, norm):
    with ExitStack() as c:
        sem = lambda n: K["sem"]("at_" + n)
        tile = lambda n, s, dt=F32: c.enter_context(nc.sbuf_tensor("at_" + n, s, dt))
        psP = c.enter_context(nc.psum_tensor("at_psP", [P, 2, 512], F32))
        psS = c.enter_context(nc.psum_tensor("at_psS", [P, 4, 512], F32))
        psW = c.enter_context(nc.psum_tensor("at_psW", [P, 512], F32))
        psO = c.enter_context(nc.psum_tensor("at_psO", [P, 512], F32))
        w = {"q": K["w0"], "k": K["w1"], "z": tile("w_z", [P, KC, P])}
        w["v"] = w["q"]
        qT, kT, zs, rs = (tile(n, [P, T]) for n in ("qT", "kT", "zs", "rs"))
        v = tile("v", [P, NT + 1, DE])
        ko = tile("ko", [P, NT + 1, P])
        bias = tile("bias", [P, TP])
        sbias = tile("sbias", [SR, PAST + TS])
        bones = tile("bones", [P, P])
        comb, combr = tile("comb", [SR, TS]), tile("combr", [SR, TS])
        lamrow = tile("lamrow", [SR, 1])
        rowsel = tile("rowsel", [SR, 2])
        eps64, subg = tile("eps64", [P, 1]), tile("subg", [P, 1])
        S = tile("S", [P, 2, 2, TP])
        wT = tile("wT", [P, 2, TP])
        th = wT[:, 0, 0:2 * THIRD].rearrange("p (a t) -> p a t", a=2)
        sq = S[:, 1, :, :].rearrange("p c k -> p (c k)")[:, 0:T]
        kcT = ko[:].rearrange("p t k -> p (t k)")[:, 0:2 * PAST].rearrange("p (a k) -> p a k", a=2)
        SS = S[0:SR, 0, 1, 0:PAST + TS]
        nmx, rsum, rr = tile("nmx", [P, 2, 2]), tile("rsum", [P, 2, 2]), tile("rr", [P, 2, 2])
        QZ, QN = tile("QZ", [P, SB * (SR + SL)]), tile("QN", [P, SR])
        kc, vc = tile("kc", [P, SB * NPG, P]), tile("vc", [P, SB * NPG, DE])
        snm, ssum, srr = tile("snm", [SR, 2]), tile("ssum", [SR, 1]), tile("srr", [SR, 2])
        wsT = tile("wsT", [P, NPG + 1, TS])
        pt = tile("pt", [1, SB * NPG], I32)
        hk, hb, G, ident, ones, vec = K["B2"], K["B1"], K["G"], K["ident"], K["ones"], K["vec"]

        passed = {n: K["sem"]("passed_" + n) for n in ("sp", "pool", "act", "dve")}
        s_const, s_pt, s_set, s_init = sem("const_in"), sem("pages_in"), sem("set"), sem("init")
        s_w = {n: sem(f"w_{n}_in") for n in "qkzv"}
        s_hk = K["sem"]("no_hk_ready")
        s_kc, s_vc = sem("kcache_in"), sem("vcache_in")
        s_proj, s_pfree = sem("proj_summed"), sem("proj_bank_free")
        s_qk, s_sq, s_v = sem("qk_copied"), sem("qk_squares"), sem("v_ready")
        s_rs, s_qn, s_zs = sem("qk_rstd"), sem("qk_ready"), sem("z_ready")
        s_kops, s_ko, s_kst = sem("k_turned"), sem("k_out_ready"), sem("kv_stored")
        s_bias = sem("bias_ready")
        s_sc, s_min, s_exp, s_scale, s_wc = sem("scores_summed"), sem("min_ready"), sem("exp_ready"), sem("scale_steps"), sem("weights_ready")
        s_wps, s_wT, s_pv, s_oev = sem("weights_turned"), sem("wT_ready"), sem("out_summed"), sem("out_copied")
        s_qz, s_kcps, s_kcT, s_ssc, s_smin, s_sexp = (sem("qz_ready"), sem("kcache_turned"), sem("kcT_ready"), sem("sscores_summed"),
                                                      sem("smin_ready"), sem("sexp_ready"))
        s_srec, s_comb, s_wsps, s_wsT, s_spv, s_soev = (sem("srecip"), sem("comb_ready"), sem("sweights_turned"), sem("wsT_ready"),
                                                        sem("sout_summed"), sem("sout_copied"))
        s_osq, s_oss, s_oln, s_ors, s_g1, s_g2 = (sem("o_squares"), sem("o_sums"), sem("o_log"), sem("o_rstd"),
                                                  sem("o_normed"), sem("o_gated"))
        UNITS = 12
        GROUPS = [(r, min(r + 4, NT + 1)) for r in range(0, NT + 1, 4)]
        WG = [(i + 4) // 4 for i in range(NT)]
        WB = [sum(WG[:i]) for i in range(NT + 1)]
        wd = {"q": A["w_in_b"].rearrange("(k p) n -> p k n", p=P)[:, :, 0:D], "z": A["w_in_b"].rearrange("(k p) n -> p k n", p=P)[:, :, D:2 * D],
              "k": A["w_k"].rearrange("(k p) n -> p k n", p=P), "v": A["w_v"].rearrange("(k p) n -> p k n", p=P)}

        def over_heads(eng, head):
            with eng.Fori(0, HB - 1) as i:
                head(i, False)
            head(HB - 1, True)

        with nc.Block() as block:
            @block.sync
            def _(sp):
                for dst, name in ((bias, "bias"), (sbias, "sbias"), (bones, "bones"), (comb, "comb"), (rowsel, "lamsel")):
                    sp.dma_start(dst[:], A[name]).then_inc(s_const, 16)
                sp.dma_start(pt[:], A["page_table"].rearrange("b n -> (b n)").unsqueeze(0)).then_inc(s_pt, 16)
                sp.wait_ge(s_pt, 16)
                with sp.Fori(0, HB) as i:
                    sp.wait_ge(s_kcps, i * SB + SB)
                    apart(sp, passed["sp"])
                    with sp.Fori(0, SB * NPG) as n:
                        page = sp.value_load(pt[0:1, bass.ds(n, 1)], min_val=0, max_val=A["cache_k"].shape[0] - 1)
                        sp.dma_start(kc[:, bass.ds(n, 1), :], A["cache_k"][bass.ds(page, 1), :, bass.ds(i, 1), :].rearrange("n p h d -> p (n h) d")).then_inc(s_kc, 16)
                    sp.wait_ge(s_ko, 3 * (i + 1))
                    apart(sp, passed["sp"])
                    sp.dma_start(OUT["k_p"][:, bass.ds(i, 1), :].rearrange("(t p) h e -> p t (h e)", p=P), ko[:, 0:NT, :]).then_inc(s_kst, 16)
                    sp.dma_start(OUT["k_s"][:, bass.ds(i, 1), :].rearrange("p h e -> p (h e)"), ko[0:TS, NT, :]).then_inc(s_kst, 16)
                    sp.wait_ge(s_v, 3 * (i + 1))
                    sp.wait_ge(s_kst, 64 * i + 32)
                    apart(sp, passed["sp"])
                    sp.dma_start(OUT["v_p"][:, bass.ds(i, 1), :].rearrange("(t p) h e -> p t (h e)", p=P), v[:, 0:NT, :]).then_inc(s_kst, 16)
                    sp.dma_start(OUT["v_s"][:, bass.ds(i, 1), :].rearrange("p h e -> p (h e)"), v[0:TS, NT, :]).then_inc(s_kst, 16)
                for b in range(2):
                    sp.wait_ge(s_proj, (HB + 1) * UNITS)
                    sp.dma_start(K[f"w{b}"][:], A["w_out_b"].rearrange("(k p) n -> p k n", p=P)[:, :, b * P:(b + 1) * P]).then_inc(
                        K["sem"](f"op_w_in{b}"), 16)

            @block.gpsimd
            def _(pool):
                nc.gpsimd.memset(QZ[:], 0.0).then_inc(s_set, 1)
                nc.gpsimd.memset(QN[:], 0.0).then_inc(s_set, 1)
                nc.gpsimd.memset(eps64[:], EPS * DQ).then_inc(s_set, 1)
                pool.sem_inc(s_proj, UNITS)
                pool.wait_ge(s_pt, 16)

                def load_weights(name, i, used):
                    pool.wait_ge(s_proj, i * UNITS + used)
                    apart(pool, passed["pool"])
                    pool.dma_start(w[name][:], wd[name][:, :, bass.ds(i * P, P)]).then_inc(s_w[name], 16)

                def head(i, last):
                    load_weights("z", i, 9)
                    load_weights("v", i, UNITS + 3)
                    pool.wait_ge(s_spv, i + 1)
                    apart(pool, passed["pool"])
                    with pool.Fori(0, SB * NPG) as n:
                        page = pool.value_load(pt[0:1, bass.ds(n, 1)], min_val=0, max_val=A["cache_v"].shape[0] - 1)
                        pool.dma_start(vc[:, bass.ds(n, 1), :], A["cache_v"][bass.ds(page, 1), :, bass.ds(i, 1), :].rearrange("n p h d -> p (n h) d")).then_inc(s_vc, 16)
                    if not last:
                        load_weights("q", i + 1, UNITS)
                        load_weights("k", i + 1, 6)

                over_heads(pool, head)

            @block.tensor
            def _(pe):
                pe.sem_inc(s_kcps, SB)
                pe.sem_inc(s_spv, 1)
                def project(name, i, unit, src):
                    pe.wait_ge(s_pfree, i * UNITS + unit + 1)
                    for k in range(KC):
                        mm = nc.tensor.matmul(psP[:, unit % 2, 0:THIRD], w[name][:, k, :], thirds(src[:, k, :])[unit % 3], start=(k == 0), stop=(k == KC - 1))
                    mm.then_inc(s_proj, 1)

                def project_v(r, i):
                    lo, hi = GROUPS[r]
                    pe.wait_ge(s_pfree, i * UNITS + 9 + r + 1)
                    for t in range(lo, hi):
                        n = P if t < NT else TS
                        for k in range(KC):
                            mm = nc.tensor.matmul(psP[0:n, (9 + r) % 2, (t - lo) * P:(t - lo + 1) * P], hk[:, k, t * P:t * P + n], w["v"][:, k, :],
                                                  start=(k == 0), stop=(k == KC - 1))
                    mm.then_inc(s_proj, 1)

                def head(i, last):
                    def squares(r):
                        pe.wait_ge(s_sq, 2 * i + r + 1)
                        for j in range(3):
                            mm = nc.tensor.matmul(psS[:, j, 0:THIRD], bones[:], thirds(sq)[j], start=True, stop=True)
                        mm.then_inc(s_oss, 1)

                    def turn_k(r):
                        lo, hi = GROUPS[r]
                        if r:
                            pe.wait_ge(s_ko, 3 * i + r)
                        for t in range(lo, hi):
                            n = P if t < NT else TS
                            mm = nc.tensor.transpose(psW[0:n, (t - lo) * P:(t - lo + 1) * P], kT[:, t * P:t * P + n], ident[:])
                        mm.then_inc(s_kops, 1)

                    def scores(t):
                        for comp in range(2):
                            rows = slice(DQ * comp, DQ * (comp + 1))
                            if t:
                                pe.wait_ge(s_min, 2 * NT * i + 2 * (t - 1) + comp + 1)
                            for lo in range(0, P * (t + 1), 512):
                                hi = min(lo + 512, P * (t + 1))
                                mm = nc.tensor.matmul(psS[:, 2 * comp + lo // 512, 0:hi - lo], qT[rows, t * P:(t + 1) * P], kT[rows, lo:hi], start=True, stop=True)
                            mm.then_inc(s_sc, 1)

                    def weigh(t, groups):
                        pe.wait_ge(s_wc, NT * i + t + 1)
                        for r in groups:
                            lo, hi = 4 * r, min(4 * r + 4, t + 1)
                            if t or r:
                                pe.wait_ge(s_wT, WB[NT] * i + WB[t] + r)
                            for k in range(lo, hi):
                                mm = nc.tensor.transpose(psW[:, (k - lo) * P:(k - lo + 1) * P], S[:, t % 2, 0, k * P:(k + 1) * P], ident[:])
                            mm.then_inc(s_wps, 1)

                    def values(t):
                        pe.wait_ge(s_wT, WB[NT] * i + WB[t + 1])
                        if t:
                            pe.wait_ge(s_oev, NT * i + t)
                        for k in range(t + 1):
                            mm = nc.tensor.matmul(psO[:, (t % 2) * P:(t % 2 + 1) * P], v[:, k, :], wT[:, t % 2, k * P:(k + 1) * P], start=(k == 0), stop=(k == t))
                        mm.then_inc(s_pv, 1)

                    def turn_cache(b):
                        if b:
                            pe.wait_ge(s_kcT, SB * i + b)
                        for n in range(NPG):
                            mm = nc.tensor.transpose(psP[:, 0, n * PAGE:(n + 1) * PAGE], kc[:, b * NPG + n, :], ident[:])
                        mm.then_inc(s_kcps, 1)

                    def cache_scores(b):
                        pe.wait_ge(s_kcT, SB * i + b + 1)
                        mm = nc.tensor.matmul(psP[0:SR, 1, :], QZ[:, b * SR:(b + 1) * SR], kcT[:, b % 2, :], start=(b == 0), stop=(b == SB - 1))
                        mm.then_inc(s_ssc, 1)

                    pe.wait_ge(s_w["k"], 16 * (i + 1))
                    project("k", i, 3, hk)
                    project("k", i, 4, hk)
                    pe.wait_ge(s_ors, i + 1)
                    squares(0)
                    project("k", i, 5, hk)
                    pe.wait_ge(s_w["z"], 16 * (i + 1))
                    for unit in range(6, 9):
                        project("z", i, unit, hb)
                    pe.wait_ge(s_rs, 2 * i + 1)
                    squares(1)
                    pe.wait_ge(s_w["v"], 16 * (i + 1))
                    project_v(0, i)
                    pe.wait_ge(s_qn, 2 * i + 2)
                    turn_k(0)
                    project_v(1, i)
                    turn_k(1)
                    scores(0)
                    project_v(2, i)
                    turn_k(2)
                    pe.wait_ge(s_ko, 3 * i + 3)
                    pe.wait_ge(s_v, 3 * i + 3)
                    pe.wait_ge(s_qz, i + 1)
                    pe.wait_ge(s_kc, 16 * SB * NPG * (i + 1))
                    for t in range(NT):
                        if t + 1 < NT:
                            scores(t + 1)
                        if t:
                            turn_cache(t - 1)
                            values(t - 1)
                        if t == NT - 1:
                            pe.wait_ge(s_min, 2 * NT * (i + 1))
                            nc.tensor.matmul(psS[0:SR, 1, 0:TS], QN[:], kT[:, TP:T], start=True, stop=True).then_inc(s_ssc, 1)
                            cache_scores(t - 1)
                            turn_cache(SB - 1)
                        weigh(t, [0])
                        if 0 < t < NT - 1:
                            cache_scores(t - 1)
                        if t == NT - 1:
                            cache_scores(SB - 1)
                        weigh(t, range(1, WG[t]))
                    if not last:
                        pe.wait_ge(s_w["q"], 16 * (i + 2))
                        project("q", i, UNITS, hb)
                    values(NT - 1)
                    pe.wait_ge(s_wT, WB[NT] * (i + 1))
                    pe.wait_ge(s_comb, i + 1)
                    for g in range(NPG):
                        nc.tensor.matmul(psW[:, g * TS:(g + 1) * TS], SS[:, g * PAGE:(g + 1) * PAGE], combr[:], start=True, stop=True)
                    nc.tensor.matmul(psW[0:TS, NPG * TS:(NPG + 1) * TS], SS[:, PAST:PAST + TS], combr[:], start=True, stop=True).then_inc(s_wsps, 1)
                    if not last:
                        project("q", i, UNITS + 1, hb)
                    pe.wait_ge(s_wsT, 2 * (i + 1))
                    pe.wait_ge(s_vc, 16 * SB * NPG * (i + 1))
                    pe.wait_ge(s_oev, NT * (i + 1))
                    for b in range(SB):
                        for g in range(NPG):
                            nc.tensor.matmul(psO[:, b * SL:(b + 1) * SL], vc[:, b * NPG + g, :], wsT[:, g, b * SL:(b + 1) * SL], start=(b == 0 and g == 0), stop=False)
                    nc.tensor.matmul(psO[:, 0:TS], v[0:TS, NT, :], wsT[0:TS, NPG, :], start=False, stop=True).then_inc(s_spv, 1)
                    if not last:
                        project("q", i, UNITS + 2, hb)
                    pe.wait_ge(s_osq, i + 1)
                    pe.wait_ge(s_smin, 2 * (i + 1))
                    for j in range(3):
                        mm = nc.tensor.matmul(psS[:, j, 0:THIRD], ones[:], thirds(sq)[j], start=True, stop=True)
                    mm.then_inc(s_oss, 1)

                pe.wait_ge(s_w["q"], 16)
                for unit in range(3):
                    project("q", 0, unit, hb)
                pe.wait_ge(s_const, 16 * 5)
                pe.wait_ge(s_hk, KC)
                over_heads(pe, head)

            @block.scalar
            def _(act):
                A_ = nc.scalar.activation
                act.sem_inc(s_pfree, 2)
                act.sem_inc(s_ors, 1)
                act.wait_ge(s_set, 3)

                def done(i, unit):
                    act.wait_ge(s_proj, (i + 1) * UNITS + unit + 1)
                    return unit % 2

                def copy_out(dst, i, unit):
                    b = done(i, unit)
                    A_(thirds(dst[:])[unit % 3], psP[:, b, 0:THIRD], ACT.Copy).then_inc(s_qk, 1)
                    act.wait_ge(s_qk, 6 * i + (unit if unit < 6 else unit - UNITS + 6) + 1)
                    act.sem_inc(s_pfree, 1)

                def head(i, last):
                    def rstd(r):
                        act.wait_ge(s_oss, 3 * i + r + 1)
                        A_(rs[:].rearrange("p (j t) -> p j t", j=3), psS[:, 0:3, 0:THIRD], ACT.Ln, scale=(1.0, 1.0 / DQ)[r],
                           bias=(eps64, K["eps"])[r][:, 0:1]).then_inc(s_oln, 1)
                        act.wait_ge(s_oln, 3 * i + r + 1)
                        A_(rs[:], rs[:], ACT.Exp, scale=-0.5).then_inc(s_rs, 1)

                    act.wait_ge(s_qk, 6 * i + 3)
                    A_(sq, qT[:], ACT.Square).then_inc(s_sq, 1)
                    copy_out(kT, i, 3)
                    copy_out(kT, i, 4)
                    act.wait_ge(s_g2, i + 1)
                    rstd(0)
                    copy_out(kT, i, 5)
                    A_(sq, kT[:], ACT.Square).then_inc(s_sq, 1)
                    for j in range(3):
                        b = done(i, 6 + j)
                        if j == 2:
                            act.wait_ge(s_zs, 3 * i + 1)
                        A_(thirds(zs[:])[j], psP[:, b, 0:THIRD], ACT.Copy, scale=0.5)
                        A_(th[:, j % 2, :], psP[:, b, 0:THIRD], ACT.Tanh, scale=0.5).then_inc(s_pfree, 1)
                    act.wait_ge(s_qn, 2 * i + 1)
                    rstd(1)
                    for r, (lo, hi) in enumerate(GROUPS):
                        b = done(i, 9 + r)
                        n = P if lo < NT else TS
                        A_(v[0:n, lo:hi, :].rearrange("p a d -> p (a d)"), psP[0:n, b, 0:(hi - lo) * P], ACT.Copy).then_inc(s_v, 1)
                        act.wait_ge(s_v, 3 * i + r + 1)
                        act.sem_inc(s_pfree, 1)
                        act.wait_ge(s_kops, 3 * i + r + 1)
                        A_(ko[0:n, lo:hi, :].rearrange("p a d -> p (a d)"), psW[0:n, 0:(hi - lo) * P], ACT.Copy).then_inc(s_ko, 1)

                    def exps(t):
                        n = P * (t + 1)
                        for comp in range(2):
                            act.wait_ge(s_min, 2 * NT * i + 2 * t + comp + 1)
                            s = S[:, t % 2, comp, 0:n]
                            A_(s, s, ACT.Exp, scale=-1.0, bias=nmx[:, t % 2, comp:comp + 1], accum_out=rsum[:, t % 2, comp:comp + 1]).then_inc(s_exp, 1)

                    def copies(t):
                        for r in range(WG[t]):
                            lo, hi = 4 * r, min(4 * r + 4, t + 1)
                            act.wait_ge(s_wps, WB[NT] * i + WB[t] + r + 1)
                            if t >= 2:
                                act.wait_ge(s_pv, NT * i + t - 1)
                            A_(wT[:, t % 2, lo * P:hi * P], psW[:, 0:(hi - lo) * P], ACT.Copy).then_inc(s_wT, 1)

                    def out(t):
                        act.wait_ge(s_pv, NT * i + t + 1)
                        apart(act, passed["act"])
                        A_(G[:, bass.ds(i, 1), t * P:(t + 1) * P].rearrange("p a t -> p (a t)"), psO[:, (t % 2) * P:(t % 2 + 1) * P], ACT.Copy).then_inc(s_oev, 1)

                    exps(0)

                    def cached(b):
                        act.wait_ge(s_kcps, SB * i + SB + b + 1)
                        if b >= 2:
                            act.wait_ge(s_ssc, (SB + 1) * i + b - 1)
                        A_(kcT[:, b % 2, :], psP[:, 0, :], ACT.Copy).then_inc(s_kcT, 1)

                    for t in range(NT):
                        if t == 1:
                            act.wait_ge(s_kst, 64 * i + 32)
                        if t:
                            cached(t - 1)
                        if t == NT - 1:
                            cached(SB - 1)
                        copies(t)
                        if t + 1 < NT:
                            exps(t + 1)
                        if t:
                            out(t - 1)
                    act.wait_ge(s_smin, 2 * (i + 1))
                    A_(SS, SS, ACT.Exp, scale=-1.0, bias=snm[:, 1:2], accum_out=ssum[:]).then_inc(s_sexp, 1)
                    if not last:
                        copy_out(qT, i, UNITS)
                    out(NT - 1)
                    act.wait_ge(s_kst, 64 * (i + 1))
                    act.wait_ge(s_wsps, i + 1)
                    A_(wsT[:, 0:NPG, :].rearrange("p a d -> p (a d)"), psW[:, 0:NPG * TS], ACT.Copy).then_inc(s_wsT, 1)
                    A_(wsT[0:TS, NPG, :], psW[0:TS, NPG * TS:(NPG + 1) * TS], ACT.Copy).then_inc(s_wsT, 1)
                    if not last:
                        copy_out(qT, i, UNITS + 1)
                    g = G[:, bass.ds(i, 1), :].rearrange("p a t -> p (a t)")
                    act.wait_ge(s_spv, i + 2)
                    apart(act, passed["act"])
                    A_(g[:, TP:T], psO[:, 0:TS], ACT.Copy).then_inc(s_soev, 1)
                    act.wait_ge(s_soev, i + 1)
                    act.wait_ge(s_oev, NT * (i + 1))
                    apart(act, passed["act"])
                    A_(sq, g, ACT.Square).then_inc(s_osq, 1)
                    if not last:
                        copy_out(qT, i, UNITS + 2)
                    act.wait_ge(s_oss, 3 * i + 3)
                    A_(rs[:].rearrange("p (j t) -> p j t", j=3), psS[:, 0:3, 0:THIRD], ACT.Ln, scale=1.0 / DE, bias=K["eps"][:, 0:1]).then_inc(s_oln, 1)
                    act.wait_ge(s_oln, 3 * i + 3)
                    A_(rs[:], rs[:], ACT.Exp, scale=-0.5).then_inc(s_ors, 1)

                norm.act_affine(act, norm.affine[1:], s_hk)
                for unit in range(3):
                    copy_out(qT, 0, unit)
                over_heads(act, head)

            @block.vector
            def _(dve):
                V = nc.vector
                lam_init = 0.8 - 0.6 * float(np.exp(-0.3))
                dve.wait_ge(s_const, 16 * 5)
                V.tensor_scalar(subg[:], vec[:, V_SUBLN:V_SUBLN + 1], 1.0 - lam_init, None, ALU.mult).then_inc(s_init, 1)
                V.scalar_tensor_tensor(lamrow[:], rowsel[:, 1:2], K["nlam"][0:SR, 0:1], rowsel[:, 0:1], ALU.mult, ALU.add).then_inc(s_init, 1)
                dve.wait_ge(s_init, 2)
                dve.wait_ge(s_set, 3)
                dve.sem_inc(s_g2, 1)
                with dve.Fori(0, HB) as i:
                    V.tensor_scalar(bias[:], bias[:], 0.5, None, ALU.mult).then_inc(s_bias, 1)
                    V.tensor_scalar(sbias[:], sbias[:], 0.5, None, ALU.mult).then_inc(s_bias, 1)
                    def norm(r, dst, col):
                        dve.wait_ge(s_rs, 2 * i + r + 1)
                        V.scalar_tensor_tensor(dst[:], dst[:], vec[:, col:col + 1], rs[:], ALU.mult, ALU.mult).then_inc(s_qn, 1)

                    dve.wait_ge(s_sq, 2 * i + 1)
                    norm(0, qT, V_GQ)
                    for j in range(3):
                        dve.wait_ge(s_pfree, 2 + i * UNITS + 6 + j + 1)
                        z = thirds(zs[:])[j]
                        V.scalar_tensor_tensor(z, th[:, j % 2, :], 1.0, z, ALU.add, ALU.mult).then_inc(s_zs, 1)
                    dve.wait_ge(s_sq, 2 * i + 2)
                    norm(1, kT, V_GK)
                    dve.wait_ge(s_qn, 2 * i + 2)
                    for comp in range(2):
                        rows = slice(DQ * comp, DQ * (comp + 1))
                        V.tensor_copy(QZ[rows, :].rearrange("p (b r) -> p b r", r=SR + SL)[:, :, comp * TS:comp * TS + SL],
                                      qT[rows, TP:T].rearrange("p (b t) -> p b t", b=SB))
                        last = V.tensor_copy(QN[rows, comp * TS:(comp + 1) * TS], qT[rows, TP:T])
                    last.then_inc(s_qz, 1)
                    dve.wait_ge(s_bias, 2 * (i + 1))

                    def mins(t):
                        n = P * (t + 1)
                        for comp in range(2):
                            dve.wait_ge(s_sc, 2 * NT * i + 2 * t + comp + 1)
                            if t >= 2:
                                dve.wait_ge(s_wps, WB[NT] * i + WB[t - 1])
                                dve.wait_ge(s_wc, NT * i + t - 1)
                            apart(dve, passed["dve"])
                            V.tensor_tensor_reduce(S[:, t % 2, comp, 0:n], psS[:, 2 * comp:2 * comp + 2, :].rearrange("p a k -> p (a k)")[:, 0:n],
                                                   bias[:, TP - n:TP], -1.0, 3.0e38, ALU.add, ALU.min, nmx[:, t % 2, comp:comp + 1]).then_inc(s_min, 1)

                    def combine(t):
                        n = P * (t + 1)
                        dve.wait_ge(s_exp, 2 * NT * i + 2 * t + 2)
                        V.reciprocal(rr[:, t % 2, :], rsum[:, t % 2, :]).then_inc(s_scale, 1)
                        dve.wait_ge(s_scale, 3 * NT * i + 3 * t + 1)
                        V.tensor_tensor(rr[:, t % 2, 1:2], rr[:, t % 2, 1:2], K["nlam"][:], ALU.mult).then_inc(s_scale, 1)
                        dve.wait_ge(s_scale, 3 * NT * i + 3 * t + 2)
                        V.tensor_scalar(S[:, t % 2, 1, 0:n], S[:, t % 2, 1, 0:n], rr[:, t % 2, 1:2], None, ALU.mult).then_inc(s_scale, 1)
                        dve.wait_ge(s_scale, 3 * NT * i + 3 * t + 3)
                        V.scalar_tensor_tensor(S[:, t % 2, 0, 0:n], S[:, t % 2, 0, 0:n], rr[:, t % 2, 0:1], S[:, t % 2, 1, 0:n],
                                               ALU.mult, ALU.add).then_inc(s_wc, 1)

                    mins(0)
                    for t in range(NT):
                        combine(t)
                        if t + 1 < NT:
                            mins(t + 1)
                    dve.wait_ge(s_ssc, (SB + 1) * (i + 1))
                    apart(dve, passed["dve"])
                    V.tensor_tensor_reduce(SS[:, 0:PAST], psP[0:SR, 1, :], sbias[:, 0:PAST], -1.0, 3.0e38, ALU.add, ALU.min, snm[:, 0:1]).then_inc(s_smin, 1)
                    dve.wait_ge(s_smin, 2 * i + 1)
                    apart(dve, passed["dve"])
                    V.tensor_tensor_reduce(SS[:, PAST:PAST + TS], psS[0:SR, 1, 0:TS], sbias[:, PAST:PAST + TS], -1.0, snm[:, 0:1], ALU.add, ALU.min,
                                           snm[:, 1:2]).then_inc(s_smin, 1)
                    dve.wait_ge(s_sexp, i + 1)
                    V.reciprocal(srr[:, 0:1], ssum[:]).then_inc(s_srec, 1)
                    dve.wait_ge(s_srec, 2 * i + 1)
                    V.tensor_tensor(srr[:, 1:2], srr[:, 0:1], lamrow[:], ALU.mult).then_inc(s_srec, 1)
                    dve.wait_ge(s_srec, 2 * i + 2)
                    V.tensor_scalar(combr[:], comb[:], srr[:, 1:2], None, ALU.mult).then_inc(s_comb, 1)
                    dve.wait_ge(s_ors, i + 2)
                    g = G[:, bass.ds(i, 1), :].rearrange("p a t -> p (a t)")
                    V.scalar_tensor_tensor(g, g, subg[:, 0:1], rs[:], ALU.mult, ALU.mult).then_inc(s_g1, 1)
                    dve.wait_ge(s_g1, i + 1)
                    dve.wait_ge(s_zs, 3 * i + 3)
                    V.tensor_tensor(g, g, zs[:], ALU.mult).then_inc(s_g2, 1)
                    dve.wait_ge(s_g2, i + 2)



def shape_constants():
    s, t = np.arange(P)[:, None], np.arange(P)[None, :]
    f = np.float32

    def level(L):
        return (s // (2 * L) == t // (2 * L)) & (s % (2 * L) < L) & (t % (2 * L) >= L)

    masks = np.stack([level(L) for L in LEVELS] + [s == t], 1).astype(f)
    seq = (s // SL == t // SL)[:TS, :TS]
    smasks = np.stack([level(2)[:TS, :TS] & seq, level(1)[:TS, :TS] & seq, (s == t)[:TS, :TS]], 1).astype(f)
    restart = np.ones((P, T), f)
    restart[:, 0:TP:P] = 0.0
    restart[:, TP:T:SL] = 0.0
    rowsel = (np.arange(TS)[:, None] // SL == np.arange(SB)[None, :]).astype(f)
    x = np.arange(TP)[None, :] - np.arange(P)[:, None] - (TP - P)
    bias = np.where(x <= 0, x, NEG).astype(f)
    r = np.arange(SR)
    seq_r, q_r = (r % TS) // SL, r % SL
    past = np.arange(PAST)[None, :] - (PAST + q_r)[:, None]
    n = np.arange(TS)
    new = np.where((seq_r[:, None] == n[None, :] // SL) & (n[None, :] % SL <= q_r[:, None]), n[None, :] % SL - q_r[:, None], NEG)
    sbias = np.concatenate([past, new], 1).astype(f)
    bones = (s // DQ == t // DQ).astype(f)
    comb = (r[:, None] % TS == n[None, :]).astype(f)
    lamsel = np.stack([r < TS, r >= TS], 1).astype(f)
    return {"ident": np.eye(P, dtype=f), "ones": np.ones((P, P), f), "masks": masks, "smasks": smasks, "restart": restart, "rowsel": rowsel,
            "bias": bias, "sbias": sbias, "bones": bones, "comb": comb, "lamsel": lamsel}


_OUTS = {"y_p": (TP, D), "y_s": (TS, D), "state_p": (HA, DK, DV), "state_s": (SB, HA, DK, DV), "k_p": (TP, HB, P), "v_p": (TP, HB, DE),
         "k_s": (TS, HB, P), "v_s": (TS, HB, DE)}


def kernel(**inputs):
    import concourse.bacc as bacc
    from concourse.bass_utils import run_bass_kernel_spmd

    a = {k: np.asarray(v) for k, v in inputs.items()}
    flat = {
        "x_prompt": a["x_prompt"].reshape(TP, D), "x_sample": a["x_sample"].reshape(TS, D),
        "cache_k": a["cache_k"].reshape(-1, PAGE, HB, P), "cache_v": a["cache_v"].reshape(-1, PAGE, HB, DE),
        "state_gla": a["state_gla"].reshape(SB, HA, DK, DV),
    }
    for k in ("norm_a", "ada_w_a", "ada_b_a", "w_in_a", "w_g2_a", "b_g_a", "onorm_a", "w_out_a", "norm_b", "ada_w_b", "ada_b_b", "w_in_b",
              "g_q", "lambda_q1", "lambda_k1", "lambda_q2", "lambda_k2", "subln_b", "w_out_b"):
        flat[k] = a[k][0]
    for k in ("c_prompt", "c_sample", "page_table", "norm_kv", "ada_w_kv", "ada_b_kv", "w_k", "w_v", "g_k"):
        flat[k] = a[k]
    flat.update(shape_constants())
    nc = bacc.Bacc("TRN2", target_bir_lowering=False, num_devices=1)
    arrays, ins = {}, {}
    for name, x in flat.items():
        arrays["in_" + name] = np.ascontiguousarray(x)
        ins[name] = nc.dram_tensor("in_" + name, x.shape, mybir.dt.from_np(x.dtype), kind="ExternalInput").ap()
    outs = {name: nc.dram_tensor("out_" + name, shape, F32, kind="ExternalOutput").ap() for name, shape in _OUTS.items()}
    scratch = {name: nc.dram_tensor("scr_" + name, (D, T), F32, kind="Internal").ap() for name in ("xT", "x1T", "G")}
    build(nc, ins, outs, scratch)
    r = run_bass_kernel_spmd(nc, [arrays], core_ids=[0]).results[0]
    o = {name: r["out_" + name] for name in _OUTS}
    return (o["y_p"].reshape(1, TP, D), o["y_s"].reshape(SB, SL, D), o["state_p"].reshape(1, 1, HA, DK, DV),
            o["state_s"].reshape(1, SB, HA, DK, DV), o["k_p"].reshape(1, TP, HB, 2, DQ), o["v_p"].reshape(1, TP, HB, DE),
            o["k_s"].reshape(SB, SL, HB, 2, DQ), o["v_s"].reshape(SB, SL, HB, DE))
```
